# Optimizing a Trainium2 kernel written in Bass

```python
import math
import jax, jax.numpy as jnp
from jax import lax
import numpy as np

D_MODEL = 1024
BATCH = 1
SEQ = 256
DEPTH = 2

CHUNK = 64
Q_BLOCK = 128
N_EVEN = (DEPTH + 1) // 2
N_ODD = DEPTH // 2
DN_ALPHA = (2.0 * DEPTH) ** 0.25
DN_BETA = (8.0 * DEPTH) ** -0.25
LN_EPS = 1e-5
RMS_EPS = 1e-6

GLA_HEADS = 4
GLA_DK = 64
GLA_DV = 128
GLA_GATE_RANK = 16
GLA_TAU = 16.0
GLA_QK = GLA_HEADS * GLA_DK
GLA_V = GLA_HEADS * GLA_DV
GLA_SPLITS = (GLA_QK, GLA_QK, GLA_V, GLA_V, GLA_GATE_RANK)
GLA_IN = sum(GLA_SPLITS)
GLA_OFFSETS = tuple(int(o) for o in np.cumsum(GLA_SPLITS)[:-1])

RW_HEADS = 8
RW_N = 64
RW_W = RW_HEADS * RW_N
RW_DECAY_RANK = 64
RW_A_RANK = 64
RW_GATE_RANK = 160
RW_GN_EPS = 64e-5
RW_SPLITS = (RW_W, RW_W, RW_W, RW_DECAY_RANK, RW_A_RANK, RW_GATE_RANK)
RW_IN = sum(RW_SPLITS)
RW_OFFSETS = tuple(int(o) for o in np.cumsum(RW_SPLITS)[:-1])

EVEN_IN = GLA_IN + RW_IN
EVEN_MIX = GLA_V + RW_W

MLA_HEADS = 16
MLA_NOPE = 64
MLA_ROPE = 32
MLA_V = 64
MLA_Q_RANK = 768
MLA_KV_RANK = 256
ODD_IN = MLA_Q_RANK + MLA_KV_RANK + MLA_ROPE
MLA_MIX = MLA_HEADS * MLA_V
ROPE_THETA = 10000.0

FFN_HIDDEN = math.ceil(8 * D_MODEL / 3 / 256) * 256


def layer_norm(x, g, b):
    xf = x.astype(jnp.float32)
    mu = xf.mean(-1, keepdims=True)
    var = jnp.square(xf - mu).mean(-1, keepdims=True)
    return ((xf - mu) * lax.rsqrt(var + LN_EPS) * g + b).astype(x.dtype)

def rms_norm(x, g):
    xf = x.astype(jnp.float32)
    return (xf * lax.rsqrt(jnp.mean(xf * xf, -1, keepdims=True) + RMS_EPS) * g).astype(x.dtype)

def token_shift(t):
    return jnp.pad(t[:, :-1], ((0, 0), (1, 0), (0, 0)))

def gla_chunked(q, k, v, log_a):
    B, S, H, DK = q.shape
    DV = v.shape[-1]
    n = S // CHUNK

    def to_chunks(t):
        return t.astype(jnp.float32).reshape(B, n, CHUNK, H, t.shape[-1]).transpose(1, 0, 3, 2, 4)

    qc, kc, vc, gc = to_chunks(q), to_chunks(k), to_chunks(v), to_chunks(log_a)
    causal = jnp.tril(jnp.ones((CHUNK, CHUNK), bool))[None, None, :, :, None]

    def step(state, inp):
        qi, ki, vi, gi = inp
        b = jnp.cumsum(gi, axis=2)
        o_inter = jnp.einsum('bhck,bhkv->bhcv', qi * jnp.exp(b), state)
        rel = jnp.where(causal, b[:, :, :, None, :] - b[:, :, None, :, :], -jnp.inf)
        attn = jnp.einsum('bhik,bhjk,bhijk->bhij', qi, ki, jnp.exp(rel))
        o_intra = jnp.einsum('bhij,bhjv->bhiv', attn, vi)
        b_last = b[:, :, -1:, :]
        new_state = (jnp.exp(b_last[:, :, 0, :])[..., None] * state
                     + jnp.einsum('bhck,bhcv->bhkv', ki * jnp.exp(b_last - b), vi))
        return new_state, o_inter + o_intra

    s0 = jnp.zeros((B, H, DK, DV), jnp.float32)
    _, o = lax.scan(step, s0, (qc, kc, vc, gc))
    return o.transpose(1, 0, 3, 2, 4).reshape(B, S, H, DV)

def rwkv7_scan(r, w, k, v, a_vec, b_vec):
    B, S, H, N = r.shape

    def tm(t):
        return t.astype(jnp.float32).transpose(1, 0, 2, 3)

    def step(state, inp):
        rt, wt, kt, vt, at, bt = inp
        sa = jnp.einsum('bhvk,bhk->bhv', state, at)
        state = state * wt[:, :, None, :] + sa[..., None] * bt[:, :, None, :] + vt[..., None] * kt[:, :, None, :]
        return state, jnp.einsum('bhvk,bhk->bhv', state, rt)

    s0 = jnp.zeros((B, H, N, N), jnp.float32)
    _, y = lax.scan(step, s0, (tm(r), tm(w), tm(k), tm(v), tm(a_vec), tm(b_vec)))
    return y.transpose(1, 0, 2, 3)

def even_mixer(x, w_in, gla_gate_w2, gla_gate_b, gla_norm_g, rw_mu, rw_w0, rw_w2, rw_a0, rw_a2,
               rw_g2, rw_k_k, rw_k_a, rw_r_k, rw_ln_g, rw_ln_b, w_out):
    B, S, _ = x.shape
    p = x @ w_in
    p_gla, p_rw = p[..., :GLA_IN], p[..., GLA_IN:]

    def heads(t, d):
        return t.reshape(B, S, -1, d)

    gq, gk, gv, gg, glr = jnp.split(p_gla, GLA_OFFSETS, axis=-1)
    log_a = jax.nn.log_sigmoid((glr @ gla_gate_w2 + gla_gate_b).astype(jnp.float32)) / GLA_TAU
    o_a = gla_chunked(heads(gq, GLA_DK) * GLA_DK ** -0.5, heads(gk, GLA_DK),
                      heads(gv, GLA_DV), heads(log_a, GLA_DK))
    o_a = (rms_norm(o_a, gla_norm_g) * jax.nn.silu(heads(gg, GLA_DV).astype(jnp.float32)))
    o_a = o_a.reshape(B, S, GLA_V).astype(x.dtype)

    p_rw = p_rw + rw_mu * (token_shift(p_rw) - p_rw)
    r, k, v, wl, al, gl = jnp.split(p_rw, RW_OFFSETS, axis=-1)
    w = -jax.nn.softplus(-(rw_w0 + jnp.tanh(wl) @ rw_w2)) - 0.5
    decay = jnp.exp(-jnp.exp(w.astype(jnp.float32)))
    a = jax.nn.sigmoid(rw_a0 + al @ rw_a2)
    g = jax.nn.sigmoid(gl) @ rw_g2
    kk = heads(k * rw_k_k, RW_N).astype(jnp.float32)
    kk = kk * lax.rsqrt(jnp.maximum(jnp.sum(kk * kk, -1, keepdims=True), 1e-24))
    k = k * (1 + (a - 1) * rw_k_a)
    r_h, k_h, v_h, a_h = heads(r, RW_N), heads(k, RW_N), heads(v, RW_N), heads(a, RW_N)
    y = rwkv7_scan(r_h, heads(decay, RW_N), k_h, v_h, -kk, kk * a_h)
    mu = y.mean(-1, keepdims=True)
    var = jnp.square(y - mu).mean(-1, keepdims=True)
    y = ((y - mu) * lax.rsqrt(var + RW_GN_EPS)).reshape(B, S, RW_W) * rw_ln_g + rw_ln_b
    bonus = jnp.sum(r_h * k_h * rw_r_k, -1, keepdims=True) * v_h
    o_b = ((heads(y, RW_N) + bonus).reshape(B, S, RW_W) * g).astype(x.dtype)

    return jnp.concatenate([o_a, o_b], axis=-1) @ w_out

def apply_rope(t, cos, sin):
    t2 = t.astype(jnp.float32).reshape(t.shape[:-1] + (-1, 2))
    x1, x2 = t2[..., 0], t2[..., 1]
    out = jnp.stack([x1 * cos - x2 * sin, x1 * sin + x2 * cos], axis=-1)
    return out.reshape(t.shape).astype(t.dtype)

def block_causal_mla_attention(q_nope, q_pe, k_nope, k_pe, v):
    B, S, H, _ = q_nope.shape
    scale = (MLA_NOPE + MLA_ROPE) ** -0.5
    key_chunk = jnp.arange(S) // CHUNK

    def block(i):
        start = i * Q_BLOCK
        qn = lax.dynamic_slice_in_dim(q_nope, start, Q_BLOCK, axis=1)
        qp = lax.dynamic_slice_in_dim(q_pe, start, Q_BLOCK, axis=1)
        s = (jnp.einsum('bqhd,bkhd->bhqk', qn, k_nope)
             + jnp.einsum('bqhr,bkr->bhqk', qp, k_pe)).astype(jnp.float32) * scale
        q_chunk = (start + jnp.arange(Q_BLOCK)) // CHUNK
        s = jnp.where(key_chunk[None, :] <= q_chunk[:, None], s, -jnp.inf)
        pr = jax.nn.softmax(s, axis=-1).astype(v.dtype)
        return jnp.einsum('bhqk,bkhd->bqhd', pr, v)

    o = lax.map(block, jnp.arange(S // Q_BLOCK))
    return o.transpose(1, 0, 2, 3, 4).reshape(B, S, H, MLA_V)

def odd_mixer(x, positions, w_in, q_norm_g, w_q_b, kv_norm_g, w_kv_b, w_out):
    B, S, _ = x.shape
    p = x @ w_in
    cq = p[..., :MLA_Q_RANK]
    ckv = p[..., MLA_Q_RANK:MLA_Q_RANK + MLA_KV_RANK]
    k_pe = p[..., MLA_Q_RANK + MLA_KV_RANK:]
    q = (rms_norm(cq, q_norm_g) @ w_q_b).reshape(B, S, MLA_HEADS, MLA_NOPE + MLA_ROPE)
    kv = (rms_norm(ckv, kv_norm_g) @ w_kv_b).reshape(B, S, MLA_HEADS, MLA_NOPE + MLA_V)
    q_nope, q_pe = q[..., :MLA_NOPE], q[..., MLA_NOPE:]
    k_nope, v = kv[..., :MLA_NOPE], kv[..., MLA_NOPE:]
    inv_freq = ROPE_THETA ** (-jnp.arange(0, MLA_ROPE, 2, dtype=jnp.float32) / MLA_ROPE)
    ang = positions.astype(jnp.float32)[..., None] * inv_freq
    cos, sin = jnp.cos(ang), jnp.sin(ang)
    q_pe = apply_rope(q_pe, cos[:, :, None, :], sin[:, :, None, :])
    k_pe = apply_rope(k_pe, cos, sin)
    o = block_causal_mla_attention(q_nope, q_pe, k_nope, k_pe, v)
    return o.reshape(B, S, MLA_MIX) @ w_out

def swiglu_ffn(x, w_gate_up, w_down):
    gu = x @ w_gate_up
    gate, up = gu[..., :FFN_HIDDEN], gu[..., FFN_HIDDEN:]
    return (jax.nn.silu(gate) * up) @ w_down

def first_inputs(seed: int = 0) -> dict:
    key = jax.random.key(seed)
    ks = iter(jax.random.split(key, 64))

    def dense(lead, fan_in, fan_out, scale=1.0):
        return jax.random.normal(next(ks), lead + (fan_in, fan_out), jnp.float32) * (scale * fan_in ** -0.5)

    def vec(shape, base, noise):
        return base + noise * jax.random.normal(next(ks), shape, jnp.float32)

    E, O = (N_EVEN,), (N_ODD,)
    x = jax.random.normal(next(ks), (BATCH, SEQ, D_MODEL), jnp.float32)
    positions = (jax.random.randint(next(ks), (BATCH, 1), 0, 4096, jnp.int32)
                 + jnp.arange(SEQ, dtype=jnp.int32)[None, :])

    even_scales = (1.0, 1.0, DN_BETA, 1.0, 1.0) + (1.0, 1.0, DN_BETA, 1.0, 1.0, 1.0)
    even_w_in = jnp.concatenate([dense(E, D_MODEL, c, s) for c, s in zip(GLA_SPLITS + RW_SPLITS, even_scales)], -1)

    mla_w_kv_b = jnp.concatenate([
        dense(O, MLA_KV_RANK, MLA_NOPE, 1.0).reshape(O + (MLA_KV_RANK, 1, MLA_NOPE)) * jnp.ones((1, MLA_HEADS, 1)),
        dense(O, MLA_KV_RANK, MLA_HEADS * MLA_V, DN_BETA).reshape(O + (MLA_KV_RANK, MLA_HEADS, MLA_V)),
    ], -1)
    mla_w_kv_b = mla_w_kv_b + 0.3 * dense(O, MLA_KV_RANK, MLA_HEADS * (MLA_NOPE + MLA_V)).reshape(mla_w_kv_b.shape) * jnp.concatenate([jnp.ones((MLA_NOPE,)), jnp.zeros((MLA_V,))])

    return {
        "x": x,
        "positions": positions,
        "even_w_in": even_w_in,
        "gla_gate_w2": dense(E, GLA_GATE_RANK, GLA_QK),
        "gla_gate_b": vec(E + (GLA_QK,), 0.0, 0.1),
        "gla_norm_g": vec(E + (GLA_DV,), 1.0, 0.02),
        "rwkv_mu": jax.random.uniform(next(ks), E + (RW_IN,), jnp.float32),
        "rwkv_w0": vec(E + (RW_W,), 0.0, 0.5),
        "rwkv_w2": dense(E, RW_DECAY_RANK, RW_W),
        "rwkv_a0": vec(E + (RW_W,), 0.0, 0.1),
        "rwkv_a2": dense(E, RW_A_RANK, RW_W),
        "rwkv_g2": dense(E, RW_GATE_RANK, RW_W),
        "rwkv_k_k": vec(E + (RW_W,), 0.85, 0.02),
        "rwkv_k_a": vec(E + (RW_W,), 1.0, 0.02),
        "rwkv_r_k": vec(E + (RW_HEADS, RW_N), 0.0, 0.1),
        "rwkv_ln_g": vec(E + (RW_W,), 1.0, 0.02),
        "rwkv_ln_b": vec(E + (RW_W,), 0.0, 0.02),
        "even_w_out": dense(E, EVEN_MIX, D_MODEL, DN_BETA),
        "mla_w_in": dense(O, D_MODEL, ODD_IN),
        "mla_q_norm_g": vec(O + (MLA_Q_RANK,), 1.0, 0.02),
        "mla_w_q_b": dense(O, MLA_Q_RANK, MLA_HEADS * (MLA_NOPE + MLA_ROPE)),
        "mla_kv_norm_g": vec(O + (MLA_KV_RANK,), 1.0, 0.02),
        "mla_w_kv_b": mla_w_kv_b.reshape(O + (MLA_KV_RANK, MLA_HEADS * (MLA_NOPE + MLA_V))),
        "mla_w_out": dense(O, MLA_MIX, D_MODEL, DN_BETA),
        "ffn_w_gate_up": dense((DEPTH,), D_MODEL, 2 * FFN_HIDDEN, DN_BETA),
        "ffn_w_down": dense((DEPTH,), FFN_HIDDEN, D_MODEL, DN_BETA),
        "ln_g": vec((DEPTH, 2, D_MODEL), 1.0, 0.02),
        "ln_b": vec((DEPTH, 2, D_MODEL), 0.0, 0.02),
    }

def first_block(x, positions, even_w_in, gla_gate_w2, gla_gate_b, gla_norm_g, rwkv_mu, rwkv_w0, rwkv_w2,
              rwkv_a0, rwkv_a2, rwkv_g2, rwkv_k_k, rwkv_k_a, rwkv_r_k, rwkv_ln_g, rwkv_ln_b, even_w_out,
              mla_w_in, mla_q_norm_g, mla_w_q_b, mla_kv_norm_g, mla_w_kv_b, mla_w_out,
              ffn_w_gate_up, ffn_w_down, ln_g, ln_b):
    for i in range(DEPTH):
        j = i // 2
        if i % 2 == 0:
            h = even_mixer(x, even_w_in[j], gla_gate_w2[j], gla_gate_b[j], gla_norm_g[j], rwkv_mu[j],
                           rwkv_w0[j], rwkv_w2[j], rwkv_a0[j], rwkv_a2[j], rwkv_g2[j], rwkv_k_k[j],
                           rwkv_k_a[j], rwkv_r_k[j], rwkv_ln_g[j], rwkv_ln_b[j], even_w_out[j])
        else:
            h = odd_mixer(x, positions, mla_w_in[j], mla_q_norm_g[j], mla_w_q_b[j], mla_kv_norm_g[j],
                          mla_w_kv_b[j], mla_w_out[j])
        x = layer_norm(DN_ALPHA * x + h, ln_g[i, 0], ln_b[i, 0])
        x = layer_norm(DN_ALPHA * x + swiglu_ffn(x, ffn_w_gate_up[i], ffn_w_down[i]), ln_g[i, 1], ln_b[i, 1])
    return x


DEPTH_2 = 1

HEAD_DIM = 64
N_HEADS_TOTAL = D_MODEL // HEAD_DIM
N_HEADS_MOBA = N_HEADS_TOTAL // 2
N_HEADS_SWA = N_HEADS_TOTAL - N_HEADS_MOBA
N_KV_SWA = 2
GQA_GROUP = N_HEADS_SWA // N_KV_SWA
MIX_WIDTH = N_HEADS_TOTAL * HEAD_DIM
MOBA_BLOCK = 256
MOBA_TOPK = 3
MOBA_QCHUNK = 16
SWA_WINDOW = 128
N_BUCKETS = 32
MAX_DISTANCE = 128
D_FF = 4 * D_MODEL
EPS = 1e-6
W_A = N_HEADS_MOBA * HEAD_DIM
W_QB = N_HEADS_SWA * HEAD_DIM
W_KVB = N_KV_SWA * HEAD_DIM
D_IN = 3 * W_A + W_QB + 2 * W_KVB


def rmsnorm(x, g):
    xf = x.astype(jnp.float32)
    y = xf * lax.rsqrt(jnp.mean(xf * xf, axis=-1, keepdims=True) + EPS)
    return (y * g.astype(jnp.float32)).astype(x.dtype)

def t5_bucket(dist):
    n = jnp.maximum(dist, 0)
    max_exact = N_BUCKETS // 2
    nf = jnp.maximum(n, 1).astype(jnp.float32)
    large = max_exact + (jnp.log(nf / max_exact) / math.log(MAX_DISTANCE / max_exact)
                         * (N_BUCKETS - max_exact)).astype(jnp.int32)
    large = jnp.minimum(large, N_BUCKETS - 1)
    return jnp.where(n < max_exact, n, large)

def moba_attention(q, k, v, bias_hb):
    B, H, S, dh = q.shape
    nb = -(-S // MOBA_BLOCK)
    sp = nb * MOBA_BLOCK
    padw = ((0, 0), (0, 0), (0, sp - S), (0, 0))
    q, k, v = jnp.pad(q, padw), jnp.pad(k, padw), jnp.pad(v, padw)
    kb = k.reshape(B, H, nb, MOBA_BLOCK, dh)
    vb = v.reshape(B, H, nb, MOBA_BLOCK, dh)
    k_mean = jnp.mean(kb.astype(jnp.float32), axis=3)
    gate = jnp.einsum('bhsd,bhnd->bhsn', q.astype(jnp.float32), k_mean)
    q_block = jnp.arange(sp) // MOBA_BLOCK
    fully_past = jnp.arange(nb)[None, :] < q_block[:, None]
    gate = jnp.where(fully_past, gate, -jnp.inf)
    n_sel = min(MOBA_TOPK, nb)
    sel_score, sel_idx = lax.top_k(gate, n_sel)
    sel_valid = jnp.isfinite(sel_score)
    scale = dh ** -0.5
    b_idx = jnp.arange(B)[:, None, None, None]
    h_idx = jnp.arange(H)[None, :, None, None]
    offs = jnp.arange(MOBA_BLOCK)

    def chunk(ci):
        q0 = ci * MOBA_QCHUNK
        qc = lax.dynamic_slice_in_dim(q, q0, MOBA_QCHUNK, axis=2)
        idx = lax.dynamic_slice_in_dim(sel_idx, q0, MOBA_QCHUNK, axis=2)
        valid = lax.dynamic_slice_in_dim(sel_valid, q0, MOBA_QCHUNK, axis=2)
        qpos = q0 + jnp.arange(MOBA_QCHUNK)
        k_sel = kb[b_idx, h_idx, idx]
        v_sel = vb[b_idx, h_idx, idx]
        s_sel = jnp.einsum('bhqd,bhqnjd->bhqnj', qc, k_sel).astype(jnp.float32) * scale
        kpos_sel = idx[..., None] * MOBA_BLOCK + offs
        s_sel = s_sel + bias_hb[h_idx[..., None], t5_bucket(qpos[:, None, None] - kpos_sel)]
        s_sel = jnp.where(valid[..., None], s_sel, -jnp.inf)
        ob = q0 // MOBA_BLOCK
        k_own = lax.dynamic_slice_in_dim(k, ob * MOBA_BLOCK, MOBA_BLOCK, axis=2)
        v_own = lax.dynamic_slice_in_dim(v, ob * MOBA_BLOCK, MOBA_BLOCK, axis=2)
        s_own = jnp.einsum('bhqd,bhjd->bhqj', qc, k_own).astype(jnp.float32) * scale
        dist = qpos[:, None] - (ob * MOBA_BLOCK + offs)[None, :]
        s_own = s_own + bias_hb[:, t5_bucket(dist)][None]
        s_own = jnp.where(dist >= 0, s_own, -jnp.inf)
        logits = jnp.concatenate(
            [s_sel.reshape(B, H, MOBA_QCHUNK, n_sel * MOBA_BLOCK), s_own], axis=-1)
        p = jax.nn.softmax(logits, axis=-1)
        p_sel = p[..., :n_sel * MOBA_BLOCK].reshape(B, H, MOBA_QCHUNK, n_sel, MOBA_BLOCK).astype(v.dtype)
        p_own = p[..., n_sel * MOBA_BLOCK:].astype(v.dtype)
        return (jnp.einsum('bhqnj,bhqnjd->bhqd', p_sel, v_sel)
                + jnp.einsum('bhqj,bhjd->bhqd', p_own, v_own))

    outs = lax.map(chunk, jnp.arange(sp // MOBA_QCHUNK))
    out = jnp.moveaxis(outs, 0, 2).reshape(B, H, sp, dh)
    return out[:, :, :S]

def swa_attention(q, k, v, bias_hb, sinks):
    B, HKV, G, S, dh = q.shape
    W = SWA_WINDOW
    nbq = S // W
    qb = q.reshape(B, HKV, G, nbq, W, dh)
    kb = k.reshape(B, HKV, nbq, W, dh)
    vb = v.reshape(B, HKV, nbq, W, dh)
    pad_prev = ((0, 0), (0, 0), (1, 0), (0, 0), (0, 0))
    k_band = jnp.concatenate([jnp.pad(kb[:, :, :-1], pad_prev), kb], axis=3)
    v_band = jnp.concatenate([jnp.pad(vb[:, :, :-1], pad_prev), vb], axis=3)
    s = jnp.einsum('bkgnqd,bknjd->bkgnqj', qb, k_band).astype(jnp.float32) * (dh ** -0.5)
    blk = jnp.arange(nbq)
    qpos = blk[:, None] * W + jnp.arange(W)[None, :]
    kpos = (blk[:, None] - 1) * W + jnp.arange(2 * W)[None, :]
    dist = qpos[:, :, None] - kpos[:, None, :]
    allowed = (dist >= 0) & (dist < W) & (kpos[:, None, :] >= 0)
    bias = bias_hb[:, t5_bucket(dist)].reshape(HKV, G, nbq, W, 2 * W)
    s = jnp.where(allowed, s + bias, -jnp.inf)
    sink = jnp.broadcast_to(sinks.astype(jnp.float32).reshape(1, HKV, G, 1, 1, 1), s.shape[:-1] + (1,))
    p = jax.nn.softmax(jnp.concatenate([s, sink], axis=-1), axis=-1)[..., :-1]
    out = jnp.einsum('bkgnqj,bknjd->bkgnqd', p.astype(v.dtype), v_band)
    return out.reshape(B, HKV, G, S, dh)

def token_mixer(h, w_in, w_out, sinks, bias_hb):
    B, S, _ = h.shape
    proj = h @ w_in
    qa, ka, va, qb, kb, vb = jnp.split(
        proj, [W_A, 2 * W_A, 3 * W_A, 3 * W_A + W_QB, 3 * W_A + W_QB + W_KVB], axis=-1)
    heads = lambda t, n: t.reshape(B, S, n, HEAD_DIM).transpose(0, 2, 1, 3)
    out_a = moba_attention(heads(qa, N_HEADS_MOBA), heads(ka, N_HEADS_MOBA),
                           heads(va, N_HEADS_MOBA), bias_hb[:N_HEADS_MOBA])
    out_a = out_a.transpose(0, 2, 1, 3).reshape(B, S, W_A)
    q_swa = qb.reshape(B, S, N_KV_SWA, GQA_GROUP, HEAD_DIM).transpose(0, 2, 3, 1, 4)
    out_b = swa_attention(q_swa, heads(kb, N_KV_SWA), heads(vb, N_KV_SWA),
                          bias_hb[N_HEADS_MOBA:], sinks)
    out_b = out_b.transpose(0, 3, 1, 2, 4).reshape(B, S, W_QB)
    return jnp.concatenate([out_a, out_b], axis=-1) @ w_out

def second_inputs(seed: int = 0) -> dict:
    key = jax.random.key(seed)
    ks = jax.random.split(key, 13)
    f32 = jnp.float32
    nrm = lambda k, shape, s: jax.random.normal(k, shape, f32) * s
    return {
        "x": nrm(ks[0], (BATCH, SEQ, D_MODEL), 1.0),
        "c": nrm(ks[1], (BATCH, D_MODEL), 1.0),
        "w_in": nrm(ks[2], (DEPTH_2, D_MODEL, D_IN), D_MODEL ** -0.5),
        "w_out": nrm(ks[3], (DEPTH_2, MIX_WIDTH, D_MODEL), MIX_WIDTH ** -0.5),
        "sinks": nrm(ks[4], (DEPTH_2, N_HEADS_SWA), 0.5),
        "rel_bias": nrm(ks[5], (N_BUCKETS, N_HEADS_TOTAL), 0.5),
        "w_ada": nrm(ks[6], (DEPTH_2, D_MODEL, 6 * D_MODEL), D_MODEL ** -0.5),
        "b_ada": nrm(ks[7], (DEPTH_2, 6 * D_MODEL), 0.02),
        "norm_gains": 1.0 + nrm(ks[8], (DEPTH_2, 4, D_MODEL), 0.05),
        "w1": nrm(ks[9], (DEPTH_2, D_MODEL, D_FF), D_MODEL ** -0.5),
        "b1": nrm(ks[10], (DEPTH_2, D_FF), 0.02),
        "w2": nrm(ks[11], (DEPTH_2, D_FF, D_MODEL), D_FF ** -0.5),
        "b2": nrm(ks[12], (DEPTH_2, D_MODEL), 0.02),
    }

def second_block(x, c, w_in, w_out, sinks, rel_bias, w_ada, b_ada, norm_gains, w1, b1, w2, b2):
    bias_hb = rel_bias.T
    c_act = jax.nn.silu(c)
    for l in range(DEPTH_2):
        mod = c_act @ w_ada[l] + b_ada[l]
        sh1, sc1, g1, sh2, sc2, g2 = [m[:, None, :] for m in jnp.split(mod, 6, axis=-1)]
        h = rmsnorm(x, norm_gains[l, 0]) * (1.0 + sc1) + sh1
        y = token_mixer(h, w_in[l], w_out[l], sinks[l], bias_hb)
        x = x + g1 * rmsnorm(y, norm_gains[l, 1])
        h = rmsnorm(x, norm_gains[l, 2]) * (1.0 + sc2) + sh2
        y = jnp.square(jax.nn.relu(h @ w1[l] + b1[l])) @ w2[l] + b2[l]
        x = x + g2 * rmsnorm(y, norm_gains[l, 3])
    return x


def setup_inputs(seed=0):
    out = dict(first_inputs(seed))
    for name, value in second_inputs(seed + 1).items():
        if name != "x":
            out[name + "_2"] = value
    return out


def reference(
    x, positions, even_w_in, gla_gate_w2, gla_gate_b, gla_norm_g, rwkv_mu, rwkv_w0, rwkv_w2,
    rwkv_a0, rwkv_a2, rwkv_g2, rwkv_k_k, rwkv_k_a, rwkv_r_k, rwkv_ln_g, rwkv_ln_b, even_w_out,
    mla_w_in, mla_q_norm_g, mla_w_q_b, mla_kv_norm_g, mla_w_kv_b, mla_w_out, ffn_w_gate_up,
    ffn_w_down, ln_g, ln_b, c_2, w_in_2, w_out_2, sinks_2, rel_bias_2, w_ada_2, b_ada_2,
    norm_gains_2, w1_2, b1_2, w2_2, b2_2,
):
    x = first_block(
        x, positions, even_w_in, gla_gate_w2, gla_gate_b, gla_norm_g, rwkv_mu, rwkv_w0, rwkv_w2,
        rwkv_a0, rwkv_a2, rwkv_g2, rwkv_k_k, rwkv_k_a, rwkv_r_k, rwkv_ln_g, rwkv_ln_b,
        even_w_out, mla_w_in, mla_q_norm_g, mla_w_q_b, mla_kv_norm_g, mla_w_kv_b, mla_w_out,
        ffn_w_gate_up, ffn_w_down, ln_g, ln_b,
    )
    return second_block(
        x, c_2, w_in_2, w_out_2, sinks_2, rel_bias_2, w_ada_2, b_ada_2, norm_gains_2, w1_2,
        b1_2, w2_2, b2_2,
    )


_drawn_inputs = setup_inputs


def setup_inputs(seed=0):
    import zlib

    import numpy as np

    out = dict(_drawn_inputs(seed))
    spreads = {}
    factors = {'gla_gate_w2': 4.094,
     'gla_gate_b': 8.0,
     'gla_norm_g': 8.0,
     'rwkv_w2': 3.735,
     'rwkv_a0': 8.0,
     'rwkv_k_k': 8.0,
     'rwkv_k_a': 8.0,
     'rwkv_r_k': 4.03,
     'rwkv_ln_g': 8.0,
     'rwkv_ln_b': 8.0,
     'mla_q_norm_g': 8.0,
     'mla_kv_norm_g': 8.0,
     'sinks_2': 8.0,
     'b1_2': 6.953,
     'b2_2': 8.0}
    for name, (base, spread) in spreads.items():
        noise = np.random.default_rng([zlib.crc32(name.encode()), seed]).standard_normal(out[name].shape)
        drawn = base * np.exp(spread * noise) if base else spread * noise
        out[name] = __import__('jax').numpy.asarray(drawn.astype(out[name].dtype))
    for name, factor in factors.items():
        out[name] = (out[name] * factor).astype(out[name].dtype)
    return out
```

```python
from contextlib import ExitStack

import numpy as np

import concourse.bass as bass
from concourse import mybir

P = 128
S = 256
D = 1024
F32 = mybir.dt.float32
I32 = mybir.dt.int32
ALU = mybir.AluOpType
ACT = mybir.ActivationFunctionType
AX = mybir.AxisListType.X

ALPHA = 4.0 ** 0.25
LN_EPS = 1e-5
RMS_EPS = 1e-6
GN_EPS = 64e-5
FFN = 2816
DFF = 4096
DECAY = float(np.exp(-0.5))
MLA_SCALE = 96.0 ** -0.5
NEG = -1e30

NAMES = (["ident", "cinc", "cexc", "strict", "incl", "heads"]
         + [f"lvl{i}" for i in range(7)] + [f"acc{i}" for i in range(7)] + ["after", "upto", "ones", "swap"])
COLS = {n: 128 * i for i, n in enumerate(NAMES)}
WIDE = 128 * len(NAMES)


def constants():
    s = np.arange(128)[:, None]
    t = np.arange(128)[None, :]
    out = {"ident": s == t, "strict": s < t, "incl": s <= t, "heads": s // 64 == t // 64,
           "cinc": (s <= t) * 1.0 - (s < 64), "cexc": (s < t) * 1.0 - (s < 64),
           "after": s > t, "upto": s <= t, "ones": (s >= 0) & (t >= 0), "swap": s == (t + 64) % 128}
    for i in range(7):
        m = 1 << i
        same = s // (2 * m) == t // (2 * m)
        right = (t // m) % 2 == 1
        out[f"lvl{i}"] = same & right & ((s // m) % 2 == 0)
        edge = t // (2 * m) * (2 * m) + m
        out[f"acc{i}"] = np.where(right, (s >= edge) & (s <= t), (s > t) & (s < edge))
    return np.concatenate([out[n].astype(np.float32) for n in NAMES], 1)


def bucket_rows():
    n = np.clip(255 - np.arange(384), 0, None)
    nf = np.maximum(n, 1).astype(np.float32)
    large = 16 + (np.log(nf / np.float32(16)) / np.float32(np.log(8.0)) * np.float32(16)).astype(np.int32)
    b = np.where(n < 16, n, np.minimum(large, 31))
    dist = 255 - np.arange(384)
    hot = (np.arange(32)[:, None] == b[None]).astype(np.float32)
    moba = np.where(dist >= 0, 0.0, NEG)
    swa = np.where((dist >= 0) & (dist < 128), 0.0, NEG)
    mask = np.concatenate([np.tile(moba, (8, 1)), np.tile(swa, (8, 1))]).astype(np.float32)
    return hot, mask


def mla_mask():
    q = np.arange(128)[:, None]
    k = np.arange(256)[None]
    near = np.where(k[:, :128] // 64 <= q // 64, 0.0, NEG)
    far = np.where(k // 64 <= (q + 128) // 64, 0.0, NEG)
    return np.concatenate([near, far], 1).astype(np.float32)


def rope_rows():
    f = (np.float32(10000.0) ** (-np.arange(0, 32, 2, dtype=np.float32) / np.float32(32))).astype(np.float32)
    return np.tile(f[None], (128, 1))


class Queue:

    def __init__(self, sem):
        self.sem, self.n, self.todo, self.met = sem, 0, [], {}

    def wait(self, *after):
        for tok in after:
            if tok is None:
                continue
            if isinstance(tok, list):
                self.wait(*tok)
                continue
            sem, value = tok
            if self.met.get(sem.name, 0) < value:
                self.met[sem.name] = value
                self.todo.append(lambda e, sem=sem, value=value: e.wait_ge(sem, value))

    def do(self, fn, *after):
        self.wait(*after)
        self.n += 1
        self.todo.append(lambda e: fn(e).then_inc(self.sem, 1))
        return (self.sem, self.n)

    def start(self, fn, *after):
        self.wait(*after)
        self.todo.append(fn)

    def now(self):
        return (self.sem, self.n)

    def emit(self, e):
        for fn in self.todo:
            fn(e)


class Dma:

    def __init__(self, sem):
        self.sem, self.n = sem, 0

    def issue(self, queue, out, in_, *after, **kw):
        self.n += 16
        queue.start(lambda e: e.dma_start(out, in_, **kw).then_inc(self.sem, 16), *after)
        return (self.sem, self.n)


class Buf:

    def __init__(self, ap, dma=None):
        self.ap, self.dma, self.free = ap, dma, []


def program(nc, a):
    ctx = ExitStack()
    with ctx:
        def sb(name, shape, dt=F32):
            return ctx.enter_context(nc.sbuf_tensor(name, shape, dt))[(slice(None),) * len(shape)]

        def sem(name):
            return ctx.enter_context(nc.semaphore(name))

        pe, dve, act, pool, sp = (Queue(sem(n)) for n in ("s_pe", "s_dve", "s_act", "s_pool", "s_sp"))

        NSLOT = 5
        ring = [Buf(sb(f"ring{i}", [P, 2048]), Dma(sem(f"s_ring{i}"))) for i in range(NSLOT)]
        psum = [Buf(ctx.enter_context(nc.psum_tensor(f"ps{i}", [P, 512], F32))) for i in range(8)]
        turn = {"ring": 0, "psum": 0, "banks": 8}

        X = sb("X", [P, 2, D])
        XN = sb("XN", [P, 2, D])
        XT = sb("XT", [P, 8, S])
        CST = sb("CST", [P, WIDE])
        VEC = sb("VEC", [P, 2, P])
        GB = sb("GB", [P, 2, D])
        SM = sb("SM", [P, 64])
        ROW = sb("ROW", [1, 128])
        ARENA = 30400
        AR = sb("AR", [P, ARENA])

        def cst(name):
            return CST[:, COLS[name]:COLS[name] + 128]

        ident = cst("ident")

        def at(off, *shape):
            n = int(np.prod(shape))
            assert off + n <= ARENA, (off, n)
            v = AR[:, off:off + n]
            if len(shape) == 1:
                return v
            names = "abcd"[:len(shape)]
            kw = {c: k for c, k in zip(names[1:], shape[1:])}
            return v.rearrange(f"p ({' '.join(names)}) -> p {' '.join(names)}", **kw)

        s_const = Dma(sem("s_const"))
        s_gain = Dma(sem("s_gain"))

        def bank():
            b = psum[turn["psum"] % turn["banks"]]
            turn["psum"] += 1
            return b

        def load(src, n, dims=None):
            slot = ring[turn["ring"] % NSLOT]
            turn["ring"] += 1
            dst = slot.ap[:, 0:n]
            if dims:
                dst = dst.rearrange("p (c n) -> p c n", c=dims)
            return slot, dst, slot.dma.issue(sp, dst, src, slot.free)

        def mm(out, lhsT, rhs, first, last, *after):
            pe.start(lambda e: e.matmul(out, lhsT, rhs, start=first, stop=last), *after)

        def mm_last(out, lhsT, rhs, first, last, *after):
            return pe.do(lambda e: e.matmul(out, lhsT, rhs, start=first, stop=last), *after)

        def tr(out, in_, *after, np_=128):
            pe.start(lambda e: e.transpose(out, in_, ident[0:np_, 0:np_]), *after)

        def tr_last(out, in_, *after, np_=128):
            return pe.do(lambda e: e.transpose(out, in_, ident[0:np_, 0:np_]), *after)

        def tt(q, out, x, y, op, *after):
            return q.do(lambda e: e.tensor_tensor(out, x, y, op), *after)

        def ts(q, out, x, s1, s2, op0, op1, *after):
            if s2 is None:
                return q.do(lambda e: e.tensor_scalar(out, x, s1, None, op0), *after)
            return q.do(lambda e: e.tensor_scalar(out, x, s1, s2, op0, op1), *after)

        def stt(out, x, s, y, op0, op1, *after):
            return dve.do(lambda e: e.scalar_tensor_tensor(out, x, s, y, op0, op1), *after)

        def fn(out, x, f, *after, **kw):
            return act.do(lambda e: e.activation(out, x, f, **kw), *after)

        def recip(out, x, *after):
            return dve.do(lambda e: e.reciprocal(out, x), *after)

        def total(out, x, *after):
            return dve.do(lambda e: e.tensor_reduce(out, x, AX, ALU.add), *after)

        def ttr(out, x, y, start, op0, op1, acc, *after):
            return dve.do(lambda e: e.tensor_tensor_reduce(out, x, y, 1.0, start, op0, op1, acc), *after)

        def fill(q, out, value, *after):
            return q.do(lambda e: e.memset(out, value), *after)

        def select(out, mask, x, *after):
            return dve.do(lambda e: e.copy_predicated(out, mask, x), *after)

        def moments(out, x, *after):
            return dve.do(lambda e: e.bn_stats(out, x), *after)

        def gather_moments(out, x, *after):
            return dve.do(lambda e: e.bn_aggr(out, x), *after)

        def cp(q, out, x, *after):
            if q is act:
                return fn(out, x, ACT.Copy, *after)
            return q.do(lambda e: e.tensor_copy(out, x), *after)


        def columns(W, kc, cols, xT, got, *after, width=256):
            i = 0
            while i < len(cols):
                b = bank()
                pair = cols[i:i + 2]
                c0, c1 = pair[0][0], pair[-1][0] + pair[-1][1]
                n = c1 - c0
                slot, w, there = load(W[:, c0:c1].rearrange("(c p) n -> p c n", p=P), kc * n, kc)
                for h, (start, count) in enumerate(pair):
                    for c in range(kc):
                        last = c == kc - 1
                        f = mm_last if last else mm
                        done = f(b.ap[0:count, h * 256:h * 256 + 256],
                                 w[:, c, start - c0:start - c0 + count], xT[:, c, :],
                                 c == 0, last, there, b.free, *after)
                slot.free = [done]
                got(i, b, len(pair), done)
                i += 2

        def rows(W, kc, c0, n, xT, got, bias=None, *after):
            parts = [(o, min(512, n - o)) for o in range(0, n, 512)]
            bs = [[bank() for _ in parts] for _ in range(2)]
            per = max(1, 2048 // n)
            for k0 in range(0, kc, per):
                k1 = min(kc, k0 + per)
                src = W[k0 * P:k1 * P, c0:c0 + n].rearrange("(c p) n -> p c n", p=P)
                slot, w, there = load(src, (k1 - k0) * n, k1 - k0)
                for t in range(2):
                    for j, (o, m) in enumerate(parts):
                        for c in range(k0, k1):
                            last = c == kc - 1 and bias is None
                            f = mm_last if c == k1 - 1 else mm
                            done = f(bs[t][j].ap[:, 0:m], xT[:, c, t * P:t * P + P],
                                     w[:, c - k0, o:o + m], c == 0, last,
                                     there, bs[t][j].free if c == 0 else None, *after)
                        if k1 == kc:
                            if bias is not None:
                                done = mm_last(bs[t][j].ap[:, 0:m], ones1, bias[0:1, o:o + m], False, True)
                            got(t, o, m, bs[t][j], done)
                slot.free = [pe.now()]

        eps_ln, eps_rms, eps_gn = SM[:, 0:1], SM[:, 1:2], SM[:, 2:3]
        ones1 = ROW[0:1, 0:128]
        STAT = sb("STAT", [P, 2, 16])

        def rstd(out, var, eps, scale, *after):
            k = fn(out, var, ACT.Sqrt, *after, bias=eps, scale=scale)
            return recip(out, out, k)

        def transposed(src, dst, c_n, ready, scale=None, shift=None, free=None):
            done = []
            for c in range(0, c_n, 2):
                b = bank()
                m = min(2, c_n - c)
                for i in range(m):
                    for t in range(2):
                        f = tr_last if (i, t) == (m - 1, 1) else tr
                        k = f(b.ap[:, i * 256 + t * P:i * 256 + t * P + P],
                              src[:, t, (c + i) * P:(c + i + 1) * P], ready[t], b.free)
                use = act if (c // 2) % 2 else dve
                if scale is None:
                    d = cp(use, dst[:, c:c + m, :], b.ap[:, 0:m * 256].rearrange("p (c t) -> p c t", c=m), k, free)
                else:
                    for i in range(m):
                        sc = scale(c + i)
                        sh = shift(c + i) if shift else None
                        x = b.ap[:, i * 256:i * 256 + 256]
                        if use is act:
                            if sh is None:
                                d = fn(dst[:, c + i, :], x, ACT.Copy, k, free, scale=sc)
                            else:
                                d = fn(dst[:, c + i, :], x, ACT.Identity, k, free, bias=sh, scale=sc)
                        elif sh is None:
                            d = ts(dve, dst[:, c + i, :], x, sc, None, ALU.mult, None, k, free)
                        else:
                            d = ts(dve, dst[:, c + i, :], x, sc, sh, ALU.mult, ALU.add, k, free)
                b.free = [d]
                done.append(d)
            return done

        def gain_rows(i, *after):
            g = a["ln_g"].rearrange("a b d -> (a b) d")[i:i + 1, :]
            b = a["ln_b"].rearrange("a b d -> (a b) d")[i:i + 1, :]
            s_gain.issue(sp, GB[:, 0, :], g.to_broadcast([P, D]), *after)
            return s_gain.issue(sp, GB[:, 1, :], b.to_broadcast([P, D]), *after)

        state = {"x": None, "gb": None}

        def residual_norm(i):
            def got(t, o, m, b, done):
                k = stt(XN[:, t, o:o + m], X[:, t, o:o + m], ALPHA, b.ap[:, 0:m], ALU.mult, ALU.add,
                        done, state["x"])
                b.free = [k]
                k = moments(STAT[:, t, 6 * (o // 512):6 * (o // 512) + 6], XN[:, t, o:o + m], k)
                state[("st", t, o)] = k
            return got

        def finish_norm(i, xt_free):
            ready = []
            for t in range(2):
                k = gather_moments(STAT[:, t, 12:14], STAT[:, t, 0:12], state[("st", t, 0)], state[("st", t, 512)])
                k = rstd(STAT[:, t, 14:15], STAT[:, t, 13:14], eps_ln, 1.0, k)
                k = ts(dve, XN[:, t, :], XN[:, t, :], STAT[:, t, 12:13], STAT[:, t, 14:15],
                       ALU.subtract, ALU.mult, k)
                ready.append(k)
            ev = transposed(XN, XT, 8, ready, lambda c: VEC[:, 0, 31 + 8 * i + c:32 + 8 * i + c],
                            lambda c: VEC[:, 0, 63 + 8 * i + c:64 + 8 * i + c], xt_free)
            out = []
            for t in range(2):
                k = tt(pool, X[:, t, :], XN[:, t, :], GB[:, 0, :], ALU.mult, ready[t], state["gb"])
                out.append(tt(pool, X[:, t, :], X[:, t, :], GB[:, 1, :], ALU.add, k))
            state["x"] = out
            state["xn"] = ready
            if i < 3:
                state["gb"] = gain_rows(i + 1, out)
            return ev

        t_x = s_const.issue(act, X[:, :, :], a["x"].rearrange("b (t p) d -> p (b t) d", p=P))
        s_c2 = Dma(sem("s_c2"))
        t_cst = s_c2.issue(act, CST[:, :], a["consts"])
        VR = at(0, 2, 128)
        k = fill(pool, VR, 0.0)
        fill(pool, eps_ln, LN_EPS)
        fill(pool, eps_rms, RMS_EPS)
        fill(pool, eps_gn, GN_EPS)
        fill(pool, SM[:, 3:4], 1.0)
        k_sm = fill(pool, SM[:, 4:6], 0.0)
        k_sm = fill(pool, SM[64:128, 4:5], 1.0, k_sm)
        k_sm = fill(pool, SM[0:64, 5:6], 1.0, k_sm)
        t_eps = fill(pool, ones1, 1.0, k_sm)
        for q in (pe, dve, act, pool):
            q.wait(t_eps, t_cst)
        s_vec = Dma(sem("s_vec"))

        def vrow(half, r, src, n):
            full = n // P
            flat = src
            if full:
                s_vec.issue(act, VR[r:r + full, half, :], flat[:, 0:full * P].rearrange("a (r p) -> (a r) p", p=P), k)
            if n % P:
                s_vec.issue(act, VR[r + full:r + full + 1, half, 0:n % P], flat[:, full * P:n], k)

        for r, name, n in ((0, "rwkv_mu", 1824), (15, "rwkv_k_k", 512), (19, "rwkv_k_a", 512),
                           (23, "rwkv_a0", 512)):
            vrow(0, r, a[name], n)
        vrow(0, 27, a["rwkv_r_k"].rearrange("a h n -> a (h n)"), 512)
        s_vec.issue(act, VR[31:63, 0, :], a["ln_g"].rearrange("a b (r p) -> (a b r) p", p=P), k)
        s_vec.issue(act, VR[63:95, 0, :], a["ln_b"].rearrange("a b (r p) -> (a b r) p", p=P), k)
        vrow(0, 95, a["mla_q_norm_g"], 768)
        vrow(0, 101, a["mla_kv_norm_g"], 256)
        vrow(1, 0, a["b1_2"], 4096)
        vrow(1, 32, a["b_ada_2"], 6144)
        s_vec.issue(act, VR[80:112, 1, :], a["norm_gains_2"].rearrange("a b (r p) -> (a b r) p", p=P), k)
        vrow(1, 112, a["c_2"], 1024)
        t_vec = (s_vec.sem, s_vec.n)
        O_ = {}
        off = [256]

        def take(name, *shape):
            n = int(np.prod(shape))
            O_[name] = at(off[0], *shape)
            off[0] += n
            return O_[name]

        GW2 = take("gw2", 256)
        W2A2 = take("w2a2", 512)
        G2 = take("g2", 2, 512)
        LNG = take("lng", 512)
        LNB = take("lnb", 512)
        GNG = take("gng", 128)
        RW0 = sb("RW0", [1, 768])
        s_ev = Dma(sem("s_ev"))
        s_ev.issue(act, GW2[0:16, :], a["gla_gate_w2"][0])
        s_ev.issue(act, W2A2[0:64, :], a["rwkv_w2"][0])
        s_ev.issue(act, W2A2[64:128, :], a["rwkv_a2"][0])
        s_ev.issue(act, G2[:, 0, :], a["rwkv_g2"][0, 0:128, :])
        s_ev.issue(act, G2[0:32, 1, :], a["rwkv_g2"][0, 128:160, :])
        s_ev.issue(act, LNG, a["rwkv_ln_g"].to_broadcast([P, 512]))
        s_ev.issue(act, LNB, a["rwkv_ln_b"].to_broadcast([P, 512]))
        s_ev.issue(act, GNG, a["gla_norm_g"].to_broadcast([P, 128]))
        s_ev.issue(act, RW0[:, 0:512], a["rwkv_w0"])
        s_ev.issue(act, RW0[:, 512:768], a["gla_gate_b"])
        t_ev = (s_ev.sem, s_ev.n)
        state["gb"] = gain_rows(0)
        state["x"] = t_x

        for h in range(2):
            b = bank()
            k = tr_last(b.ap[:, 0:128], VR[:, h, :], t_vec, t_cst)
            t_v = cp(dve, VEC[:, h, :], b.ap[:, 0:128], k)
            b.free = [t_v]
        t_xt = transposed(X, XT, 8, [[t_x, t_cst]] * 2)

        def vec(half, i):
            return VEC[:, half, i:i + 1]

        WIN = a["even_w_in"][0]
        dm = off[0]
        Dm = take("D", 15, 256)
        PT = at(off[0], 15, 257)
        base = off[0]

        zero = fill(dve, PT[:, :, 0:1], 0.0)
        rwcols = [(1552 + 128 * i, 128) for i in range(14)] + [(3344, 32)]
        ptd = {}

        def got_rw(i, b, n, done):
            if i + n == 15:
                k = cp(act, PT[0:32, 14, 1:257], b.ap[0:32, 0:256], done)
            else:
                k = cp(act, PT[:, i:i + n, 1:257], b.ap[:, :].rearrange("p (c t) -> p c t", c=2), done)
            b.free = [k]
            for j in range(i, i + n):
                pn = 32 if j == 14 else 128
                d = tt(dve, Dm[0:pn, j, :], PT[0:pn, j, 0:256], PT[0:pn, j, 1:257], ALU.subtract, k, zero)
                ptd[j] = stt(Dm[0:pn, j, :], Dm[0:pn, j, :], VEC[0:pn, 0, j:j + 1], PT[0:pn, j, 1:257],
                             ALU.mult, ALU.add, d, t_v)

        columns(WIN, 8, rwcols[12:], XT, lambda i, b, n, done: got_rw(i + 12, b, n, done), t_xt)
        columns(WIN, 8, rwcols[:12], XT, got_rw, t_xt)

        off[0] += 15 * 257
        GQK = take("gqk", 4, 256)
        GLR = take("glr", 256)
        GV = take("gv", 2, 512)
        GG = take("gg", 2, 512)
        gl = {}

        def got_qk(i, b, n, done):
            src = b.ap[:, :].rearrange("p (c t) -> p c t", c=2)
            if i == 0:
                gl["q"] = fn(GQK[:, 0:2, :], src, ACT.Copy, done, scale=0.125)
                b.free = [gl["q"]]
            else:
                gl["k"] = cp(act, GQK[:, 2:4, :], src, done)
                b.free = [gl["k"]]

        def got_lr(i, b, n, done):
            gl["lr"] = cp(act, GLR[0:16, :], b.ap[0:16, 0:256], done)
            b.free = [gl["lr"]]

        def got_vg(t, o, m, b, done):
            if o == 0:
                gl["v", t] = cp(act, GV[:, t, :], b.ap[:, :], done)
            else:
                gl["v", t] = fn(GG[:, t, :], b.ap[:, :], ACT.Silu, done)
                gl["g", t] = gl["v", t]
            b.free = [gl["v", t]]

        def gla_projections():
            columns(WIN, 8, [(1536, 16)], XT, got_lr)
            columns(WIN, 8, [(0, 128), (128, 128), (256, 128), (384, 128)], XT, got_qk)
            rows(WIN, 8, 512, 1024, XT, got_vg)

        SIG = take("sig", 2, 512)
        ee = off[0]
        EE = take("ee", 3, 4, 256)
        AA = take("aa", 4, 256)
        KK = take("kk", 4, 256)
        KP = take("kp", 4, 256)
        CAR = take("car", 4, 2, 2, 128)
        kt = off[0]
        KT = take("kt", 4, 256)
        BT = take("bt", 4, 256)
        G = take("g", 2, 512)
        VT = take("vt", 2, 512)
        KB = G2
        S0 = at(dm + 3072, 4, 64)
        RHS = at(dm + 3328, 512)
        RKM = take("rkm", 4, 8)
        SML = take("sml", 128)
        r_, k_, v_ = Dm[:, 0:4, :], Dm[:, 4:8, :], Dm[:, 8:12, :]
        t_th = fn(Dm[0:64, 12, :], Dm[0:64, 12, :], ACT.Tanh, ptd[12])
        t_sg = fn(Dm[:, 13, :], Dm[:, 13, :], ACT.Sigmoid, ptd[13])
        t_sg = fn(Dm[0:32, 14, :], Dm[0:32, 14, :], ACT.Sigmoid, ptd[14])
        t_sig = []
        for t in range(2):
            b = bank()
            mm(b.ap[:, :], Dm[0:64, 12, t * P:t * P + P], W2A2[0:64, :], True, False, t_th, t_ev, b.free)
            k = mm_last(b.ap[:, :], ones1, RW0[0:1, 0:512], False, True, t_eps)
            t_sig.append(fn(SIG[:, t, :], b.ap[:, :], ACT.Sigmoid, k))
            b.free = [t_sig[-1]]
        t_a = []
        for i in range(4):
            b = bank()
            k = mm_last(b.ap[:, 0:256], W2A2[64:128, i * P:i * P + P], Dm[64:128, 12, :], True, True,
                        ptd[12], t_ev, b.free)
            t_a.append(fn(AA[:, i, :], b.ap[:, 0:256], ACT.Sigmoid, k, t_v, bias=vec(0, 23 + i)))
            b.free = [t_a[-1]]
        t_g = []
        for t in range(2):
            b = bank()
            mm(b.ap[:, :], Dm[:, 13, t * P:t * P + P], G2[:, 0, :], True, False, t_sg, t_ev, b.free)
            k = mm_last(b.ap[:, :], Dm[0:32, 14, t * P:t * P + P], G2[0:32, 1, :], False, True)
            t_g.append(cp(act, G[:, t, :], b.ap[:, :], k))
            b.free = [t_g[-1]]
        t_e = {}
        for i in range(4):
            b = bank()
            for w, name in enumerate(("cinc", "cexc")):
                for t in range(2):
                    f = mm_last if (w, t) == (1, 1) else mm
                    k = f(b.ap[:, w * 256 + t * P:w * 256 + t * P + P], SIG[:, t, i * P:i * P + P],
                          cst(name), True, True, t_sig[t], b.free)
            fn(EE[:, 0, i, :], b.ap[:, 0:256], ACT.Exp, k, scale=-DECAY)
            fn(EE[:, 1, i, :], b.ap[:, 0:256], ACT.Exp, k, scale=DECAY)
            t_e[i] = fn(EE[:, 2, i, :], b.ap[:, 256:512], ACT.Exp, k, scale=-DECAY)
            b.free = [t_e[i]]
        b = bank()
        for i in range(4):
            mm(b.ap[:, i:i + 1], SIG[:, 0, i * P:i * P + P], SM[:, 4:5], True, False, b.free)
            k = mm_last(b.ap[:, i:i + 1], SIG[:, 1, i * P:i * P + P], SM[:, 5:6], False, True)
        t_gm = fn(SML[:, 0:4], b.ap[:, 0:4], ACT.Exp, k, scale=-DECAY)
        b.free = [t_gm]
        t_kk = []
        for i in range(4):
            k = ts(dve, KK[:, i, :], Dm[:, 4 + i, :], vec(0, 15 + i), None, ALU.mult, None, ptd[4 + i])
            t_kk.append(tt(dve, KP[:, i, :], KK[:, i, :], KK[:, i, :], ALU.mult, k))
        sq = []
        for i in range(0, 4, 2):
            b = bank()
            mm(b.ap[:, 0:256], cst("heads"), KP[:, i, :], True, True, t_kk[i], b.free)
            k = mm_last(b.ap[:, 256:512], cst("heads"), KP[:, i + 1, :], True, True, t_kk[i + 1])
            k = ts(dve, KP[:, i:i + 2, :], b.ap[:, :].rearrange("p (c t) -> p c t", c=2), 1e-24, None,
                   ALU.max, None, k)
            b.free = [k]
            k = fn(KP[:, i:i + 2, :], KP[:, i:i + 2, :], ACT.Sqrt, k)
            k = recip(KP[:, i:i + 2, :], KP[:, i:i + 2, :], k)
            sq.append(tt(dve, KK[:, i:i + 2, :], KK[:, i:i + 2, :], KP[:, i:i + 2, :], ALU.mult, k))
        tl = []
        for i in range(4):
            ka = vec(0, 19 + i)
            k = ts(dve, KP[:, i, :], AA[:, i, :], 1.0, ka, ALU.subtract, ALU.mult, t_a[i], sq)
            k = stt(KP[:, i, :], KP[:, i, :], 1.0, Dm[:, 4 + i, :], ALU.add, ALU.mult, k)
            tl.append(tt(dve, KT[:, i, :], KP[:, i, :], EE[:, 1, i, :], ALU.mult, k, t_e[i]))
            tl.append(stt(CAR[:, i, :, 0, :], KK[:, i, :].rearrange("p (a b) -> p a b", a=2), -1.0,
                          EE[:, 2, i, :].rearrange("p (a b) -> p a b", a=2), ALU.mult, ALU.mult, t_e[i]))
            k2 = tt(pool, AA[:, i, :], AA[:, i, :], KK[:, i, :], ALU.mult, sq, t_a[i], k)
            tl.append(tt(pool, BT[:, i, :], AA[:, i, :], EE[:, 1, i, :], ALU.mult, k2, t_e[i]))
            tl.append(tt(pool, CAR[:, i, :, 1, :], Dm[:, i, :].rearrange("p (a b) -> p a b", a=2),
                         EE[:, 0, i, :].rearrange("p (a b) -> p a b", a=2), ALU.mult, t_e[i], ptd[i]))
            tl.append(tt(pool, KP[:, i, :], KP[:, i, :], Dm[:, i, :], ALU.mult, k, tl[-4]))
        t_til = tl
        k = fill(pool, RKM, 0.0)
        for i in range(4):
            for hh in range(2):
                k = cp(pool, RKM[64 * hh:64 * hh + 64, i, 2 * i + hh:2 * i + hh + 1],
                       VEC[64 * hh:64 * hh + 64, 0, 27 + i:28 + i], k, t_v)
        t_rkm = k
        b = bank()
        for t in range(2):
            for i in range(4):
                f = mm_last if (t, i) == (1, 3) else mm
                k = f(b.ap[:, 8 * t:8 * t + 8], KP[:, i, t * P:t * P + P], RKM[:, i, :], i == 0, i == 3,
                      t_til, t_rkm, b.free)
        t_bon = cp(dve, SML[:, 8:24], b.ap[:, 0:16], k)
        b.free = [t_bon]
        t_vt = []
        for t in range(2):
            b = bank()
            for i in range(4):
                f = tr_last if i == 3 else tr
                k = f(b.ap[:, i * P:i * P + P], Dm[:, 8 + i, t * P:t * P + P], ptd[8 + i], b.free)
            t_vt.append(cp(act, VT[:, t, :], b.ap[:, :], k))
            b.free = [t_vt[-1]]
        for w, src in enumerate((KT, BT)):
            b = bank()
            for i in range(4):
                f = tr_last if i == 3 else tr
                k = f(b.ap[:, i * P:i * P + P], src[:, i, 0:P], b.free)
            t_kb = cp(act, KB[:, w, :], b.ap[:, :], k, t_g)
            b.free = [t_kb]

        AAB = at(base, 16, 128)
        PP = at(base + 2048, 8, 128)
        AAK = at(ee + 2048, 16, 128)
        ARB = at(ee + 4096, 16, 128)
        ARK = take("ark", 16, 128)
        TI = at(dm, 16, 128)
        PP2 = at(dm + 2048, 8, 128)
        TJ = at(kt, 16, 128)
        ALA = at(ee, 16, 128)
        t_m = {}
        for s in range(16):
            t, h = s // 8, s % 8
            r = slice(64 * (h % 2), 64 * (h % 2) + 64)
            b = bank()
            for j, lhs in enumerate((BT, KT)):
                k = (mm_last if j else mm)(
                    b.ap[:, 256 * j:256 * j + 256], lhs[r, h // 2, t * P:t * P + P],
                    CAR[r, h // 2, t, :, :].rearrange("p a b -> p (a b)"), True, True, t_til, t_bon, b.free)
            for i, (dst, m) in enumerate(((AAB, "strict"), (ARB, "incl"), (AAK, "strict"), (ARK, "incl"))):
                t_m[s] = tt(dve, dst[:, s, :], b.ap[:, 128 * i:128 * i + 128], cst(m), ALU.mult, k)
            b.free = [t_m[s]]
        gla_projections()
        NG = 4
        t_ti = [None] * NG
        t_tj = [None] * NG
        t_al = [None] * NG
        t_pp = [None] * NG

        def group(x, g):
            return x[:, 4 * g:4 * g + 4, :]

        def pview(g):
            return PP[:, 4 * g:4 * g + 4, :] if g < 2 else PP2[:, 4 * g - 8:4 * g - 4, :]

        def flat(x):
            return x.rearrange("p s t -> p (s t)")

        bc = lambda name: cst(name).unsqueeze(1).to_broadcast([P, 4, P])
        free_al = [None] * NG
        for lv in range(7):
            for g in range(NG):
                need = t_m[4 * g + 3]
                t_al[g] = tt(pool, group(ALA, g), group(AAB, g), bc(f"lvl{lv}"), ALU.mult, need, t_til,
                             free_al[g])
                b = bank()
                for s in range(4):
                    k = (mm_last if s == 3 else mm)(
                        b.ap[:, s * P:s * P + P], ALA[:, 4 * g + s, :],
                        ident if lv == 0 else TI[:, 4 * g + s, :], True, True,
                        t_al[g], t_ti[g], b.free)
                free_al[g] = k
                if lv == 0:
                    t_ti[g] = tt(dve, group(TI, g), b.ap[:, :].rearrange("p (s t) -> p s t", s=4),
                                 bc("ident"), ALU.add, k, t_vt, t_til)
                    b.free = [t_ti[g]]
                    t_tj[g] = tt(dve, group(TJ, g), group(ALA, g), bc("ident"), ALU.add, t_al[g], t_kb)
                    free_al[g] = [k, t_tj[g]]
                else:
                    t_pp[g] = cp(act, pview(g), b.ap[:, :].rearrange("p (s t) -> p s t", s=4), k, t_ti[g], t_tj[g])
                    b.free = [t_pp[g]]
            if lv == 0:
                continue
            for g in range(NG):
                p_ = pview(g)
                bj = bank()
                for s in range(4):
                    kj = (mm_last if s == 3 else mm)(bj.ap[:, s * P:s * P + P], p_[:, s, :],
                                                     TJ[:, 4 * g + s, :], True, True, t_pp[g], t_tj[g], bj.free)
                if lv < 6:
                    bi = bank()
                    for s in range(4):
                        ki = (mm_last if s == 3 else mm)(bi.ap[:, s * P:s * P + P], TJ[:, 4 * g + s, :],
                                                         p_[:, s, :], True, True, bi.free)
                    t_ti[g] = tt(dve, flat(group(TI, g)), bi.ap[:, :], flat(group(TI, g)), ALU.add, ki)
                    bi.free = [t_ti[g]]
                else:
                    ki = kj
                t_tj[g] = tt(dve, flat(group(TJ, g)), bj.ap[:, :], flat(group(TJ, g)), ALU.add, kj, ki)
                bj.free = [t_tj[g]]

        Y = [None, None]
        t_s0 = None
        O = XN
        for t in range(2):
            rd = []
            for j in range(2):
                b = bank()
                r = slice(64 * j, 64 * j + 64)
                for i in range(4):
                    h = 2 * i + j
                    sl = slice(64 * i, 64 * i + 64)
                    k = (mm_last if t == 0 and i == 3 else mm)(
                        b.ap[:, sl], AAK[:, 8 * t + h, :], VT[:, t, 64 * h:64 * h + 64], True, t == 0,
                        t_m[15], t_vt[t], b.free)
                    if t:
                        k = mm_last(b.ap[:, sl], CAR[r, i, t, 0, :], S0[r, i, :], False, True, t_s0)
                rd.append(cp(dve, RHS[:, 256 * j:256 * j + 256], b.ap[:, 0:256], k, t_s0, t_g))
                b.free = [rd[j]]
            b = bank()
            for h in range(8):
                sl = slice(256 * (h % 2) + 64 * (h // 2), 256 * (h % 2) + 64 * (h // 2) + 64)
                k2 = (mm_last if h == 7 else mm)(b.ap[:, sl], TJ[:, 8 * t + h, :], RHS[:, sl], True, True,
                                                 rd[h % 2], t_tj, b.free)
            t_u = cp(dve, RHS, b.ap[:, :], k2)
            b.free = [t_u]
            yt = []
            for j in range(2):
                b = bank()
                r = slice(64 * j, 64 * j + 64)
                for i in range(4):
                    h = 2 * i + j
                    sl = slice(64 * i, 64 * i + 64)
                    mm(b.ap[:, sl], ARK[:, 8 * t + h, :], VT[:, t, 64 * h:64 * h + 64], True, False, b.free)
                    k = (mm_last if t == 0 and i == 3 else mm)(
                        b.ap[:, sl], ARB[:, 8 * t + h, :], RHS[:, 256 * j + 64 * i:256 * j + 64 * i + 64],
                        False, t == 0, t_u)
                    if t:
                        k = mm_last(b.ap[:, sl], CAR[r, i, t, 1, :], S0[r, i, :], False, True)
                dst = O[:, t, 512:1024].rearrange("p (i j n) -> p j i n", i=4, j=2)[:, j]
                yt.append(cp(act, dst, b.ap[:, 0:256].rearrange("p (i n) -> p i n", i=4), k))
                b.free = [yt[j]]
            Y[t] = yt
            if t == 0:
                b = bank()
                for i in range(4):
                    sl = slice(128 * i, 128 * i + 128)
                    mm(b.ap[:, sl], KB[:, 0, sl], VT[:, 0, sl], True, False, t_kb, b.free)
                    k = mm_last(b.ap[:, sl], KB[:, 1, sl],
                                RHS.rearrange("p (j i v) -> p i j v", j=2, i=4)[:, i], False, True)
                for j in range(2):
                    pr = slice(64 * j, 64 * j + 64)
                    t_s0 = tt(dve, S0[pr, :, :],
                              b.ap[pr, :].rearrange("p (i v) -> p i v", i=4)[:, :, 64 * j:64 * j + 64],
                              SML[pr, 0:4].unsqueeze(2).to_broadcast([64, 4, 64]), ALU.mult, k, t_gm, t_g)
                b.free = [t_s0]
        TM = TI.rearrange("p s t -> p (s t)")
        for t in range(2):
            y = O[:, t, 512:1024].rearrange("p (h n) -> p h n", h=8)
            tm = TM[:, t * 512:t * 512 + 512].rearrange("p (h n) -> p h n", h=8)
            tm2 = TM[:, 1024 + t * 512:1536 + t * 512].rearrange("p (h n) -> p h n", h=8)
            st = SML[:, 32 + 16 * t:48 + 16 * t]
            mu, va = st[:, 0:8], st[:, 8:16]
            b8 = lambda v: v.unsqueeze(2).to_broadcast([P, 8, 64])
            k = total(mu, y, Y[t])
            k = ts(dve, mu, mu, 1.0 / 64, None, ALU.mult, None, k)
            k = tt(dve, y, y, b8(mu), ALU.subtract, k)
            k = tt(dve, tm, y, y, ALU.mult, k, t_ti, Y)
            k = total(va, tm, k)
            k = rstd(va, va, eps_gn, 1.0 / 64, k, t_eps)
            k = tt(dve, y, y, b8(va), ALU.mult, k)
            k = tt(pool, y, y, LNG.rearrange("p (h n) -> p h n", h=8), ALU.mult, k, t_ev)
            k = tt(pool, y, y, LNB.rearrange("p (h n) -> p h n", h=8), ALU.add, k)
            k2 = tt(dve, tm2, VT[:, t, :].rearrange("p (h n) -> p h n", h=8), b8(SML[:, 8 + 8 * t:16 + 8 * t]),
                    ALU.mult, t_bon, t_vt, Y)
            k = tt(pool, y, y, tm2, ALU.add, k, k2)
            Y[t] = tt(pool, y, y, G[:, t, :].rearrange("p (h n) -> p h n", h=8), ALU.mult, k, t_g[t])

        LA = SIG
        t_la = []
        z = {}
        TM3 = TJ.rearrange("p s t -> p (s t)")
        for t in range(2):
            b = bank()
            m_ = TM3[:, t * 512:t * 512 + 256]
            e_ = TM3[:, t * 512 + 256:t * 512 + 512]
            mm(b.ap[:, 0:256], GLR[0:16, t * P:t * P + P], GW2[0:16, :], True, False, gl["lr"], t_ev, b.free)
            k = mm_last(b.ap[:, 0:256], ones1, RW0[0:1, 512:768], False, True)
            k1 = fn(e_, b.ap[:, 0:256], ACT.Abs, k, Y)
            k2 = ts(dve, m_, b.ap[:, 0:256], -1.0, 0.0, ALU.mult, ALU.max, k1)
            b.free = [k2]
            k = fn(e_, e_, ACT.Exp, k1, scale=-1.0)
            k = fn(e_, e_, ACT.Ln, k, bias=SM[:, 3:4])
            t_la.append(tt(dve, LA[:, t, 0:256], m_, e_, ALU.add, k, k2, t_gm, t_e[3]))
        AT = AAK.rearrange("p s t -> p (s t)")
        QE = [ARB.rearrange("p s t -> p (s t)")[:, 512 * i:512 * i + 512].rearrange("p (c t) -> p c t", c=2)
              for i in range(4)]
        KE = [ARK.rearrange("p s t -> p (s t)")[:, 512 * i:512 * i + 512].rearrange("p (c t) -> p c t", c=2)
              for i in range(4)]
        EG = [AAB.rearrange("p s t -> p (s t)")[:, 512 * i:512 * i + 512].rearrange("p (c t) -> p c t", c=2)
              for i in range(4)]
        at0 = fill(dve, AT[:, 0:1024], 0.0, Y)
        t_at = at0
        gq, gk = GQK[:, 0:2, :], GQK[:, 2:4, :]
        used = [Y] * 4
        for lv in range(-1, 8):
            i = (lv + 1) % 4
            if lv < 0:
                q_, k_e = gq, gk
                ready = [gl["q"], gl["k"]]
            else:
                b = bank()
                for c in range(2):
                    for t in range(2):
                        m = cst(f"acc{lv}") if lv < 7 else cst(("after", "upto")[t])
                        k = (mm_last if (c, t) == (1, 1) else mm)(
                            b.ap[:, c * 256 + t * P:c * 256 + t * P + P], LA[:, t, c * P:c * P + P], m,
                            True, True, t_la, b.free)
                k = fn(EG[i], b.ap[:, :].rearrange("p (c t) -> p c t", c=2), ACT.Exp, k, used[i], scale=-1.0 / 16)
                b.free = [k]
                q_, k_e = QE[i], KE[i]
                ready = [tt(dve, q_, gq, EG[i], ALU.mult, k, gl["q"], used[i]),
                         tt(pool, k_e, gk, EG[i], ALU.mult, k, gl["k"], used[i])]
            if lv < 7:
                for j in range(2):
                    r = slice(64 * j, 64 * j + 64)
                    b = bank()
                    for c in range(2):
                        for t in range(2):
                            k = (mm_last if (c, t) == (1, 1) else mm)(
                                b.ap[:, (2 * c + t) * P:(2 * c + t) * P + P],
                                k_e[r, c, t * P:t * P + P], q_[r, c, t * P:t * P + P], True, True,
                                ready, b.free)
                    name = "ident" if lv < 0 else f"lvl{lv}"
                    mask = cst(name).bitcast(I32).unsqueeze(1).to_broadcast([P, 4, P])
                    dst = AT[:, 512 * j:512 * j + 512].rearrange("p (s t) -> p s t", s=4)
                    t_at = select(dst, mask, b.ap[:, :].rearrange("p (s t) -> p s t", s=4), k, t_at)
                    b.free = [t_at]
                used[i] = [k]
            else:
                for j in range(2):
                    r = slice(64 * j, 64 * j + 64)
                    b = bank()
                    for c in range(2):
                        k = (mm_last if c else mm)(b.ap[:, c * P:c * P + P], k_e[r, c, 0:P],
                                                   q_[r, c, P:2 * P], True, True, ready, b.free)
                    t_cr = cp(dve, AT[:, 1024 + 256 * j:1280 + 256 * j], b.ap[:, 0:256], k, at0)
                    b.free = [t_cr]
        for t in range(2):
            b = bank()
            for h in range(4):
                sl = slice(h * P, h * P + P)
                blk = 512 * (h % 2) + (2 * (h // 2) + t) * P
                crs = 1024 + 256 * (h % 2) + 128 * (h // 2)
                k = (mm_last if t == 0 and h == 3 else mm)(
                    b.ap[:, sl], AT[:, blk:blk + P], GV[:, t, sl], True, t == 0,
                    t_at, gl["v", 0], gl["v", 1], b.free)
                if t:
                    k = mm_last(b.ap[:, sl], AT[:, crs:crs + P], GV[:, 0, sl], False, True, t_cr)
            o = O[:, t, 0:512].rearrange("p (h n) -> p h n", h=4)
            k = cp(act, O[:, t, 0:512], b.ap[:, :], k)
            b.free = [k]
            tm = TM3[:, t * 512:t * 512 + 512].rearrange("p (h n) -> p h n", h=4)
            ss = SML[:, 64 + 4 * t:68 + 4 * t]
            b4 = ss.unsqueeze(2).to_broadcast([P, 4, P])
            k1 = tt(dve, tm, o, o, ALU.mult, k, t_la)
            k1 = total(ss, tm, k1)
            k1 = rstd(ss, ss, eps_rms, 1.0 / 128, k1)
            gg = GG[:, t, :].rearrange("p (h n) -> p h n", h=4)
            k2 = tt(pool, gg, gg, GNG.unsqueeze(1).to_broadcast([P, 4, P]), ALU.mult, gl["g", t], t_ev)
            k = tt(dve, o, o, b4, ALU.mult, k1)
            Y[t] = [Y[t], tt(dve, o, o, gg, ALU.mult, k, k2)]
        OT = at(dm, 8, 256)
        k = transposed(O, OT, 8, Y)
        rows(a["even_w_out"][0], 8, 0, 1024, OT, residual_norm(0), None, k)
        t_xt = finish_norm(0, pe.now())

        def ffn(layer, i):
            nonlocal t_xt
            HT = at(0, 22, 256)
            UP = at(22 * 256, 2, 512)
            W = a["ffn_w_gate_up"][layer]
            ks = []
            for j in range(0, 22, 2):
                slot, w, there = load(W[:, j * P:j * P + 256].rearrange("(c p) n -> p c n", p=P), 2048, 8)
                slot2, w2, there2 = load(W[:, FFN + j * P:FFN + j * P + 256].rearrange("(c p) n -> p c n", p=P), 2048, 8)
                bg, bu = bank(), bank()
                for (ww, th, bb) in ((w, there, bg), (w2, there2, bu)):
                    for h in range(2):
                        for c in range(8):
                            k = (mm_last if c == 7 else mm)(
                                bb.ap[:, 256 * h:256 * h + 256], ww[:, c, h * P:h * P + P], XT[:, c, :],
                                c == 0, c == 7, th, bb.free, t_xt)
                    if bb is bg:
                        slot.free = [k]
                        kg = k
                slot2.free = [k]
                u = UP[:, (j // 2) % 2, :]
                prev = ks[-2] if len(ks) > 1 else None
                kg = fn(u, bg.ap[:, :], ACT.Silu, kg, prev)
                bg.free = [kg]
                d = tt(dve, HT[:, j:j + 2, :].rearrange("p c t -> p (c t)"), bu.ap[:, :], u, ALU.mult, k, kg)
                bu.free = [d]
                ks.append(d)
            rows(a["ffn_w_down"][layer], 22, 0, 1024, HT, residual_norm(i), None, ks)
            t_xt = finish_norm(i, pe.now())

        ffn(0, 1)

        off[0] = 0
        CQ = take("cq", 2, 1056)
        CT = take("ct", 8, 256)
        QQ = take("qq", 2, 1536)
        KF = take("kf", 2, 1536)
        V2 = take("v2", 2, 1024)
        O2 = take("o2", 2, 1024)
        OT2 = take("ot2", 8, 256)
        PR = take("pr", 4, 2, 256)
        PX = take("px", 2, 512)
        MK = take("mk", 384)
        PS_ = take("pos", 2)
        FR = take("fr", 16)
        CS = take("cs", 2, 2, 16)
        RT = take("rt", 2, 4, 16)
        R2 = take("r2", 2, 2, 256)
        ST2 = take("st2", 256)
        PI_ = sb("PI", [P, 2], I32)
        prev = [state["x"], t_xt, pe.now()]
        s_odd = Dma(sem("s_odd"))
        s_odd.issue(sp, MK, a["mla_mask"], *prev)
        s_odd.issue(sp, FR, a["rope_freq"], *prev)
        t_odd = s_odd.issue(sp, PI_[:, :], a["positions"].rearrange("b (t p) -> p (b t)", p=P),
                            allow_slow_non_contiguous=True)
        k = cp(dve, PS_, PI_[:, :], t_odd)
        parts = [6.28125]
        rest = 2 * np.pi - parts[0]
        for bits in (14, 22):
            p_ = float(np.floor(rest * 2.0 ** bits) / 2.0 ** bits)
            parts.append(p_)
            rest -= p_
        parts.append(float(np.float32(rest)))
        MAGIC = 1.5 * 2.0 ** 23
        t_cs = []
        for t in range(2):
            ang, n_ = RT[:, t, 0, :], RT[:, t, 1, :]
            k1 = ts(dve, ang, FR, PS_[:, t:t + 1], None, ALU.mult, None, k)
            k1 = ts(dve, n_, ang, float(1 / (2 * np.pi)), MAGIC, ALU.mult, ALU.add, k1)
            k1 = ts(dve, n_, n_, MAGIC, None, ALU.subtract, None, k1)
            for p_ in parts:
                k1 = stt(ang, n_, -p_, ang, ALU.mult, ALU.add, k1)
            k1 = ts(dve, ang, ang, 3.1415925, -3.1415925, ALU.min, ALU.max, k1)
            k2 = fn(CS[:, t, 1, :], ang, ACT.Sin, k1)
            k2 = fn(n_, ang, ACT.Sin, k2, scale=0.5)
            k2 = tt(dve, n_, n_, n_, ALU.mult, k2)
            t_cs.append(ts(dve, CS[:, t, 0, :], n_, -2.0, 1.0, ALU.mult, ALU.add, k2))

        od = {}
        SQ = QQ

        def got_p(t, o, m, b, done):
            k = cp(act if o == 512 else dve, CQ[:, t, o:o + m], b.ap[:, 0:m], done)
            b.free = [k]
            od[t, o] = k

        rows(a["mla_w_in"][0], 8, 0, 1056, XT, got_p, None, t_xt)
        kn = []
        for t in range(2):
            k = stats = None
            for j, (lo, n) in enumerate(((0, 768), (768, 256))):
                acc = ST2[:, 2 * t + j:2 * t + j + 1]
                k = ttr(SQ[:, t, lo:lo + n], CQ[:, t, lo:lo + n], CQ[:, t, lo:lo + n], 0.0, ALU.mult, ALU.add, acc, od[t, 0], od[t, 512])
                k = rstd(acc, acc, eps_rms, 1.0 / n, k)
                k = ts(dve, CQ[:, t, lo:lo + n], CQ[:, t, lo:lo + n], acc, None, ALU.mult, None, k)
            kn.append(k)
        k = transposed(CQ, CT, 8, kn, lambda c: vec(0, 95 + c) if c < 6 else vec(0, 101 + c - 6))

        def rope(x, t, n, *after):
            pr = x.rearrange("p h (i two) -> p h i two", two=2)
            x1, x2 = pr[:, :, :, 0], pr[:, :, :, 1]
            cos = CS[:, t, 0, :].unsqueeze(1).to_broadcast([P, n, 16])
            sin = CS[:, t, 1, :].unsqueeze(1).to_broadcast([P, n, 16])
            u = R2[:, 0, 0, 0:n * 16].rearrange("p (h i) -> p h i", h=n)
            v = R2[:, 0, 1, 0:n * 16].rearrange("p (h i) -> p h i", h=n)
            w = R2[:, 1, 0, 0:n * 16].rearrange("p (h i) -> p h i", h=n)
            y = R2[:, 1, 1, 0:n * 16].rearrange("p (h i) -> p h i", h=n)
            k1 = tt(dve, u, x1, cos, ALU.mult, t_cs, dve.now(), *after)
            k2 = tt(dve, v, x2, sin, ALU.mult)
            k3 = tt(dve, w, x1, sin, ALU.mult)
            k4 = tt(dve, y, x2, cos, ALU.mult)
            k5 = tt(dve, x1, u, v, ALU.subtract, k4)
            return tt(dve, x2, w, y, ALU.add, k5)

        def got_q(t, o, m, b, done):
            k = fn(QQ[:, t, o:o + m], b.ap[:, 0:m], ACT.Copy, done, kn, scale=MLA_SCALE)
            b.free = [k]
            od["q", t] = k

        rows(a["mla_w_q_b"][0], 6, 0, 1536, CT, got_q, None, k)

        def got_kv(half):
            def got(t, o, m, b, done):
                h0 = 8 * half + 4 * (o // 512)
                src = b.ap[:, :].rearrange("p (h n) -> p h n", h=4)
                kf = KF[:, t, :].rearrange("p (h n) -> p h n", h=16)[:, h0:h0 + 4, 0:64]
                v2 = V2[:, t, :].rearrange("p (h n) -> p h n", h=16)[:, h0:h0 + 4, :]
                k = cp(act, kf, src[:, :, 0:64], done)
                k = cp(act, v2, src[:, :, 64:128], done)
                b.free = [k]
                od["kv", t] = k
            return got

        for half in range(2):
            rows(a["mla_w_kv_b"][0], 2, 1024 * half, 1024, CT[:, 6:8, :], got_kv(half), None, k)
        t_q = []
        t_k = []
        for t in range(2):
            q16 = QQ[:, t, :].rearrange("p (h n) -> p h n", h=16)
            t_q.append(rope(q16[:, :, 64:96], t, 16, od["q", t]))
            kpe = CQ[:, t, 1024:1056].unsqueeze(1)
            kr = rope(kpe, t, 1, od[t, 1024])
            kf = KF[:, t, :].rearrange("p (h n) -> p h n", h=16)[:, :, 64:96]
            kr = cp(dve, kf, CQ[:, t, 1024:1056].unsqueeze(1).to_broadcast([P, 16, 32]), kr)
            t_k.append([kr, od["kv", t]])

        def attend(heads, q_of, k_of, mask_of, v_of, out, sink=None, ready=None):
            MX = ST2[:, 16:48]
            SU = ST2[:, 48:80]
            NM = ST2[:, 80:112]
            RS = ST2[:, 112:144]
            last_pv = {}
            result = []
            turn["banks"] = 6
            for t in range(2):
                nk = P * (t + 1)
                mx = {}
                for h in range(heads):
                    w = (t * heads + h) % 4
                    col = t * 16 + h
                    q, kq = q_of(h, t)
                    kk, kkk = k_of(h, nk)
                    b = bank()
                    k = mm_last(b.ap[:, 0:nk], q, kk, True, True, kq, kkk, b.free)
                    pr = PR[:, w, 0, 0:nk]
                    k = ttr(pr, b.ap[:, 0:nk], mask_of(h, t), NEG, ALU.add, ALU.max,
                            MX[:, col:col + 1], k, last_pv.get(w), ready)
                    b.free = [k]
                    if sink is not None:
                        k = tt(dve, MX[:, col:col + 1], MX[:, col:col + 1], sink[:, h:h + 1], ALU.max, k)
                    k = ts(dve, NM[:, col:col + 1], MX[:, col:col + 1], -1.0, None, ALU.mult, None, k)
                    ex = PR[:, w, 1, 0:nk]
                    k = fn(ex, pr, ACT.Exp, k, bias=NM[:, col:col + 1], accum_out=SU[:, col:col + 1])
                    if sink is not None:
                        k = fn(RS[:, col:col + 1], sink[:, h:h + 1], ACT.Exp, k, bias=NM[:, col:col + 1])
                    mx[h] = k
                    b = bank()
                    for j in range(t + 1):
                        kt = (tr_last if j == t else tr)(b.ap[:, j * P:j * P + P], ex[:, j * P:j * P + P], k, b.free)
                    px = PX[:, h % 2, 0:nk]
                    kc = cp(act if h % 2 else dve, px, b.ap[:, 0:nk], kt, last_pv.get(("px", h % 2)))
                    b.free = [kc]
                    bo = psum[6 + h // 8]
                    hs = slice(64 * (h % 8), 64 * (h % 8) + 64)
                    for j in range(t + 1):
                        v, kv = v_of(h, j)
                        kp = (mm_last if j == t else mm)(bo.ap[:, hs], px[:, j * P:j * P + P], v,
                                                         j == 0, j == t, kc, kv, bo.free)
                    last_pv[w] = kt
                    last_pv["px", h % 2] = kp
                    if h % 8 == 7:
                        c0 = t * 16 + h - 7
                        k = mx[h]
                        if sink is not None:
                            k = tt(dve, SU[:, c0:c0 + 8], SU[:, c0:c0 + 8], RS[:, c0:c0 + 8], ALU.add, k)
                        k = recip(RS[:, c0:c0 + 8], SU[:, c0:c0 + 8], k)
                        o = out(h - 7, t)
                        k = tt(dve, o.rearrange("p (h n) -> p h n", h=8),
                               bo.ap[:, :].rearrange("p (h n) -> p h n", h=8),
                               RS[:, c0:c0 + 8].unsqueeze(2).to_broadcast([P, 8, 64]), ALU.mult, k, kp)
                        bo.free = [k]
                        result.append(k)
            turn["banks"] = 8
            return result

        QT = at(0, 16, 256)
        KTA = take("kta", 16, 256)
        t_hd = {}
        for h in range(16):
            for key, src, toks in (("q", QQ, t_q), ("k", KF, t_k)):
                dst = QT if key == "q" else KTA
                b = bank()
                for t in range(2):
                    k = (tr_last if t else tr)(b.ap[0:96, t * P:t * P + P], src[:, t, 96 * h:96 * h + 96],
                                               toks[t], b.free)
                k = cp(act if key == "q" else dve, dst[0:96, h, :], b.ap[0:96, 0:256], k, t_q, t_k, pe.now())
                b.free = [k]
                t_hd[key, h] = k
        res = attend(16,
                     lambda h, t: (QT[0:96, h, t * P:t * P + P], t_hd["q", h]),
                     lambda h, nk: (KTA[0:96, h, 0:nk], t_hd["k", h]),
                     lambda h, t: MK[:, 128 * t:128 * t + 128 + 128 * t],
                     lambda h, j: (V2[:, j, 64 * h:64 * h + 64], od["kv", j]),
                     lambda h, t: O2[:, t, 64 * h:64 * h + 512], None, t_odd)
        k = transposed(O2, OT2, 8, [res, res])
        rows(a["mla_w_out"][0], 8, 0, 1024, OT2, residual_norm(2), None, k)
        t_xt = finish_norm(2, pe.now())
        ffn(1, 3)

        off[0] = 8192
        MOD = take("mod", 48)
        ACCA = take("acca", 2, 1024)
        CSL = take("csl", 8)
        G12 = take("g12", 2, 1024)
        GN = take("gn", 2, 1024)
        RB = take("rb", 16)
        HOT = take("hot", 384)
        MKV = take("mkv", 384)
        BV = take("bv", 384)
        SNK = take("snk", 8)
        base2 = off[0]
        prev = [state["x"], t_xt, pe.now(), dve.now(), act.now(), pool.now()]
        s_n = Dma(sem("s_n"))
        s_n.issue(sp, RB[0:32, :], a["rel_bias_2"], *prev)
        s_n.issue(sp, HOT[0:32, :], a["bucket_hot"])
        s_n.issue(sp, MKV[0:16, :], a["bucket_mask"])
        s_n.issue(sp, SNK, a["sinks_2"].to_broadcast([P, 8]))
        s_n.issue(sp, GN[:, 0, :], a["norm_gains_2"][0, 1:2, :].to_broadcast([P, D]))
        s_n.issue(sp, GN[:, 1, :], a["norm_gains_2"][0, 3:4, :].to_broadcast([P, D]))
        t_n = (s_n.sem, s_n.n)
        b = bank()
        k = mm_last(b.ap[0:16, 0:384], RB[0:32, :], HOT[0:32, :], True, True, t_n, b.free)
        k = tt(dve, BV[0:16, :], b.ap[0:16, 0:384], MKV[0:16, :], ALU.add, k)
        b.free = [k]
        s_bv = Dma(sem("s_bv"))
        sc = nc.dram_tensor("scratch", [16, P, 384], F32, kind="Internal").ap()
        k = s_bv.issue(sp, sc, BV[0:16, :].unsqueeze(1).to_broadcast([16, P, 384]), k)
        BIAS = take("bias", 16, 256)
        t_bias = s_bv.issue(sp, BIAS, bass.AP(sc.tensor, sc.offset + 127, [[383, 128], [384 * P, 16], [1, 256]]), k)
        k_c = fn(CSL, VEC[:, 1, 112:120], ACT.Silu, *prev)
        WA = a["w_ada_2"][0]
        t_mod = None
        t_acc = [prev, prev]
        for j in range(6):
            acc = ACCA[:, j % 2, :]
            k = None
            for k0 in range(0, 8, 2):
                slot, w, there = load(WA[k0 * P:k0 * P + 256, 1024 * j:1024 * j + 1024]
                                      .rearrange("(c p) n -> p c n", p=P), 2048, 2)
                for c in range(2):
                    if k0 + c == 0:
                        k = ts(dve, acc, w[:, c, :], CSL[:, 0:1], None, ALU.mult, None, there, k_c, t_acc[j % 2])
                    else:
                        k = stt(acc, w[:, c, :], CSL[:, k0 + c:k0 + c + 1], acc, ALU.mult, ALU.add, there, k)
                slot.free = [k]
            if j in (2, 5):
                g = G12[:, j // 3, :]
                kb = Dma(sem(f"s_ada{j}")).issue(sp, g, a["b_ada_2"][:, 1024 * j:1024 * j + 1024].to_broadcast([P, D]), *prev)
                for o in range(0, 1024, 512):
                    b = bank()
                    k2 = mm_last(b.ap[:, :], cst("ones"), acc[:, o:o + 512], True, True, k, b.free)
                    k3 = tt(dve, g[:, o:o + 512], b.ap[:, :], g[:, o:o + 512], ALU.add, k2, kb)
                    k3 = tt(dve, g[:, o:o + 512], g[:, o:o + 512], GN[:, j // 3, o:o + 512], ALU.mult, k3)
                    b.free = [k3]
                t_g12 = k3
                t_acc[j % 2] = [k2]
            else:
                b = bank()
                for i in range(8):
                    k2 = (mm_last if i == 7 else mm)(b.ap[:, i:i + 1], acc[:, i * P:i * P + P], SM[:, 3:4],
                                                     True, True, k, b.free)
                t_mod = tt(dve, MOD[:, 8 * j:8 * j + 8], b.ap[:, 0:8], VEC[:, 1, 32 + 8 * j:40 + 8 * j],
                           ALU.add, k2, t_v)
                b.free = [t_mod]
                t_acc[j % 2] = [k2]
        k = stt(MOD[:, 8:16], MOD[:, 8:16], 1.0, VEC[:, 1, 80:88], ALU.add, ALU.mult, t_mod)
        t_mod = stt(MOD[:, 32:40], MOD[:, 32:40], 1.0, VEC[:, 1, 96:104], ALU.add, ALU.mult, k)

        def modulated(i, xt_free):
            ready = []
            for t in range(2):
                acc = STAT[:, t, 0:1]
                k = ttr(XN[:, t, :], X[:, t, :], X[:, t, :], 0.0, ALU.mult, ALU.add, acc, state["x"], xt_free)
                k = rstd(acc, acc, eps_rms, 1.0 / D, k)
                ready.append(ts(dve, XN[:, t, :], X[:, t, :], acc, None, ALU.mult, None, k))
            return transposed(XN, XT, 8, ready, lambda c: MOD[:, 24 * i + 8 + c:24 * i + 9 + c],
                              lambda c: MOD[:, 24 * i + c:24 * i + c + 1], [t_mod, xt_free])

        def gated_residual(i):
            def got(t, o, m, b, done):
                k = cp(act, XN[:, t, o:o + m], b.ap[:, 0:m], done)
                b.free = [k]
                state["h", t, o] = k
            return got

        def finish_gated(i):
            out = []
            for t in range(2):
                acc = STAT[:, t, 0:1]
                SQ2 = at(base2 + 4096, 2, 1024)
                k = ttr(SQ2[:, t, :], XN[:, t, :], XN[:, t, :], 0.0, ALU.mult, ALU.add, acc,
                           state["h", t, 0], state["h", t, 512])
                k = rstd(acc, acc, eps_rms, 1.0 / D, k)
                k = stt(XN[:, t, :], XN[:, t, :], acc, G12[:, i, :], ALU.mult, ALU.mult, k, t_g12)
                out.append(tt(dve, X[:, t, :], X[:, t, :], XN[:, t, :], ALU.add, k))
            state["x"] = out
            return out

        t_xt = modulated(0, [t_xt, pe.now()])
        off[0] = base2 + 4096 + 2048
        QA = at(0, 12, 256)
        KBT = at(3072, 3, 256)
        VA = at(3840, 2, 640)
        O3 = at(5120, 2, 1024)
        OT3 = take("ot3", 8, 256)
        PR = take("pr3", 4, 2, 256)
        PX = take("px3", 2, 512)
        ST2 = take("st3", 256)
        W2 = a["w_in_2"][0]
        qk = {}

        def got_q2(i, b, n, done):
            src = b.ap[:, 0:256 * n].rearrange("p (c t) -> p c t", c=n)
            if i < 4 or i >= 8:
                if i == 12:
                    k = cp(act, KBT[:, 0, :], b.ap[:, 0:256], done)
                else:
                    k = fn(QA[:, i:i + n, :], src, ACT.Copy, done, scale=0.125)
            else:
                k = cp(act, QA[:, i:i + n, :], src, done)
            b.free = [k]
            for j in range(n):
                qk[i + j] = k

        cols2 = [(128 * i, 128) for i in range(8)] + [(1536 + 128 * i, 128) for i in range(4)]
        columns(W2, 8, cols2, XT, got_q2, t_xt)
        columns(W2, 8, [(2048, 128)], XT, lambda i, b, n, done: got_q2(12, b, n, done), t_xt)
        b = bank()
        k = mm_last(b.ap[:, 0:256], cst("swap"), KBT[:, 0, :], True, True, qk[12], b.free)
        t_sw = cp(act, KBT[:, 1, :], b.ap[:, 0:256], k)
        b.free = [t_sw]
        vv = {}

        def got_va(c0):
            def got(t, o, m, b, done):
                k = cp(act, VA[:, t, c0:c0 + m], b.ap[:, 0:m], done)
                b.free = [k]
                vv[t] = k
            return got

        rows(W2, 8, 1024, 512, XT, got_va(0), None, t_xt)
        rows(W2, 8, 2176, 128, XT, got_va(512), None, t_xt)

        def q2(h, t):
            r = slice(64 * (h % 2), 64 * (h % 2) + 64)
            i = h // 2 if h < 8 else 8 + (h - 8) // 2
            return QA[r, i, t * P:t * P + P], qk[i]

        def k2_(h, nk):
            r = slice(64 * (h % 2), 64 * (h % 2) + 64)
            if h < 8:
                return QA[r, 4 + h // 2, 0:nk], qk[4 + h // 2]
            g = (h - 8) // 4
            return KBT[r, 0 if g == h % 2 else 1, 0:nk], [qk[12], t_sw]

        def v2_(h, j):
            if h < 8:
                return VA[:, j, 64 * h:64 * h + 64], vv[j]
            g = (h - 8) // 4
            return VA[:, j, 512 + 64 * g:576 + 64 * g], vv[j]

        SK = take("sk", 16)
        k = fill(pool, SK[:, 0:8], NEG, prev)
        t_sk = cp(pool, SK[:, 8:16], SNK, t_n, k)
        res = attend(16, q2, k2_, lambda h, t: BIAS[:, h, 128 * (1 - t):256], v2_,
                     lambda h, t: O3[:, t, 64 * h:64 * h + 512], SK, [t_bias, t_sk])
        k = transposed(O3, OT3, 8, [res, res])
        rows(a["w_out_2"][0], 8, 0, 1024, OT3, gated_residual(0), None, k)
        finish_gated(0)
        t_xt = modulated(1, pe.now())
        HT = at(0, 32, 256)
        hs = []
        BT2 = take("b2row", 1024)
        t_b2 = Dma(sem("s_b2")).issue(sp, BT2[0:1, :], a["b2_2"], *prev)

        def got_h(i, b, n, done):
            for j in range(n):
                k = fn(HT[:, i + j, :], b.ap[:, 256 * j:256 * j + 256], ACT.Relu, done, bias=VEC[:, 1, i + j:i + j + 1])
            b.free = [k]
            v = HT[:, i:i + n, :]
            hs.append(tt(dve if (i // 2) % 2 else pool, v, v, v, ALU.mult, k))

        columns(a["w1_2"][0], 8, [(128 * i, 128) for i in range(32)], XT, got_h, t_xt)
        rows(a["w2_2"][0], 32, 0, 1024, HT, gated_residual(1), BT2, hs, t_b2)
        res = finish_gated(1)
        s_out = Dma(sem("s_out"))
        od_ = a["out"].rearrange("b (t p) d -> p (b t) d", p=P)
        for t in range(2):
            k = s_out.issue(sp, od_[:, t, :], X[:, t, :], res[t])
        sp.wait(k)

        block = ctx.enter_context(nc.Block())
        block.sync(sp.emit)
        block.scalar(act.emit)
        block.vector(dve.emit)
        block.gpsimd(pool.emit)
        block.tensor(pe.emit)


_INS = ["x", "positions", "even_w_in", "gla_gate_w2", "gla_gate_b", "gla_norm_g", "rwkv_mu", "rwkv_w0", "rwkv_w2",
        "rwkv_a0", "rwkv_a2", "rwkv_g2", "rwkv_k_k", "rwkv_k_a", "rwkv_r_k", "rwkv_ln_g", "rwkv_ln_b", "even_w_out",
        "mla_w_in", "mla_q_norm_g", "mla_w_q_b", "mla_kv_norm_g", "mla_w_kv_b", "mla_w_out", "ffn_w_gate_up",
        "ffn_w_down", "ln_g", "ln_b", "c_2", "w_in_2", "w_out_2", "sinks_2", "rel_bias_2", "w_ada_2", "b_ada_2",
        "norm_gains_2", "w1_2", "b1_2", "w2_2", "b2_2"]


def kernel(**inputs):
    import numpy as _np
    import concourse.bacc as _bacc
    from concourse import mybir as _mybir
    from concourse.bass_utils import run_bass_kernel_spmd as _run

    nc = _bacc.Bacc("TRN2", target_bir_lowering=False, num_devices=1)
    hot, mask = bucket_rows()
    given = {name: _np.ascontiguousarray(inputs[name]) for name in _INS}
    given.update(consts=constants(), bucket_hot=hot, bucket_mask=mask, mla_mask=mla_mask(), rope_freq=rope_rows())
    arrays, aps = {}, {}
    for name, x in given.items():
        arrays[f"in_{name}_dram"] = x
        aps[name] = nc.dram_tensor(f"in_{name}_dram", x.shape, _mybir.dt.from_np(x.dtype), kind="ExternalInput").ap()
    aps["out"] = nc.dram_tensor("out_0_dram", (1, S, D), _mybir.dt.float32, kind="ExternalOutput").ap()
    program(nc, aps)
    r = _run(nc, [arrays], core_ids=[0])
    return r.results[0]["out_0_dram"]
```

```python
from contextlib import ExitStack

import numpy as np

import concourse.bass as bass
from concourse import mybir

P = 128
S = 256
D = 1024
F32 = mybir.dt.float32
I32 = mybir.dt.int32
ALU = mybir.AluOpType
ACT = mybir.ActivationFunctionType
AX = mybir.AxisListType.X

ALPHA = 4.0 ** 0.25
LN_EPS = 1e-5
RMS_EPS = 1e-6
GN_EPS = 64e-5
FFN = 2816
DFF = 4096
DECAY = float(np.exp(-0.5))
MLA_SCALE = 96.0 ** -0.5
NEG = -1e30

NAMES = (["ident", "cinc", "cexc", "strict", "incl", "heads"]
         + [f"lvl{i}" for i in range(7)] + [f"acc{i}" for i in range(7)] + ["after", "upto", "ones", "swap"])
COLS = {n: 128 * i for i, n in enumerate(NAMES)}
WIDE = 128 * len(NAMES)


def constants():
    s = np.arange(128)[:, None]
    t = np.arange(128)[None, :]
    out = {"ident": s == t, "strict": s < t, "incl": s <= t, "heads": s // 64 == t // 64,
           "cinc": (s <= t) * 1.0 - (s < 64), "cexc": (s < t) * 1.0 - (s < 64),
           "after": s > t, "upto": s <= t, "ones": (s >= 0) & (t >= 0), "swap": s == (t + 64) % 128}
    for i in range(7):
        m = 1 << i
        same = s // (2 * m) == t // (2 * m)
        right = (t // m) % 2 == 1
        out[f"lvl{i}"] = same & right & ((s // m) % 2 == 0)
        edge = t // (2 * m) * (2 * m) + m
        out[f"acc{i}"] = np.where(right, (s >= edge) & (s <= t), (s > t) & (s < edge))
    return np.concatenate([out[n].astype(np.float32) for n in NAMES], 1)


def bucket_rows():
    n = np.clip(255 - np.arange(384), 0, None)
    nf = np.maximum(n, 1).astype(np.float32)
    large = 16 + (np.log(nf / np.float32(16)) / np.float32(np.log(8.0)) * np.float32(16)).astype(np.int32)
    b = np.where(n < 16, n, np.minimum(large, 31))
    dist = 255 - np.arange(384)
    hot = (np.arange(32)[:, None] == b[None]).astype(np.float32)
    moba = np.where(dist >= 0, 0.0, NEG)
    swa = np.where((dist >= 0) & (dist < 128), 0.0, NEG)
    mask = np.concatenate([np.tile(moba, (8, 1)), np.tile(swa, (8, 1))]).astype(np.float32)
    return hot, mask


def mla_mask():
    q = np.arange(128)[:, None]
    k = np.arange(256)[None]
    near = np.where(k[:, :128] // 64 <= q // 64, 0.0, NEG)
    far = np.where(k // 64 <= (q + 128) // 64, 0.0, NEG)
    return np.concatenate([near, far], 1).astype(np.float32)


def rope_rows():
    f = (np.float32(10000.0) ** (-np.arange(0, 32, 2, dtype=np.float32) / np.float32(32))).astype(np.float32)
    return np.tile(f[None], (128, 1))


class Queue:

    def __init__(self, sem):
        self.sem, self.n, self.todo, self.met = sem, 0, [], {}

    def wait(self, *after):
        for tok in after:
            if tok is None:
                continue
            if isinstance(tok, list):
                self.wait(*tok)
                continue
            sem, value = tok
            if self.met.get(sem.name, 0) < value:
                self.met[sem.name] = value
                self.todo.append(lambda e, sem=sem, value=value: e.wait_ge(sem, value))

    def do(self, fn, *after):
        self.wait(*after)
        self.n += 1
        self.todo.append(lambda e: fn(e).then_inc(self.sem, 1))
        return (self.sem, self.n)

    def start(self, fn, *after):
        self.wait(*after)
        self.todo.append(fn)

    def now(self):
        return (self.sem, self.n)

    def emit(self, e):
        for fn in self.todo:
            fn(e)


class Dma:

    def __init__(self, sem):
        self.sem, self.n = sem, 0

    def issue(self, queue, out, in_, *after, **kw):
        self.n += 16
        queue.start(lambda e: e.dma_start(out, in_, **kw).then_inc(self.sem, 16), *after)
        return (self.sem, self.n)


class Buf:

    def __init__(self, ap, dma=None):
        self.ap, self.dma, self.free = ap, dma, []


def program(nc, a):
    ctx = ExitStack()
    with ctx:
        def sb(name, shape, dt=F32):
            return ctx.enter_context(nc.sbuf_tensor(name, shape, dt))[(slice(None),) * len(shape)]

        def sem(name):
            return ctx.enter_context(nc.semaphore(name))

        pe, dve, act, pool, sp = (Queue(sem(n)) for n in ("s_pe", "s_dve", "s_act", "s_pool", "s_sp"))

        NSLOT = 5
        ring = [Buf(sb(f"ring{i}", [P, 2048]), Dma(sem(f"s_ring{i}"))) for i in range(NSLOT)]
        psum = [Buf(ctx.enter_context(nc.psum_tensor(f"ps{i}", [P, 512], F32))) for i in range(8)]
        turn = {"ring": 0, "psum": 0, "banks": 8}

        X = sb("X", [P, 2, D])
        XN = sb("XN", [P, 2, D])
        XT = sb("XT", [P, 8, S])
        CST = sb("CST", [P, WIDE])
        VEC = sb("VEC", [P, 2, P])
        GB = sb("GB", [P, 2, D])
        SM = sb("SM", [P, 64])
        ROW = sb("ROW", [1, 128])
        ARENA = 30400
        AR = sb("AR", [P, ARENA])

        def cst(name):
            return CST[:, COLS[name]:COLS[name] + 128]

        ident = cst("ident")

        def at(off, *shape):
            n = int(np.prod(shape))
            assert off + n <= ARENA, (off, n)
            v = AR[:, off:off + n]
            if len(shape) == 1:
                return v
            names = "abcd"[:len(shape)]
            kw = {c: k for c, k in zip(names[1:], shape[1:])}
            return v.rearrange(f"p ({' '.join(names)}) -> p {' '.join(names)}", **kw)

        s_const = Dma(sem("s_const"))
        s_gain = Dma(sem("s_gain"))

        def bank():
            b = psum[turn["psum"] % turn["banks"]]
            turn["psum"] += 1
            return b

        def load(src, n, dims=None):
            slot = ring[turn["ring"] % NSLOT]
            turn["ring"] += 1
            dst = slot.ap[:, 0:n]
            if dims:
                dst = dst.rearrange("p (c n) -> p c n", c=dims)
            return slot, dst, slot.dma.issue(sp, dst, src, slot.free)

        def mm(out, lhsT, rhs, first, last, *after):
            pe.start(lambda e: e.matmul(out, lhsT, rhs, start=first, stop=last), *after)

        def mm_last(out, lhsT, rhs, first, last, *after):
            return pe.do(lambda e: e.matmul(out, lhsT, rhs, start=first, stop=last), *after)

        def tr(out, in_, *after, np_=128):
            pe.start(lambda e: e.transpose(out, in_, ident[0:np_, 0:np_]), *after)

        def tr_last(out, in_, *after, np_=128):
            return pe.do(lambda e: e.transpose(out, in_, ident[0:np_, 0:np_]), *after)

        def tt(q, out, x, y, op, *after):
            return q.do(lambda e: e.tensor_tensor(out, x, y, op), *after)

        def ts(q, out, x, s1, s2, op0, op1, *after):
            if s2 is None:
                return q.do(lambda e: e.tensor_scalar(out, x, s1, None, op0), *after)
            return q.do(lambda e: e.tensor_scalar(out, x, s1, s2, op0, op1), *after)

        def stt(out, x, s, y, op0, op1, *after):
            return dve.do(lambda e: e.scalar_tensor_tensor(out, x, s, y, op0, op1), *after)

        def fn(out, x, f, *after, **kw):
            return act.do(lambda e: e.activation(out, x, f, **kw), *after)

        def recip(out, x, *after):
            return dve.do(lambda e: e.reciprocal(out, x), *after)

        def total(out, x, *after):
            return dve.do(lambda e: e.tensor_reduce(out, x, AX, ALU.add), *after)

        def ttr(out, x, y, start, op0, op1, acc, *after):
            return dve.do(lambda e: e.tensor_tensor_reduce(out, x, y, 1.0, start, op0, op1, acc), *after)

        def fill(q, out, value, *after):
            return q.do(lambda e: e.memset(out, value), *after)

        def select(out, mask, x, *after):
            return dve.do(lambda e: e.copy_predicated(out, mask, x), *after)

        def moments(out, x, *after):
            return dve.do(lambda e: e.bn_stats(out, x), *after)

        def gather_moments(out, x, *after):
            return dve.do(lambda e: e.bn_aggr(out, x), *after)

        def cp(q, out, x, *after):
            if q is act:
                return fn(out, x, ACT.Copy, *after)
            return q.do(lambda e: e.tensor_copy(out, x), *after)


        def columns(W, kc, cols, xT, got, *after, width=256):
            i = 0
            while i < len(cols):
                b = bank()
                pair = cols[i:i + 2]
                c0, c1 = pair[0][0], pair[-1][0] + pair[-1][1]
                n = c1 - c0
                slot, w, there = load(W[:, c0:c1].rearrange("(c p) n -> p c n", p=P), kc * n, kc)
                for h, (start, count) in enumerate(pair):
                    for c in range(kc):
                        last = c == kc - 1
                        f = mm_last if last else mm
                        done = f(b.ap[0:count, h * 256:h * 256 + 256],
                                 w[:, c, start - c0:start - c0 + count], xT[:, c, :],
                                 c == 0, last, there, b.free, *after)
                slot.free = [done]
                got(i, b, len(pair), done)
                i += 2

        def rows(W, kc, c0, n, xT, got, bias=None, *after):
            parts = [(o, min(512, n - o)) for o in range(0, n, 512)]
            bs = [[bank() for _ in parts] for _ in range(2)]
            per = max(1, 2048 // n)
            for k0 in range(0, kc, per):
                k1 = min(kc, k0 + per)
                src = W[k0 * P:k1 * P, c0:c0 + n].rearrange("(c p) n -> p c n", p=P)
                slot, w, there = load(src, (k1 - k0) * n, k1 - k0)
                for t in range(2):
                    for j, (o, m) in enumerate(parts):
                        for c in range(k0, k1):
                            last = c == kc - 1 and bias is None
                            f = mm_last if c == k1 - 1 else mm
                            done = f(bs[t][j].ap[:, 0:m], xT[:, c, t * P:t * P + P],
                                     w[:, c - k0, o:o + m], c == 0, last,
                                     there, bs[t][j].free if c == 0 else None, *after)
                        if k1 == kc:
                            if bias is not None:
                                done = mm_last(bs[t][j].ap[:, 0:m], ones1, bias[0:1, o:o + m], False, True)
                            got(t, o, m, bs[t][j], done)
                slot.free = [pe.now()]

        eps_ln, eps_rms, eps_gn = SM[:, 0:1], SM[:, 1:2], SM[:, 2:3]
        ones1 = ROW[0:1, 0:128]
        STAT = sb("STAT", [P, 2, 16])

        def rstd(out, var, eps, scale, *after):
            k = fn(out, var, ACT.Sqrt, *after, bias=eps, scale=scale)
            return recip(out, out, k)

        def transposed(src, dst, c_n, ready, scale=None, shift=None, free=None):
            done = []
            for c in range(0, c_n, 2):
                b = bank()
                m = min(2, c_n - c)
                for i in range(m):
                    for t in range(2):
                        f = tr_last if (i, t) == (m - 1, 1) else tr
                        k = f(b.ap[:, i * 256 + t * P:i * 256 + t * P + P],
                              src[:, t, (c + i) * P:(c + i + 1) * P], ready[t], b.free)
                use = act if (c // 2) % 2 else dve
                if scale is None:
                    d = cp(use, dst[:, c:c + m, :], b.ap[:, 0:m * 256].rearrange("p (c t) -> p c t", c=m), k, free)
                else:
                    for i in range(m):
                        sc = scale(c + i)
                        sh = shift(c + i) if shift else None
                        x = b.ap[:, i * 256:i * 256 + 256]
                        if use is act:
                            if sh is None:
                                d = fn(dst[:, c + i, :], x, ACT.Copy, k, free, scale=sc)
                            else:
                                d = fn(dst[:, c + i, :], x, ACT.Identity, k, free, bias=sh, scale=sc)
                        elif sh is None:
                            d = ts(dve, dst[:, c + i, :], x, sc, None, ALU.mult, None, k, free)
                        else:
                            d = ts(dve, dst[:, c + i, :], x, sc, sh, ALU.mult, ALU.add, k, free)
                b.free = [d]
                done.append(d)
            return done

        def gain_rows(i, *after):
            g = a["ln_g"].rearrange("a b d -> (a b) d")[i:i + 1, :]
            b = a["ln_b"].rearrange("a b d -> (a b) d")[i:i + 1, :]
            s_gain.issue(pool, GB[:, 0, :], g.to_broadcast([P, D]), *after)
            return s_gain.issue(pool, GB[:, 1, :], b.to_broadcast([P, D]), *after)

        state = {"x": None, "gb": None}

        def residual_norm(i):
            def got(t, o, m, b, done):
                k = stt(XN[:, t, o:o + m], X[:, t, o:o + m], ALPHA, b.ap[:, 0:m], ALU.mult, ALU.add,
                        done, state["x"])
                b.free = [k]
                k = moments(STAT[:, t, 6 * (o // 512):6 * (o // 512) + 6], XN[:, t, o:o + m], k)
                state[("st", t, o)] = k
            return got

        def finish_norm(i, xt_free):
            rs, ready = [], []
            for t in range(2):
                k = gather_moments(STAT[:, t, 12:14], STAT[:, t, 0:12], state[("st", t, 0)], state[("st", t, 512)])
                rs.append(fn(STAT[:, t, 14:15], STAT[:, t, 13:14], ACT.Sqrt, k, bias=eps_ln))
            for t in range(2):
                k = recip(STAT[:, t, 14:15], STAT[:, t, 14:15], rs[t])
                ready.append(ts(dve, XN[:, t, :], XN[:, t, :], STAT[:, t, 12:13], STAT[:, t, 14:15],
                                ALU.subtract, ALU.mult, k))
            ev = transposed(XN, XT, 8, ready, lambda c: VEC[:, 0, 31 + 8 * i + c:32 + 8 * i + c],
                            lambda c: VEC[:, 0, 63 + 8 * i + c:64 + 8 * i + c], xt_free)
            out = []
            for t in range(2):
                k = tt(pool, X[:, t, :], XN[:, t, :], GB[:, 0, :], ALU.mult, ready[t], state["gb"])
                out.append(tt(pool, X[:, t, :], X[:, t, :], GB[:, 1, :], ALU.add, k))
            state["x"] = out
            state["xn"] = ready
            if i < 3:
                state["gb"] = gain_rows(i + 1, out)
            return ev

        t_x = s_const.issue(act, X[:, :, :], a["x"].rearrange("b (t p) d -> p (b t) d", p=P))
        s_c2 = Dma(sem("s_c2"))
        t_id = s_c2.issue(act, CST[:, 0:P], a["consts"][:, 0:P])
        VR = at(0, 2, 128)
        k = fill(pool, VR, 0.0)
        fill(pool, eps_ln, LN_EPS)
        fill(pool, eps_rms, RMS_EPS)
        fill(pool, eps_gn, GN_EPS)
        fill(pool, SM[:, 3:4], 1.0)
        k_sm = fill(pool, SM[:, 4:6], 0.0)
        k_sm = fill(pool, SM[64:128, 4:5], 1.0, k_sm)
        k_sm = fill(pool, SM[0:64, 5:6], 1.0, k_sm)
        t_eps = fill(pool, ones1, 1.0, k_sm)
        s_vec = Dma(sem("s_vec"))

        def vrow(half, r, src, n):
            full = n // P
            flat = src
            if full:
                s_vec.issue(act, VR[r:r + full, half, :], flat[:, 0:full * P].rearrange("a (r p) -> (a r) p", p=P), k)
            if n % P:
                s_vec.issue(act, VR[r + full:r + full + 1, half, 0:n % P], flat[:, full * P:n], k)

        for r, name, n in ((0, "rwkv_mu", 1824), (15, "rwkv_k_k", 512), (19, "rwkv_k_a", 512),
                           (23, "rwkv_a0", 512)):
            vrow(0, r, a[name], n)
        vrow(0, 27, a["rwkv_r_k"].rearrange("a h n -> a (h n)"), 512)
        s_vec.issue(act, VR[31:63, 0, :], a["ln_g"].rearrange("a b (r p) -> (a b r) p", p=P), k)
        s_vec.issue(act, VR[63:95, 0, :], a["ln_b"].rearrange("a b (r p) -> (a b r) p", p=P), k)
        vrow(0, 95, a["mla_q_norm_g"], 768)
        vrow(0, 101, a["mla_kv_norm_g"], 256)
        vrow(1, 0, a["b1_2"], 4096)
        vrow(1, 32, a["b_ada_2"], 6144)
        s_vec.issue(act, VR[80:112, 1, :], a["norm_gains_2"].rearrange("a b (r p) -> (a b r) p", p=P), k)
        vrow(1, 112, a["c_2"], 1024)
        t_vec = (s_vec.sem, s_vec.n)
        t_cst = Dma(sem("s_cst")).issue(act, CST[:, P:], a["consts"][:, P:])
        O_ = {}
        off = [256]

        def take(name, *shape):
            n = int(np.prod(shape))
            O_[name] = at(off[0], *shape)
            off[0] += n
            return O_[name]

        GW2 = take("gw2", 256)
        W2A2 = take("w2a2", 512)
        G2 = take("g2", 2, 512)
        LNG = take("lng", 512)
        LNB = take("lnb", 512)
        GNG = take("gng", 128)
        RW0 = sb("RW0", [1, 768])
        s_ev = Dma(sem("s_ev"))
        s_ev.issue(act, GW2[0:16, :], a["gla_gate_w2"][0])
        s_ev.issue(act, W2A2[0:64, :], a["rwkv_w2"][0])
        s_ev.issue(act, W2A2[64:128, :], a["rwkv_a2"][0])
        s_ev.issue(act, G2[:, 0, :], a["rwkv_g2"][0, 0:128, :])
        s_ev.issue(act, G2[0:32, 1, :], a["rwkv_g2"][0, 128:160, :])
        s_ev.issue(act, LNG, a["rwkv_ln_g"].to_broadcast([P, 512]))
        s_ev.issue(act, LNB, a["rwkv_ln_b"].to_broadcast([P, 512]))
        s_ev.issue(act, GNG, a["gla_norm_g"].to_broadcast([P, 128]))
        s_ev.issue(act, RW0[:, 0:512], a["rwkv_w0"])
        s_ev.issue(act, RW0[:, 512:768], a["gla_gate_b"])
        t_ev = (s_ev.sem, s_ev.n)
        state["gb"] = gain_rows(0)
        state["x"] = t_x

        t_xt = transposed(X, XT, 8, [[t_x, t_id]] * 2)
        for h in range(2):
            b = bank()
            k = tr_last(b.ap[:, 0:128], VR[:, h, :], t_vec)
            t_v = cp(dve, VEC[:, h, :], b.ap[:, 0:128], k)
            b.free = [t_v]

        for q in (pe, dve, act, pool):
            q.wait(t_eps, t_cst)

        def vec(half, i):
            return VEC[:, half, i:i + 1]

        WIN = a["even_w_in"][0]
        dm = off[0]
        Dm = take("D", 15, 256)
        PT = at(off[0], 15, 257)
        base = off[0]

        zero = fill(dve, PT[:, :, 0:1], 0.0)
        rwcols = [(1552 + 128 * i, 128) for i in range(14)] + [(3344, 32)]
        ptd = {}

        def got_rw(i, b, n, done):
            if i + n == 15:
                k = cp(act, PT[0:32, 14, 1:257], b.ap[0:32, 0:256], done)
            else:
                k = cp(act, PT[:, i:i + n, 1:257], b.ap[:, :].rearrange("p (c t) -> p c t", c=2), done)
            b.free = [k]
            for j in range(i, i + n):
                pn = 32 if j == 14 else 128
                d = tt(dve, Dm[0:pn, j, :], PT[0:pn, j, 0:256], PT[0:pn, j, 1:257], ALU.subtract, k, zero)
                ptd[j] = stt(Dm[0:pn, j, :], Dm[0:pn, j, :], VEC[0:pn, 0, j:j + 1], PT[0:pn, j, 1:257],
                             ALU.mult, ALU.add, d, t_v)

        columns(WIN, 8, rwcols[12:], XT, lambda i, b, n, done: got_rw(i + 12, b, n, done), t_xt)
        columns(WIN, 8, rwcols[:12], XT, got_rw, t_xt)

        off[0] += 15 * 257
        GQK = take("gqk", 4, 256)
        GLR = take("glr", 256)
        GV = take("gv", 2, 512)
        GG = take("gg", 2, 512)
        gl = {}

        def got_qk(i, b, n, done):
            src = b.ap[:, :].rearrange("p (c t) -> p c t", c=2)
            if i == 0:
                gl["q"] = fn(GQK[:, 0:2, :], src, ACT.Copy, done, scale=0.125)
                b.free = [gl["q"]]
            else:
                gl["k"] = cp(act, GQK[:, 2:4, :], src, done)
                b.free = [gl["k"]]

        def got_lr(i, b, n, done):
            gl["lr"] = cp(act, GLR[0:16, :], b.ap[0:16, 0:256], done)
            b.free = [gl["lr"]]

        def got_vg(t, o, m, b, done):
            if o == 0:
                gl["v", t] = cp(act, GV[:, t, :], b.ap[:, :], done)
            else:
                gl["v", t] = fn(GG[:, t, :], b.ap[:, :], ACT.Silu, done)
                gl["g", t] = gl["v", t]
            b.free = [gl["v", t]]


        SIG = take("sig", 2, 512)
        ee = off[0]
        EE = take("ee", 3, 4, 256)
        AA = take("aa", 4, 256)
        KK = take("kk", 4, 256)
        KP = take("kp", 4, 256)
        CAR = take("car", 4, 2, 2, 128)
        kt = off[0]
        KT = take("kt", 4, 256)
        BT = take("bt", 4, 256)
        G = take("g", 2, 512)
        VT = take("vt", 2, 512)
        KB = G2
        S0 = at(dm + 3072, 4, 64)
        RHS = at(dm + 3328, 512)
        RKM = take("rkm", 4, 8)
        SML = take("sml", 128)
        r_, k_, v_ = Dm[:, 0:4, :], Dm[:, 4:8, :], Dm[:, 8:12, :]
        t_th = fn(Dm[0:64, 12, :], Dm[0:64, 12, :], ACT.Tanh, ptd[12])
        t_sg = fn(Dm[:, 13, :], Dm[:, 13, :], ACT.Sigmoid, ptd[13])
        t_sg = fn(Dm[0:32, 14, :], Dm[0:32, 14, :], ACT.Sigmoid, ptd[14])
        t_sig = []
        for t in range(2):
            b = bank()
            mm(b.ap[:, :], Dm[0:64, 12, t * P:t * P + P], W2A2[0:64, :], True, False, t_th, t_ev, b.free)
            k = mm_last(b.ap[:, :], ones1, RW0[0:1, 0:512], False, True, t_eps)
            t_sig.append(fn(SIG[:, t, :], b.ap[:, :], ACT.Sigmoid, k))
            b.free = [t_sig[-1]]
        t_a = []
        for i in range(4):
            b = bank()
            k = mm_last(b.ap[:, 0:256], W2A2[64:128, i * P:i * P + P], Dm[64:128, 12, :], True, True,
                        ptd[12], t_ev, b.free)
            t_a.append(fn(AA[:, i, :], b.ap[:, 0:256], ACT.Sigmoid, k, t_v, bias=vec(0, 23 + i)))
            b.free = [t_a[-1]]
        t_g = []
        for t in range(2):
            b = bank()
            mm(b.ap[:, :], Dm[:, 13, t * P:t * P + P], G2[:, 0, :], True, False, t_sg, t_ev, b.free)
            k = mm_last(b.ap[:, :], Dm[0:32, 14, t * P:t * P + P], G2[0:32, 1, :], False, True)
            t_g.append(cp(act, G[:, t, :], b.ap[:, :], k))
            b.free = [t_g[-1]]
        t_e = {}
        for i in range(4):
            b = bank()
            for w, name in enumerate(("cinc", "cexc")):
                for t in range(2):
                    f = mm_last if (w, t) == (1, 1) else mm
                    k = f(b.ap[:, w * 256 + t * P:w * 256 + t * P + P], SIG[:, t, i * P:i * P + P],
                          cst(name), True, True, t_sig[t], b.free)
            fn(EE[:, 0, i, :], b.ap[:, 0:256], ACT.Exp, k, scale=-DECAY)
            fn(EE[:, 1, i, :], b.ap[:, 0:256], ACT.Exp, k, scale=DECAY)
            t_e[i] = fn(EE[:, 2, i, :], b.ap[:, 256:512], ACT.Exp, k, scale=-DECAY)
            b.free = [t_e[i]]
        b = bank()
        for i in range(4):
            mm(b.ap[:, i:i + 1], SIG[:, 0, i * P:i * P + P], SM[:, 4:5], True, False, b.free)
            k = mm_last(b.ap[:, i:i + 1], SIG[:, 1, i * P:i * P + P], SM[:, 5:6], False, True)
        t_gm = fn(SML[:, 0:4], b.ap[:, 0:4], ACT.Exp, k, scale=-DECAY)
        b.free = [t_gm]
        t_kk = []
        for i in range(4):
            k = ts(dve, KK[:, i, :], Dm[:, 4 + i, :], vec(0, 15 + i), None, ALU.mult, None, ptd[4 + i])
            t_kk.append(tt(dve, KP[:, i, :], KK[:, i, :], KK[:, i, :], ALU.mult, k))
        sq = []
        for i in range(0, 4, 2):
            b = bank()
            mm(b.ap[:, 0:256], cst("heads"), KP[:, i, :], True, True, t_kk[i], b.free)
            k = mm_last(b.ap[:, 256:512], cst("heads"), KP[:, i + 1, :], True, True, t_kk[i + 1])
            k = ts(dve, KP[:, i:i + 2, :], b.ap[:, :].rearrange("p (c t) -> p c t", c=2), 1e-24, None,
                   ALU.max, None, k)
            b.free = [k]
            k = fn(KP[:, i:i + 2, :], KP[:, i:i + 2, :], ACT.Sqrt, k)
            k = recip(KP[:, i:i + 2, :], KP[:, i:i + 2, :], k)
            sq.append(tt(dve, KK[:, i:i + 2, :], KK[:, i:i + 2, :], KP[:, i:i + 2, :], ALU.mult, k))
        def gla_projections():
            columns(WIN, 8, [(1536, 16)], XT, got_lr)
            columns(WIN, 8, [(0, 128), (128, 128), (256, 128), (384, 128)], XT, got_qk)
            rows(WIN, 8, 512, 1024, XT, got_vg)

        tl = []
        for i in range(4):
            ka = vec(0, 19 + i)
            k = ts(dve, KP[:, i, :], AA[:, i, :], 1.0, ka, ALU.subtract, ALU.mult, t_a[i], sq)
            k = stt(KP[:, i, :], KP[:, i, :], 1.0, Dm[:, 4 + i, :], ALU.add, ALU.mult, k)
            tl.append(tt(dve, KT[:, i, :], KP[:, i, :], EE[:, 1, i, :], ALU.mult, k, t_e[i]))
            tl.append(stt(CAR[:, i, :, 0, :], KK[:, i, :].rearrange("p (a b) -> p a b", a=2), -1.0,
                          EE[:, 2, i, :].rearrange("p (a b) -> p a b", a=2), ALU.mult, ALU.mult, t_e[i]))
            k2 = tt(pool, AA[:, i, :], AA[:, i, :], KK[:, i, :], ALU.mult, sq, t_a[i], k)
            tl.append(tt(pool, BT[:, i, :], AA[:, i, :], EE[:, 1, i, :], ALU.mult, k2, t_e[i]))
            tl.append(tt(pool, CAR[:, i, :, 1, :], Dm[:, i, :].rearrange("p (a b) -> p a b", a=2),
                         EE[:, 0, i, :].rearrange("p (a b) -> p a b", a=2), ALU.mult, t_e[i], ptd[i]))
            tl.append(tt(pool, KP[:, i, :], KP[:, i, :], Dm[:, i, :], ALU.mult, k, tl[-4]))
        t_til = tl
        gla_projections()
        k = fill(pool, RKM, 0.0)
        for i in range(4):
            for hh in range(2):
                k = cp(pool, RKM[64 * hh:64 * hh + 64, i, 2 * i + hh:2 * i + hh + 1],
                       VEC[64 * hh:64 * hh + 64, 0, 27 + i:28 + i], k, t_v)
        t_rkm = k
        b = bank()
        for t in range(2):
            for i in range(4):
                f = mm_last if (t, i) == (1, 3) else mm
                k = f(b.ap[:, 8 * t:8 * t + 8], KP[:, i, t * P:t * P + P], RKM[:, i, :], i == 0, i == 3,
                      t_til, t_rkm, b.free)
        t_bon = cp(dve, SML[:, 8:24], b.ap[:, 0:16], k)
        b.free = [t_bon]
        t_vt = []
        for t in range(2):
            b = bank()
            for i in range(4):
                f = tr_last if i == 3 else tr
                k = f(b.ap[:, i * P:i * P + P], Dm[:, 8 + i, t * P:t * P + P], ptd[8 + i], b.free)
            t_vt.append(cp(act, VT[:, t, :], b.ap[:, :], k))
            b.free = [t_vt[-1]]
        for w, src in enumerate((KT, BT)):
            b = bank()
            for i in range(4):
                f = tr_last if i == 3 else tr
                k = f(b.ap[:, i * P:i * P + P], src[:, i, 0:P], b.free)
            t_kb = cp(act, KB[:, w, :], b.ap[:, :], k, t_g)
            b.free = [t_kb]

        AAB = at(base, 16, 128)
        PP = at(base + 2048, 8, 128)
        AAK = at(ee + 2048, 16, 128)
        ARB = at(ee + 4096, 16, 128)
        ARK = take("ark", 16, 128)
        TI = at(dm, 16, 128)
        PP2 = at(dm + 2048, 8, 128)
        TJ = at(kt, 16, 128)
        ALA = at(ee, 16, 128)
        t_m = {}
        for s in range(16):
            t, h = s // 8, s % 8
            r = slice(64 * (h % 2), 64 * (h % 2) + 64)
            b = bank()
            for j, lhs in enumerate((BT, KT)):
                k = (mm_last if j else mm)(
                    b.ap[:, 256 * j:256 * j + 256], lhs[r, h // 2, t * P:t * P + P],
                    CAR[r, h // 2, t, :, :].rearrange("p a b -> p (a b)"), True, True, t_til, t_bon, b.free)
            for i, (dst, m) in enumerate(((AAB, "strict"), (ARB, "incl"), (AAK, "strict"), (ARK, "incl"))):
                t_m[s] = tt(dve, dst[:, s, :], b.ap[:, 128 * i:128 * i + 128], cst(m), ALU.mult, k)
            b.free = [t_m[s]]
        LA = SIG
        t_la = []
        for t in range(2):
            b = bank()
            m_, e_ = XN[:, t, 0:256], XN[:, t, 256:512]
            mm(b.ap[:, 0:256], GLR[0:16, t * P:t * P + P], GW2[0:16, :], True, False, gl["lr"], t_ev, b.free)
            k = mm_last(b.ap[:, 0:256], ones1, RW0[0:1, 512:768], False, True)
            k1 = fn(e_, b.ap[:, 0:256], ACT.Abs, k)
            k2 = ts(dve, m_, b.ap[:, 0:256], -1.0, 0.0, ALU.mult, ALU.max, k1)
            b.free = [k2]
            k = fn(e_, e_, ACT.Exp, k1, scale=-1.0)
            k = fn(e_, e_, ACT.Ln, k, bias=SM[:, 3:4])
            t_la.append(tt(dve, LA[:, t, 0:256], m_, e_, ALU.add, k, k2, t_gm, t_e[3]))
        NG = 4
        t_ti = [None] * NG
        t_tj = [None] * NG
        t_al = [None] * NG
        t_pp = [None] * NG

        def group(x, g):
            return x[:, 4 * g:4 * g + 4, :]

        def pview(g):
            return PP[:, 4 * g:4 * g + 4, :] if g < 2 else PP2[:, 4 * g - 8:4 * g - 4, :]

        def flat(x):
            return x.rearrange("p s t -> p (s t)")

        bc = lambda name: cst(name).unsqueeze(1).to_broadcast([P, 4, P])
        free_al = [None] * NG
        for lv in range(7):
            for g in range(NG):
                need = t_m[4 * g + 3]
                t_al[g] = tt(pool, group(ALA, g), group(AAB, g), bc(f"lvl{lv}"), ALU.mult, need, t_til,
                             free_al[g])
                b = bank()
                for s in range(4):
                    k = (mm_last if s == 3 else mm)(
                        b.ap[:, s * P:s * P + P], ALA[:, 4 * g + s, :],
                        ident if lv == 0 else TI[:, 4 * g + s, :], True, True,
                        t_al[g], t_ti[g], b.free)
                free_al[g] = k
                if lv == 0:
                    t_ti[g] = tt(dve, group(TI, g), b.ap[:, :].rearrange("p (s t) -> p s t", s=4),
                                 bc("ident"), ALU.add, k, t_vt, t_til)
                    b.free = [t_ti[g]]
                    t_tj[g] = tt(dve, group(TJ, g), group(ALA, g), bc("ident"), ALU.add, t_al[g], t_kb)
                    free_al[g] = [k, t_tj[g]]
                else:
                    t_pp[g] = cp(act, pview(g), b.ap[:, :].rearrange("p (s t) -> p s t", s=4), k, t_ti[g], t_tj[g])
                    b.free = [t_pp[g]]
            if lv == 0:
                continue
            for g in range(NG):
                p_ = pview(g)
                bj = bank()
                for s in range(4):
                    kj = (mm_last if s == 3 else mm)(bj.ap[:, s * P:s * P + P], p_[:, s, :],
                                                     TJ[:, 4 * g + s, :], True, True, t_pp[g], t_tj[g], bj.free)
                if lv < 6:
                    bi = bank()
                    for s in range(4):
                        ki = (mm_last if s == 3 else mm)(bi.ap[:, s * P:s * P + P], TJ[:, 4 * g + s, :],
                                                         p_[:, s, :], True, True, bi.free)
                    t_ti[g] = tt(dve, flat(group(TI, g)), bi.ap[:, :], flat(group(TI, g)), ALU.add, ki)
                    bi.free = [t_ti[g]]
                else:
                    ki = kj
                t_tj[g] = tt(dve, flat(group(TJ, g)), bj.ap[:, :], flat(group(TJ, g)), ALU.add, kj, ki)
                bj.free = [t_tj[g]]

        Y = [None, None]
        O = XN

        def chunk_steps():
            t_s0 = None
            for t in range(2):
                rd = []
                for j in range(2):
                    b = bank()
                    r = slice(64 * j, 64 * j + 64)
                    for i in range(4):
                        h = 2 * i + j
                        sl = slice(64 * i, 64 * i + 64)
                        k = (mm_last if t == 0 and i == 3 else mm)(
                            b.ap[:, sl], AAK[:, 8 * t + h, :], VT[:, t, 64 * h:64 * h + 64], True, t == 0,
                            t_m[15], t_vt[t], b.free)
                        if t:
                            k = mm_last(b.ap[:, sl], CAR[r, i, t, 0, :], S0[r, i, :], False, True, t_s0)
                    rd.append(cp(dve, RHS[:, 256 * j:256 * j + 256], b.ap[:, 0:256], k, t_s0, t_g))
                    b.free = [rd[j]]
                yield
                b = bank()
                for h in range(8):
                    sl = slice(256 * (h % 2) + 64 * (h // 2), 256 * (h % 2) + 64 * (h // 2) + 64)
                    k2 = (mm_last if h == 7 else mm)(b.ap[:, sl], TJ[:, 8 * t + h, :], RHS[:, sl], True, True,
                                                     rd[h % 2], t_tj, b.free)
                t_u = cp(dve, RHS, b.ap[:, :], k2)
                b.free = [t_u]
                yield
                yt = []
                for j in range(2):
                    b = bank()
                    r = slice(64 * j, 64 * j + 64)
                    for i in range(4):
                        h = 2 * i + j
                        sl = slice(64 * i, 64 * i + 64)
                        mm(b.ap[:, sl], ARK[:, 8 * t + h, :], VT[:, t, 64 * h:64 * h + 64], True, False, b.free)
                        k = (mm_last if t == 0 and i == 3 else mm)(
                            b.ap[:, sl], ARB[:, 8 * t + h, :], RHS[:, 256 * j + 64 * i:256 * j + 64 * i + 64],
                            False, t == 0, t_u)
                        if t:
                            k = mm_last(b.ap[:, sl], CAR[r, i, t, 1, :], S0[r, i, :], False, True)
                    dst = O[:, t, 512:1024].rearrange("p (i j n) -> p j i n", i=4, j=2)[:, j]
                    yt.append(cp(act, dst, b.ap[:, 0:256].rearrange("p (i n) -> p i n", i=4), k))
                    b.free = [yt[j]]
                Y[t] = yt
                yield
                if t == 0:
                    b = bank()
                    for i in range(4):
                        sl = slice(128 * i, 128 * i + 128)
                        mm(b.ap[:, sl], KB[:, 0, sl], VT[:, 0, sl], True, False, t_kb, b.free)
                        k = mm_last(b.ap[:, sl], KB[:, 1, sl],
                                    RHS.rearrange("p (j i v) -> p i j v", j=2, i=4)[:, i], False, True)
                    for j in range(2):
                        pr = slice(64 * j, 64 * j + 64)
                        t_s0 = tt(dve, S0[pr, :, :],
                                  b.ap[pr, :].rearrange("p (i v) -> p i v", i=4)[:, :, 64 * j:64 * j + 64],
                                  SML[pr, 0:4].unsqueeze(2).to_broadcast([64, 4, 64]), ALU.mult, k, t_gm, t_g)
                    b.free = [t_s0]
        AT = TI.rearrange("p s t -> p (s t)")

        def pieces(x):
            return [x.rearrange("p s t -> p (s t)")[:, 512 * i:512 * i + 512].rearrange("p (c t) -> p c t", c=2)
                    for i in range(x.shape[1] // 4)]

        QE, KE, EG = pieces(PP) + pieces(PP2), pieces(AAB), pieces(ALA)
        inverse_done = [pe.now(), dve.now(), act.now(), pool.now()]
        at0 = fill(dve, AT[:, 0:1024], 0.0, inverse_done)
        t_at, t_cr = at0, None
        gq, gk = GQK[:, 0:2, :], GQK[:, 2:4, :]
        used = [inverse_done] * 4

        def decayed(lv):
            if lv < 0:
                return gq, gk, [gl["q"], gl["k"]]
            i = lv % 4
            b = bank()
            for c in range(2):
                for t in range(2):
                    m = cst(f"acc{lv}") if lv < 7 else cst(("after", "upto")[t])
                    k = (mm_last if (c, t) == (1, 1) else mm)(
                        b.ap[:, c * 256 + t * P:c * 256 + t * P + P], LA[:, t, c * P:c * P + P], m,
                        True, True, t_la, b.free)
            k = fn(EG[i], b.ap[:, :].rearrange("p (c t) -> p c t", c=2), ACT.Exp, k, used[i], scale=-1.0 / 16)
            b.free = [k]
            return QE[i], KE[i], [tt(dve, QE[i], gq, EG[i], ALU.mult, k, gl["q"], used[i]),
                                  tt(pool, KE[i], gk, EG[i], ALU.mult, k, gl["k"], used[i])]

        def level_products(lv, q_, k_e, ready):
            nonlocal t_at, t_cr
            for j in range(2):
                r = slice(64 * j, 64 * j + 64)
                b = bank()
                if lv < 7:
                    for c in range(2):
                        for t in range(2):
                            k = (mm_last if (c, t) == (1, 1) else mm)(
                                b.ap[:, (2 * c + t) * P:(2 * c + t) * P + P],
                                k_e[r, c, t * P:t * P + P], q_[r, c, t * P:t * P + P], True, True,
                                ready, b.free)
                    name = "ident" if lv < 0 else f"lvl{lv}"
                    mask = cst(name).bitcast(I32).unsqueeze(1).to_broadcast([P, 4, P])
                    dst = AT[:, 512 * j:512 * j + 512].rearrange("p (s t) -> p s t", s=4)
                    t_at = select(dst, mask, b.ap[:, :].rearrange("p (s t) -> p s t", s=4), k, t_at)
                    b.free = [t_at]
                else:
                    for c in range(2):
                        k = (mm_last if c else mm)(b.ap[:, c * P:c * P + P], k_e[r, c, 0:P],
                                                   q_[r, c, P:2 * P], True, True, ready, b.free)
                    t_cr = cp(dve, AT[:, 1024 + 256 * j:1280 + 256 * j], b.ap[:, 0:256], k, at0)
                    b.free = [t_cr]
            if lv >= 0:
                used[lv % 4] = [k]

        ops = {lv: decayed(lv) for lv in range(-1, 2)}
        steps = chunk_steps()
        for lv in range(-1, 8):
            next(steps, None)
            if lv + 3 < 8:
                ops[lv + 3] = decayed(lv + 3)
            level_products(lv, *ops[lv])
        for _ in steps:
            pass
        TM3 = AAK.rearrange("p s t -> p (s t)")
        TM = TJ.rearrange("p s t -> p (s t)")
        for t in range(2):
            y = O[:, t, 512:1024].rearrange("p (h n) -> p h n", h=8)
            tm = TM[:, t * 512:t * 512 + 512].rearrange("p (h n) -> p h n", h=8)
            tm2 = TM[:, 1024 + t * 512:1536 + t * 512].rearrange("p (h n) -> p h n", h=8)
            st = SML[:, 32 + 16 * t:48 + 16 * t]
            mu, va = st[:, 0:8], st[:, 8:16]
            b8 = lambda v: v.unsqueeze(2).to_broadcast([P, 8, 64])
            k = total(mu, y, Y[t])
            k = ts(dve, mu, mu, 1.0 / 64, None, ALU.mult, None, k)
            k = tt(dve, y, y, b8(mu), ALU.subtract, k)
            k = tt(dve, tm, y, y, ALU.mult, k, t_ti, Y)
            k = total(va, tm, k)
            k = rstd(va, va, eps_gn, 1.0 / 64, k, t_eps)
            k = tt(dve, y, y, b8(va), ALU.mult, k)
            k = tt(pool, y, y, LNG.rearrange("p (h n) -> p h n", h=8), ALU.mult, k, t_ev)
            k = tt(pool, y, y, LNB.rearrange("p (h n) -> p h n", h=8), ALU.add, k)
            k2 = tt(dve, tm2, VT[:, t, :].rearrange("p (h n) -> p h n", h=8), b8(SML[:, 8 + 8 * t:16 + 8 * t]),
                    ALU.mult, t_bon, t_vt, Y)
            k = tt(pool, y, y, tm2, ALU.add, k, k2)
            Y[t] = tt(pool, y, y, G[:, t, :].rearrange("p (h n) -> p h n", h=8), ALU.mult, k, t_g[t])

        for t in range(2):
            b = bank()
            for h in range(4):
                sl = slice(h * P, h * P + P)
                blk = 512 * (h % 2) + (2 * (h // 2) + t) * P
                crs = 1024 + 256 * (h % 2) + 128 * (h // 2)
                k = (mm_last if t == 0 and h == 3 else mm)(
                    b.ap[:, sl], AT[:, blk:blk + P], GV[:, t, sl], True, t == 0,
                    t_at, gl["v", 0], gl["v", 1], b.free)
                if t:
                    k = mm_last(b.ap[:, sl], AT[:, crs:crs + P], GV[:, 0, sl], False, True, t_cr)
            o = O[:, t, 0:512].rearrange("p (h n) -> p h n", h=4)
            k = cp(act, O[:, t, 0:512], b.ap[:, :], k)
            b.free = [k]
            tm = TM3[:, t * 512:t * 512 + 512].rearrange("p (h n) -> p h n", h=4)
            ss = SML[:, 64 + 4 * t:68 + 4 * t]
            b4 = ss.unsqueeze(2).to_broadcast([P, 4, P])
            k1 = tt(dve, tm, o, o, ALU.mult, k, Y)
            k1 = total(ss, tm, k1)
            k1 = rstd(ss, ss, eps_rms, 1.0 / 128, k1)
            gg = GG[:, t, :].rearrange("p (h n) -> p h n", h=4)
            k2 = tt(pool, gg, gg, GNG.unsqueeze(1).to_broadcast([P, 4, P]), ALU.mult, gl["g", t], t_ev)
            k = tt(dve, o, o, b4, ALU.mult, k1)
            Y[t] = [Y[t], tt(dve, o, o, gg, ALU.mult, k, k2)]
        OT = at(dm, 8, 256)
        k = transposed(O, OT, 8, Y)
        rows(a["even_w_out"][0], 8, 0, 1024, OT, residual_norm(0), None, k)
        t_xt = finish_norm(0, pe.now())

        MOD = at(ARENA - 48, 48)
        G12 = at(ARENA - 48 - 2048, 2, 1024)
        ACCA = at(8192, 2, 1024)
        CSL = at(10240, 8)
        WA = a["w_ada_2"][0]
        ada = {"next": 0, "later": None}

        def start_modulation(which):
            prev = [dve.now(), act.now(), pe.now(), pool.now()]
            ada["c"] = fn(CSL, VEC[:, 1, 112:120], ACT.Silu, *prev)
            ada["acc"] = [prev, prev]
            g = G12[:, which, :]
            j = 2 + 3 * which
            sa = Dma(sem(f"s_ada{which}"))
            sa.issue(pool, g, a["b_ada_2"][:, 1024 * j:1024 * j + 1024].to_broadcast([P, D]), *prev)
            ada["gate"] = sa.issue(pool, at(10256, 1024), a["norm_gains_2"][0, 1 + 2 * which:2 + 2 * which, :]
                                   .to_broadcast([P, D]))

        def modulation_sums():
            if ada["later"]:
                ada["later"]()
                ada["later"] = None

        def modulation_piece():
            modulation_sums()
            j, k0 = ada["next"] // 4, 2 * (ada["next"] % 4)
            ada["next"] += 1
            acc = ACCA[:, j % 2, :]
            k = ada.get("k")
            slot, w, there = load(WA[k0 * P:k0 * P + 256, 1024 * j:1024 * j + 1024]
                                  .rearrange("(c p) n -> p c n", p=P), 2048, 2)
            for c in range(2):
                if k0 + c == 0:
                    k = ts(dve, acc, w[:, c, :], CSL[:, 0:1], None, ALU.mult, None, there, ada["c"],
                           ada["acc"][j % 2])
                else:
                    k = stt(acc, w[:, c, :], CSL[:, k0 + c:k0 + c + 1], acc, ALU.mult, ALU.add, there, k)
            slot.free = [k]
            ada["k"] = k
            if k0 == 6:
                ada["later"] = lambda: modulation_column(j, acc, k)

        def modulation_column(j, acc, k):
            b = bank()
            if j in (2, 5):
                g = G12[:, j // 3, :]
                for o in range(0, 1024, 512):
                    if o:
                        b = bank()
                    k2 = mm_last(b.ap[:, :], cst("ones"), acc[:, o:o + 512], True, True, k, b.free)
                    k3 = tt(dve, g[:, o:o + 512], b.ap[:, :], g[:, o:o + 512], ALU.add, k2, ada["gate"])
                    k3 = tt(dve, g[:, o:o + 512], g[:, o:o + 512], at(10256 + o, 512), ALU.mult, k3)
                    b.free = [k3]
                ada["g", j // 3] = k3
            else:
                for i in range(8):
                    k2 = (mm_last if i == 7 else mm)(b.ap[:, i:i + 1], acc[:, i * P:i * P + P], SM[:, 3:4],
                                                     True, True, k, b.free)
                k3 = tt(dve, MOD[:, 8 * j:8 * j + 8], b.ap[:, 0:8], VEC[:, 1, 32 + 8 * j:40 + 8 * j],
                        ALU.add, k2, t_v)
                if j in (1, 4):
                    k3 = stt(MOD[:, 8 * j:8 * j + 8], MOD[:, 8 * j:8 * j + 8], 1.0,
                             VEC[:, 1, 80 + 16 * (j // 3):88 + 16 * (j // 3)], ALU.add, ALU.mult, k3)
                b.free = [k3]
                ada["m", j] = k3
            ada["acc"][j % 2] = [k2]

        def ffn(layer, i, along=None):
            nonlocal t_xt
            HT = at(0, 22, 256)
            UP = at(22 * 256, 2, 512)
            W = a["ffn_w_gate_up"][layer]
            ks = []
            start_modulation(layer)
            for j in range(0, 22, 2):
                modulation_piece()
                if along and j == 8:
                    state["along"] = along()
                slot, w, there = load(W[:, j * P:j * P + 256].rearrange("(c p) n -> p c n", p=P), 2048, 8)
                slot2, w2, there2 = load(W[:, FFN + j * P:FFN + j * P + 256].rearrange("(c p) n -> p c n", p=P), 2048, 8)
                bg, bu = bank(), bank()
                for (ww, th, bb) in ((w, there, bg), (w2, there2, bu)):
                    for h in range(2):
                        for c in range(8):
                            k = (mm_last if c == 7 else mm)(
                                bb.ap[:, 256 * h:256 * h + 256], ww[:, c, h * P:h * P + P], XT[:, c, :],
                                c == 0, c == 7, th, bb.free, t_xt)
                    if bb is bg:
                        slot.free = [k]
                        kg = k
                slot2.free = [k]
                u = UP[:, (j // 2) % 2, :]
                prev = ks[-2] if len(ks) > 1 else None
                kg = fn(u, bg.ap[:, :], ACT.Silu, kg, prev)
                bg.free = [kg]
                d = tt(dve, HT[:, j:j + 2, :].rearrange("p c t -> p (c t)"), bu.ap[:, :], u, ALU.mult, k, kg)
                bu.free = [d]
                ks.append(d)
            modulation_piece()
            rows(a["ffn_w_down"][layer], 22, 0, 1024, HT, residual_norm(i), None, ks)
            modulation_sums()
            t_xt = finish_norm(i, pe.now())

        ffn(0, 1)

        off[0] = 0
        CQ = take("cq", 2, 1056)
        CT = take("ct", 8, 256)
        QQ = take("qq", 2, 1536)
        KF = take("kf", 2, 1536)
        V2 = take("v2", 2, 1024)
        O2 = take("o2", 2, 1024)
        OT2 = take("ot2", 8, 256)
        PR = take("pr", 4, 2, 256)
        PX = take("px", 2, 512)
        MK = take("mk", 384)
        PS_ = take("pos", 2)
        FR = take("fr", 16)
        CS = take("cs", 2, 2, 16)
        RT = take("rt", 2, 4, 16)
        R2 = take("r2", 2, 2, 256)
        ST2 = take("st2", 256)
        PI_ = sb("PI", [P, 2], I32)
        prev = [state["x"], t_xt, pe.now()]
        s_odd = Dma(sem("s_odd"))
        s_odd.issue(sp, MK, a["mla_mask"], *prev)
        s_odd.issue(sp, FR, a["rope_freq"], *prev)
        t_odd = s_odd.issue(sp, PI_[:, :], a["positions"].rearrange("b (t p) -> p (b t)", p=P),
                            allow_slow_non_contiguous=True)
        k = cp(dve, PS_, PI_[:, :], t_odd)
        parts = [6.28125]
        rest = 2 * np.pi - parts[0]
        for bits in (14, 22):
            p_ = float(np.floor(rest * 2.0 ** bits) / 2.0 ** bits)
            parts.append(p_)
            rest -= p_
        parts.append(float(np.float32(rest)))
        MAGIC = 1.5 * 2.0 ** 23
        t_cs = []
        for t in range(2):
            ang, n_ = RT[:, t, 0, :], RT[:, t, 1, :]
            k1 = ts(dve, ang, FR, PS_[:, t:t + 1], None, ALU.mult, None, k)
            k1 = ts(dve, n_, ang, float(1 / (2 * np.pi)), MAGIC, ALU.mult, ALU.add, k1)
            k1 = ts(dve, n_, n_, MAGIC, None, ALU.subtract, None, k1)
            for p_ in parts:
                k1 = stt(ang, n_, -p_, ang, ALU.mult, ALU.add, k1)
            k1 = ts(dve, ang, ang, 3.1415925, -3.1415925, ALU.min, ALU.max, k1)
            k2 = fn(CS[:, t, 1, :], ang, ACT.Sin, k1)
            k2 = fn(n_, ang, ACT.Sin, k2, scale=0.5)
            k2 = tt(dve, n_, n_, n_, ALU.mult, k2)
            t_cs.append(ts(dve, CS[:, t, 0, :], n_, -2.0, 1.0, ALU.mult, ALU.add, k2))

        od = {}
        SQ = QQ

        def got_p(t, o, m, b, done):
            k = cp(act if o == 512 else dve, CQ[:, t, o:o + m], b.ap[:, 0:m], done)
            b.free = [k]
            od[t, o] = k

        rows(a["mla_w_in"][0], 8, 0, 1056, XT, got_p, None, t_xt)
        kn = []
        for t in range(2):
            k = stats = None
            for j, (lo, n) in enumerate(((0, 768), (768, 256))):
                acc = ST2[:, 2 * t + j:2 * t + j + 1]
                k = ttr(SQ[:, t, lo:lo + n], CQ[:, t, lo:lo + n], CQ[:, t, lo:lo + n], 0.0, ALU.mult, ALU.add, acc, od[t, 0], od[t, 512])
                k = rstd(acc, acc, eps_rms, 1.0 / n, k)
                k = ts(dve, CQ[:, t, lo:lo + n], CQ[:, t, lo:lo + n], acc, None, ALU.mult, None, k)
            kn.append(k)
        k = transposed(CQ, CT, 8, kn, lambda c: vec(0, 95 + c) if c < 6 else vec(0, 101 + c - 6))

        def rope(x, t, n, *after):
            pr = x.rearrange("p h (i two) -> p h i two", two=2)
            x1, x2 = pr[:, :, :, 0], pr[:, :, :, 1]
            cos = CS[:, t, 0, :].unsqueeze(1).to_broadcast([P, n, 16])
            sin = CS[:, t, 1, :].unsqueeze(1).to_broadcast([P, n, 16])
            u = R2[:, 0, 0, 0:n * 16].rearrange("p (h i) -> p h i", h=n)
            v = R2[:, 0, 1, 0:n * 16].rearrange("p (h i) -> p h i", h=n)
            w = R2[:, 1, 0, 0:n * 16].rearrange("p (h i) -> p h i", h=n)
            y = R2[:, 1, 1, 0:n * 16].rearrange("p (h i) -> p h i", h=n)
            k1 = tt(dve, u, x1, cos, ALU.mult, t_cs, dve.now(), *after)
            k2 = tt(dve, v, x2, sin, ALU.mult)
            k3 = tt(dve, w, x1, sin, ALU.mult)
            k4 = tt(dve, y, x2, cos, ALU.mult)
            k5 = tt(dve, x1, u, v, ALU.subtract, k4)
            return tt(dve, x2, w, y, ALU.add, k5)

        def got_q(t, o, m, b, done):
            k = fn(QQ[:, t, o:o + m], b.ap[:, 0:m], ACT.Copy, done, kn, scale=MLA_SCALE)
            b.free = [k]
            od["q", t] = k

        rows(a["mla_w_q_b"][0], 6, 0, 1536, CT, got_q, None, k)

        def got_kv(half):
            def got(t, o, m, b, done):
                h0 = 8 * half + 4 * (o // 512)
                src = b.ap[:, :].rearrange("p (h n) -> p h n", h=4)
                kf = KF[:, t, :].rearrange("p (h n) -> p h n", h=16)[:, h0:h0 + 4, 0:64]
                v2 = V2[:, t, :].rearrange("p (h n) -> p h n", h=16)[:, h0:h0 + 4, :]
                k = cp(act, kf, src[:, :, 0:64], done)
                k = cp(act, v2, src[:, :, 64:128], done)
                b.free = [k]
                od["kv", t] = k
            return got

        for half in range(2):
            rows(a["mla_w_kv_b"][0], 2, 1024 * half, 1024, CT[:, 6:8, :], got_kv(half), None, k)
        t_q = []
        t_k = []
        for t in range(2):
            q16 = QQ[:, t, :].rearrange("p (h n) -> p h n", h=16)
            t_q.append(rope(q16[:, :, 64:96], t, 16, od["q", t]))
            kpe = CQ[:, t, 1024:1056].unsqueeze(1)
            kr = rope(kpe, t, 1, od[t, 1024])
            kf = KF[:, t, :].rearrange("p (h n) -> p h n", h=16)[:, :, 64:96]
            kr = cp(dve, kf, CQ[:, t, 1024:1056].unsqueeze(1).to_broadcast([P, 16, 32]), kr)
            t_k.append([kr, od["kv", t]])

        def attend(heads, q_of, k_of, mask_of, v_of, out, sink=None, ready=None):
            MX = ST2[:, 16:48]
            SU = ST2[:, 48:80]
            NM = ST2[:, 80:112]
            RS = ST2[:, 112:144]
            pr_free, px_free, result = {}, {}, []
            turn["banks"] = 6
            items = [(t, h) for t in range(2) for h in range(heads)]
            soft, moved = {}, {}

            def softened(i):
                t, h = items[i]
                nk, w, col = P * (t + 1), i % 4, t * 16 + h
                q, kq = q_of(h, t)
                kk, kkk = k_of(h, nk)
                b = bank()
                k = mm_last(b.ap[:, 0:nk], q, kk, True, True, kq, kkk, b.free)
                pr = PR[:, w, 0, 0:nk]
                k = ttr(pr, b.ap[:, 0:nk], mask_of(h, t), NEG, ALU.add, ALU.max,
                        MX[:, col:col + 1], k, pr_free.get(w), ready)
                b.free = [k]
                if sink is not None:
                    k = tt(dve, MX[:, col:col + 1], MX[:, col:col + 1], sink[:, h:h + 1], ALU.max, k)
                k = ts(dve, NM[:, col:col + 1], MX[:, col:col + 1], -1.0, None, ALU.mult, None, k)
                k = fn(PR[:, w, 1, 0:nk], pr, ACT.Exp, k, bias=NM[:, col:col + 1], accum_out=SU[:, col:col + 1])
                if sink is not None:
                    k = fn(RS[:, col:col + 1], sink[:, h:h + 1], ACT.Exp, k, bias=NM[:, col:col + 1])
                soft[i] = k

            def turned(i):
                t, h = items[i]
                nk, ex = P * (t + 1), PR[:, i % 4, 1]
                b = bank()
                for j in range(t + 1):
                    kt = (tr_last if j == t else tr)(b.ap[:, j * P:j * P + P], ex[:, j * P:j * P + P],
                                                     soft[i], b.free)
                pr_free[i % 4] = kt
                moved[i] = cp(act if i % 2 else dve, PX[:, i % 2, 0:nk], b.ap[:, 0:nk], kt, px_free.get(i % 2))
                b.free = [moved[i]]

            def weighed(i):
                t, h = items[i]
                px = PX[:, i % 2]
                bo = psum[6 + h // 8]
                hs = slice(64 * (h % 8), 64 * (h % 8) + 64)
                for j in range(t + 1):
                    v, kv = v_of(h, j)
                    kp = (mm_last if j == t else mm)(bo.ap[:, hs], px[:, j * P:j * P + P], v,
                                                     j == 0, j == t, moved[i], kv, bo.free)
                px_free[i % 2] = kp
                if h % 8 == 7:
                    c0 = t * 16 + h - 7
                    k = soft[i]
                    if sink is not None:
                        k = tt(dve, SU[:, c0:c0 + 8], SU[:, c0:c0 + 8], RS[:, c0:c0 + 8], ALU.add, k)
                    k = recip(RS[:, c0:c0 + 8], SU[:, c0:c0 + 8], k)
                    o = out(h - 7, t)
                    k = tt(dve, o.rearrange("p (h n) -> p h n", h=8),
                           bo.ap[:, :].rearrange("p (h n) -> p h n", h=8),
                           RS[:, c0:c0 + 8].unsqueeze(2).to_broadcast([P, 8, 64]), ALU.mult, k, kp)
                    bo.free = [k]
                    result.append(k)

            n = len(items)
            for i in range(n + 4):
                if i < n:
                    softened(i)
                if 0 <= i - 3 < n:
                    turned(i - 3)
                if 0 <= i - 4 < n:
                    weighed(i - 4)
            turn["banks"] = 8
            return result

        QT = at(0, 16, 256)
        KTA = take("kta", 16, 256)
        t_hd = {}
        for h in range(16):
            for key, src, toks in (("q", QQ, t_q), ("k", KF, t_k)):
                dst = QT if key == "q" else KTA
                b = bank()
                for t in range(2):
                    k = (tr_last if t else tr)(b.ap[0:96, t * P:t * P + P], src[:, t, 96 * h:96 * h + 96],
                                               toks[t], b.free)
                k = cp(act if key == "q" else dve, dst[0:96, h, :], b.ap[0:96, 0:256], k, t_q, t_k, pe.now())
                b.free = [k]
                t_hd[key, h] = k
        res = attend(16,
                     lambda h, t: (QT[0:96, h, t * P:t * P + P], t_hd["q", h]),
                     lambda h, nk: (KTA[0:96, h, 0:nk], t_hd["k", h]),
                     lambda h, t: MK[:, 128 * t:128 * t + 128 + 128 * t],
                     lambda h, j: (V2[:, j, 64 * h:64 * h + 64], od["kv", j]),
                     lambda h, t: O2[:, t, 64 * h:64 * h + 512], None, t_odd)
        k = transposed(O2, OT2, 8, [res, res])
        rows(a["mla_w_out"][0], 8, 0, 1024, OT2, residual_norm(2), None, k)
        t_xt = finish_norm(2, pe.now())

        off[0] = 11280
        RB = take("rb", 16)
        HOT = take("hot", 384)
        MKV = take("mkv", 384)
        BV = take("bv", 384)
        SNK = take("snk", 8)
        base2 = off[0]
        prev = [state["x"], t_xt, pe.now(), dve.now(), act.now(), pool.now()]
        s_n = Dma(sem("s_n"))
        s_n.issue(pool, RB[0:32, :], a["rel_bias_2"], *prev)
        s_n.issue(pool, HOT[0:32, :], a["bucket_hot"])
        s_n.issue(pool, MKV[0:16, :], a["bucket_mask"])
        s_n.issue(pool, SNK, a["sinks_2"].to_broadcast([P, 8]))
        t_n = (s_n.sem, s_n.n)
        BIAS = take("bias", 16, 256)

        def spread_biases():
            b = bank()
            k = mm_last(b.ap[0:16, 0:384], RB[0:32, :], HOT[0:32, :], True, True, t_n, b.free)
            k = tt(dve, BV[0:16, :], b.ap[0:16, 0:384], MKV[0:16, :], ALU.add, k)
            b.free = [k]
            s_bv = Dma(sem("s_bv"))
            sc = nc.dram_tensor("scratch", [16, P, 384], F32, kind="Internal").ap()
            k = s_bv.issue(pool, sc, BV[0:16, :].unsqueeze(1).to_broadcast([16, P, 384]), k)
            return s_bv.issue(pool, BIAS, bass.AP(sc.tensor, sc.offset + 127, [[383, 128], [384 * P, 16], [1, 256]]), k)


        ffn(1, 3, spread_biases)
        t_bias = state["along"]

        MODS = [ada["m", j] for j in (0, 1, 3, 4)]

        SQ_ = base2 + 4096

        def modulated(i, xt_free):
            rs, ready = [], []
            for t in range(2):
                acc = STAT[:, t, 0:1]
                if t:
                    k = fn(XN[:, t, :], X[:, t, :], ACT.Square, state["x"], xt_free, accum_out=acc)
                else:
                    k = ttr(XN[:, t, :], X[:, t, :], X[:, t, :], 0.0, ALU.mult, ALU.add, acc, state["x"], xt_free)
                rs.append(fn(acc, acc, ACT.Sqrt, k, bias=eps_rms, scale=1.0 / D))
            for t in range(2):
                acc = STAT[:, t, 0:1]
                k = recip(acc, acc, rs[t])
                ready.append(ts(dve, XN[:, t, :], X[:, t, :], acc, None, ALU.mult, None, k))
            return transposed(XN, XT, 8, ready, lambda c: MOD[:, 24 * i + 8 + c:24 * i + 9 + c],
                              lambda c: MOD[:, 24 * i + c:24 * i + c + 1], [MODS, xt_free])

        def gated_residual(i):
            def got(t, o, m, b, done):
                c = 2 * t + o // 512
                k = fn(at(SQ_ + 512 * c, 512), b.ap[:, 0:m], ACT.Square, done, state["x"], accum_out=STAT[:, t, 2 + o // 512:3 + o // 512])
                k = tt(dve, XN[:, t, o:o + m], b.ap[:, 0:m], G12[:, i, o:o + m], ALU.mult, k, ada["g", i])
                b.free = [k]
                state["h", t, o] = k
            return got

        def finish_gated(i):
            rs = []
            for t in range(2):
                acc = STAT[:, t, 2:3]
                k = tt(dve, acc, acc, STAT[:, t, 3:4], ALU.add, state["h", t, 0], state["h", t, 512])
                rs.append(fn(acc, acc, ACT.Sqrt, k, bias=eps_rms, scale=1.0 / D))
            out = []
            for t in range(2):
                acc = STAT[:, t, 2:3]
                k = recip(acc, acc, rs[t])
                out.append(stt(X[:, t, :], XN[:, t, :], acc, X[:, t, :], ALU.mult, ALU.add, k))
            state["x"] = out
            return out

        t_xt = modulated(0, [t_xt, pe.now()])
        prev = [dve.now(), act.now(), pe.now(), pool.now()]
        off[0] = base2 + 4096 + 2048
        QA = at(0, 12, 256)
        KBT = at(3072, 3, 256)
        VA = at(3840, 2, 640)
        O3 = at(5120, 2, 1024)
        OT3 = take("ot3", 8, 256)
        PR = take("pr3", 4, 2, 256)
        PX = take("px3", 2, 512)
        ST2 = take("st3", 256)
        W2 = a["w_in_2"][0]
        qk = {}

        def got_q2(i, b, n, done):
            src = b.ap[:, 0:256 * n].rearrange("p (c t) -> p c t", c=n)
            if i < 4 or i >= 8:
                if i == 12:
                    k = cp(act, KBT[:, 0, :], b.ap[:, 0:256], done)
                else:
                    k = fn(QA[:, i:i + n, :], src, ACT.Copy, done, scale=0.125)
            else:
                k = cp(act, QA[:, i:i + n, :], src, done)
            b.free = [k]
            for j in range(n):
                qk[i + j] = k

        cols2 = [(128 * i, 128) for i in range(8)] + [(1536 + 128 * i, 128) for i in range(4)]
        columns(W2, 8, cols2, XT, got_q2, t_xt)
        columns(W2, 8, [(2048, 128)], XT, lambda i, b, n, done: got_q2(12, b, n, done), t_xt)
        b = bank()
        k = mm_last(b.ap[:, 0:256], cst("swap"), KBT[:, 0, :], True, True, qk[12], b.free)
        t_sw = cp(act, KBT[:, 1, :], b.ap[:, 0:256], k)
        b.free = [t_sw]
        vv = {}

        def got_va(c0):
            def got(t, o, m, b, done):
                k = cp(act, VA[:, t, c0:c0 + m], b.ap[:, 0:m], done)
                b.free = [k]
                vv[t] = k
            return got

        rows(W2, 8, 1024, 512, XT, got_va(0), None, t_xt)
        rows(W2, 8, 2176, 128, XT, got_va(512), None, t_xt)

        def q2(h, t):
            r = slice(64 * (h % 2), 64 * (h % 2) + 64)
            i = h // 2 if h < 8 else 8 + (h - 8) // 2
            return QA[r, i, t * P:t * P + P], qk[i]

        def k2_(h, nk):
            r = slice(64 * (h % 2), 64 * (h % 2) + 64)
            if h < 8:
                return QA[r, 4 + h // 2, 0:nk], qk[4 + h // 2]
            g = (h - 8) // 4
            return KBT[r, 0 if g == h % 2 else 1, 0:nk], [qk[12], t_sw]

        def v2_(h, j):
            if h < 8:
                return VA[:, j, 64 * h:64 * h + 64], vv[j]
            g = (h - 8) // 4
            return VA[:, j, 512 + 64 * g:576 + 64 * g], vv[j]

        SK = take("sk", 16)
        k = fill(pool, SK[:, 0:8], NEG, prev)
        t_sk = cp(pool, SK[:, 8:16], SNK, t_n, k)
        res = attend(16, q2, k2_, lambda h, t: BIAS[:, h, 128 * (1 - t):256], v2_,
                     lambda h, t: O3[:, t, 64 * h:64 * h + 512], SK, [t_bias, t_sk])
        k = transposed(O3, OT3, 8, [res, res])
        rows(a["w_out_2"][0], 8, 0, 1024, OT3, gated_residual(0), None, k)
        finish_gated(0)
        t_xt = modulated(1, pe.now())
        HT = at(0, 32, 256)
        hs = []
        BT2 = take("b2row", 1024)
        t_b2 = Dma(sem("s_b2")).issue(sp, BT2[0:1, :], a["b2_2"], *prev)

        def got_h(i, b, n, done):
            for j in range(n):
                k = fn(HT[:, i + j, :], b.ap[:, 256 * j:256 * j + 256], ACT.Relu, done, bias=VEC[:, 1, i + j:i + j + 1])
            b.free = [k]
            v = HT[:, i:i + n, :]
            hs.append(tt(dve if (i // 2) % 2 else pool, v, v, v, ALU.mult, k))

        columns(a["w1_2"][0], 8, [(128 * i, 128) for i in range(32)], XT, got_h, t_xt)
        rows(a["w2_2"][0], 32, 0, 1024, HT, gated_residual(1), BT2, hs, t_b2)
        res = finish_gated(1)
        s_out = Dma(sem("s_out"))
        od_ = a["out"].rearrange("b (t p) d -> p (b t) d", p=P)
        for t in range(2):
            k = s_out.issue(sp, od_[:, t, :], X[:, t, :], res[t])
        sp.wait(k)

        block = ctx.enter_context(nc.Block())
        block.sync(sp.emit)
        block.scalar(act.emit)
        block.vector(dve.emit)
        block.gpsimd(pool.emit)
        block.tensor(pe.emit)


_INS = ["x", "positions", "even_w_in", "gla_gate_w2", "gla_gate_b", "gla_norm_g", "rwkv_mu", "rwkv_w0", "rwkv_w2",
        "rwkv_a0", "rwkv_a2", "rwkv_g2", "rwkv_k_k", "rwkv_k_a", "rwkv_r_k", "rwkv_ln_g", "rwkv_ln_b", "even_w_out",
        "mla_w_in", "mla_q_norm_g", "mla_w_q_b", "mla_kv_norm_g", "mla_w_kv_b", "mla_w_out", "ffn_w_gate_up",
        "ffn_w_down", "ln_g", "ln_b", "c_2", "w_in_2", "w_out_2", "sinks_2", "rel_bias_2", "w_ada_2", "b_ada_2",
        "norm_gains_2", "w1_2", "b1_2", "w2_2", "b2_2"]


def kernel(**inputs):
    import numpy as _np
    import concourse.bacc as _bacc
    from concourse import mybir as _mybir
    from concourse.bass_utils import run_bass_kernel_spmd as _run

    nc = _bacc.Bacc("TRN2", target_bir_lowering=False, num_devices=1)
    hot, mask = bucket_rows()
    given = {name: _np.ascontiguousarray(inputs[name]) for name in _INS}
    given.update(consts=constants(), bucket_hot=hot, bucket_mask=mask, mla_mask=mla_mask(), rope_freq=rope_rows())
    arrays, aps = {}, {}
    for name, x in given.items():
        arrays[f"in_{name}_dram"] = x
        aps[name] = nc.dram_tensor(f"in_{name}_dram", x.shape, _mybir.dt.from_np(x.dtype), kind="ExternalInput").ap()
    aps["out"] = nc.dram_tensor("out_0_dram", (1, S, D), _mybir.dt.float32, kind="ExternalOutput").ap()
    program(nc, aps)
    r = _run(nc, [arrays], core_ids=[0])
    return r.results[0]["out_0_dram"]
```

```python
from contextlib import ExitStack

import numpy as np

import concourse.bass as bass
from concourse import mybir

P = 128
S = 256
D = 1024
F32 = mybir.dt.float32
F32R = mybir.dt.float32r
I32 = mybir.dt.int32
ALU = mybir.AluOpType
ACT = mybir.ActivationFunctionType
AX = mybir.AxisListType.X

ALPHA = 4.0 ** 0.25
LN_EPS = 1e-5
RMS_EPS = 1e-6
GN_EPS = 64e-5
FFN = 2816
DFF = 4096
DECAY = float(np.exp(-0.5))
MLA_SCALE = 96.0 ** -0.5
NEG = -1e30

NAMES = (["ident", "cinc", "cexc", "strict", "incl", "heads"]
         + [f"lvl{i}" for i in range(7)] + [f"acc{i}" for i in range(7)] + ["after", "upto", "ones", "swap"])
COLS = {n: 128 * i for i, n in enumerate(NAMES)}
WIDE = 128 * len(NAMES)


def constants():
    s = np.arange(128)[:, None]
    t = np.arange(128)[None, :]
    out = {"ident": s == t, "strict": s < t, "incl": s <= t, "heads": s // 64 == t // 64,
           "cinc": (s <= t) * 1.0 - (s < 64), "cexc": (s < t) * 1.0 - (s < 64),
           "after": s > t, "upto": s <= t, "ones": (s >= 0) & (t >= 0), "swap": s == (t + 64) % 128}
    for i in range(7):
        m = 1 << i
        same = s // (2 * m) == t // (2 * m)
        right = (t // m) % 2 == 1
        out[f"lvl{i}"] = same & right & ((s // m) % 2 == 0)
        edge = t // (2 * m) * (2 * m) + m
        out[f"acc{i}"] = np.where(right, (s >= edge) & (s <= t), (s > t) & (s < edge))
    return np.concatenate([out[n].astype(np.float32) for n in NAMES], 1)


def bucket_rows():
    n = np.clip(255 - np.arange(384), 0, None)
    nf = np.maximum(n, 1).astype(np.float32)
    large = 16 + (np.log(nf / np.float32(16)) / np.float32(np.log(8.0)) * np.float32(16)).astype(np.int32)
    b = np.where(n < 16, n, np.minimum(large, 31))
    dist = 255 - np.arange(384)
    hot = (np.arange(32)[:, None] == b[None]).astype(np.float32)
    moba = np.where(dist >= 0, 0.0, NEG)
    swa = np.where((dist >= 0) & (dist < 128), 0.0, NEG)
    mask = np.concatenate([np.tile(moba, (8, 1)), np.tile(swa, (8, 1))]).astype(np.float32)
    return hot, mask


def mla_mask():
    q = np.arange(128)[:, None]
    k = np.arange(256)[None]
    near = np.where(k[:, :128] // 64 <= q // 64, 0.0, NEG)
    far = np.where(k // 64 <= (q + 128) // 64, 0.0, NEG)
    return np.concatenate([near, far], 1).astype(np.float32)


def rope_rows():
    f = (np.float32(10000.0) ** (-np.arange(0, 32, 2, dtype=np.float32) / np.float32(32))).astype(np.float32)
    return np.tile(f[None], (128, 1))


class Queue:

    def __init__(self, sem):
        self.sem, self.n, self.todo, self.met = sem, 0, [], {}

    def wait(self, *after):
        for tok in after:
            if tok is None:
                continue
            if isinstance(tok, list):
                self.wait(*tok)
                continue
            sem, value = tok
            if self.met.get(sem.name, 0) < value:
                self.met[sem.name] = value
                self.todo.append(lambda e, sem=sem, value=value: e.wait_ge(sem, value))

    def do(self, fn, *after):
        self.wait(*after)
        self.n += 1
        self.todo.append(lambda e: fn(e).then_inc(self.sem, 1))
        return (self.sem, self.n)

    def start(self, fn, *after):
        self.wait(*after)
        self.todo.append(fn)

    def now(self):
        return (self.sem, self.n)

    def emit(self, e):
        for fn in self.todo:
            fn(e)


class Dma:

    def __init__(self, sem):
        self.sem, self.n = sem, 0

    def issue(self, queue, out, in_, *after, **kw):
        self.n += 16
        queue.start(lambda e: e.dma_start(out, in_, **kw).then_inc(self.sem, 16), *after)
        return (self.sem, self.n)


class Buf:

    def __init__(self, ap, dma=None):
        self.ap, self.dma, self.free = ap, dma, []


def program(nc, a):
    ctx = ExitStack()
    with ctx:
        def sb(name, shape, dt=F32):
            return ctx.enter_context(nc.sbuf_tensor(name, shape, dt))[(slice(None),) * len(shape)]

        def sem(name):
            return ctx.enter_context(nc.semaphore(name))

        pe, dve, act, pool, sp = (Queue(sem(n)) for n in ("s_pe", "s_dve", "s_act", "s_pool", "s_sp"))

        NRAW = 3
        raw = [Buf(sb(f"ring{i}", [P, 2048]), Dma(sem(f"s_ring{i}"))) for i in range(NRAW)]
        psum = [Buf(ctx.enter_context(nc.psum_tensor(f"ps{i}", [P, 512], F32))) for i in range(8)]
        turn = {"psum": 0, "banks": 8}

        X = sb("X", [P, 2, D])
        XN = sb("XN", [P, 2, D])
        XT = (sb("XH", [P, 8, S], F32R), sb("XL", [P, 8, S], F32R))
        TF = sb("TF", [P, 2, 512])
        CST = sb("CST", [P, WIDE])
        VEC = sb("VEC", [P, 2, P])
        GB = sb("GB", [P, 2, D])
        SM = sb("SM", [P, 64])
        ARENA = 32352
        with nc.sbuf_tensor("ARR", [P, ARENA], F32R) as arr:
            ARR = arr[:, :]
        AR = sb("AR", [P, ARENA])
        SPLITS = ARENA - 3 * 4096

        def cst(name):
            return CST[:, COLS[name]:COLS[name] + 128]

        ident = cst("ident")

        def at(off, *shape, of=None):
            n = int(np.prod(shape))
            assert off + n <= ARENA, (off, n)
            v = (AR if of is None else of)[:, off:off + n]
            if len(shape) == 1:
                return v
            names = "abcd"[:len(shape)]
            kw = {c: k for c, k in zip(names[1:], shape[1:])}
            return v.rearrange(f"p ({' '.join(names)}) -> p {' '.join(names)}", **kw)

        def parts_at(off, *shape):
            n = int(np.prod(shape))
            return at(off, *shape, of=ARR), at(off + n, *shape, of=ARR)

        s_const = Dma(sem("s_const"))
        s_gain = Dma(sem("s_gain"))

        def bank():
            b = psum[turn["psum"] % turn["banks"]]
            turn["psum"] += 1
            return b

        plan = []
        flow = {"sent": 0, "made": 0, "used": 0, "open": False}
        sent, made = {}, {}
        splits = [Buf(parts_at(ARENA - 8192 + 4096 * i, 2048)) for i in range(2)]
        flow["splits"], flow["turn"] = splits, 0

        def send():
            while flow["sent"] < len(plan) and flow["sent"] < flow["made"] + NRAW:
                i = flow["sent"]
                src, n, dims, use = plan[i]
                slot = raw[i % NRAW]
                dst = slot.ap[:, 0:n].rearrange("p (c n) -> p c n", c=dims)
                sent[i] = (dst, slot.dma.issue(sp, dst, src, slot.free))
                flow["sent"] += 1

        def prepare():
            ready = len(made)
            while flow["made"] < len(plan) and ready < len(flow["splits"]) - 1:
                i = flow["made"]
                if i in gates and not flow["open"]:
                    break
                src, n, dims, use = plan[i]
                dst, there = sent[i]
                if use is not None:
                    raw[i % NRAW].free = [use(dst, there)]
                else:
                    b = flow["splits"][flow["turn"] % len(flow["splits"])]
                    flow["turn"] += 1
                    hi, lo = (x[:, 0:n].rearrange("p (c n) -> p c n", c=dims) for x in b.ap)
                    k = cp(act, hi, dst, there, b.free)
                    k = tt(dve, lo, dst, hi.bitcast(F32), ALU.subtract, k)
                    raw[i % NRAW].free = [k]
                    made[i] = (b, (hi, lo), k)
                    ready += 1
                flow["made"] += 1
                send()

        gates = []

        def next_weights(n, dims, ahead=True):
            i = flow["used"]
            while plan[i][3] is not None:
                i += 1
            if i not in made:
                prepare()
            flow["used"] = i + 1
            got = made.pop(i)
            assert plan[i][1:3] == (n, dims), (plan[i], n, dims)
            if ahead:
                prepare()
            return got

        def plan_columns(W, kc, cols):
            for i in range(0, len(cols), 2):
                pair = cols[i:i + 2]
                c0, c1 = pair[0][0], pair[-1][0] + pair[-1][1]
                plan.append((W[:, c0:c1].rearrange("(c p) n -> p c n", p=P), kc * (c1 - c0), kc, None))

        def plan_rows(W, kc, c0, n):
            per = max(1, 2048 // n)
            for k0 in range(0, kc, per):
                k1 = min(kc, k0 + per)
                plan.append((W[k0 * P:k1 * P, c0:c0 + n].rearrange("(c p) n -> p c n", p=P),
                             (k1 - k0) * n, k1 - k0, None))

        def mm(out, lhsT, rhs, first, last, *after):
            pe.start(lambda e: e.matmul(out, lhsT, rhs, start=first, stop=last), *after)

        def mm_last(out, lhsT, rhs, first, last, *after):
            return pe.do(lambda e: e.matmul(out, lhsT, rhs, start=first, stop=last), *after)

        def mm3(out, lhs, rhs, first, last, *after):
            mm(out, lhs[0], rhs[0], first, False, *after)
            mm(out, lhs[0], rhs[1], False, False)
            return mm_last(out, lhs[1], rhs[0], False, last)

        def cut(x, *idx):
            return tuple(v[idx] for v in x)

        def tr(out, in_, *after, np_=128):
            pe.start(lambda e: e.transpose(out, in_, ident[0:np_, 0:np_]), *after)

        def tr_last(out, in_, *after, np_=128):
            return pe.do(lambda e: e.transpose(out, in_, ident[0:np_, 0:np_]), *after)

        def tt(q, out, x, y, op, *after):
            return q.do(lambda e: e.tensor_tensor(out, x, y, op), *after)

        def ts(q, out, x, s1, s2, op0, op1, *after):
            if s2 is None:
                return q.do(lambda e: e.tensor_scalar(out, x, s1, None, op0), *after)
            return q.do(lambda e: e.tensor_scalar(out, x, s1, s2, op0, op1), *after)

        def stt(out, x, s, y, op0, op1, *after):
            return dve.do(lambda e: e.scalar_tensor_tensor(out, x, s, y, op0, op1), *after)

        def fn(out, x, f, *after, **kw):
            return act.do(lambda e: e.activation(out, x, f, **kw), *after)

        def recip(out, x, *after):
            return dve.do(lambda e: e.reciprocal(out, x), *after)

        def total(out, x, *after):
            return dve.do(lambda e: e.tensor_reduce(out, x, AX, ALU.add), *after)

        def ttr(out, x, y, start, op0, op1, acc, *after):
            return dve.do(lambda e: e.tensor_tensor_reduce(out, x, y, 1.0, start, op0, op1, acc), *after)

        def fill(q, out, value, *after):
            return q.do(lambda e: e.memset(out, value), *after)

        def select(out, mask, x, *after):
            return dve.do(lambda e: e.copy_predicated(out, mask, x), *after)

        def moments(out, x, *after):
            return dve.do(lambda e: e.bn_stats(out, x), *after)

        def gather_moments(out, x, *after):
            return dve.do(lambda e: e.bn_aggr(out, x), *after)

        def cp(q, out, x, *after):
            if q is act:
                return fn(out, x, ACT.Copy, *after)
            return q.do(lambda e: e.tensor_copy(out, x), *after)


        ALL = slice(None)

        def columns(kc, cols, xT, got, xready):
            for i in range(0, len(cols), 2):
                pair = cols[i:i + 2]
                b = bank()
                slot, w, there = next_weights(kc * 128 * len(pair), kc)
                for h in range(len(pair)):
                    for c in range(kc):
                        done = mm3(b.ap[:, h * 256:h * 256 + 256], cut(w, ALL, c, slice(h * P, h * P + P)),
                                   cut(xT, ALL, c), c == 0, c == kc - 1, there, b.free, xready[c // 2])
                slot.free = [done]
                got(i, b, len(pair), done)

        def rows(kc, n, xT, got, xready, bias=None, between=None):
            parts = [(o, min(512, n - o)) for o in range(0, n, 512)]
            bs = [[bank() for _ in parts] for _ in range(2)]
            per = max(1, 2048 // n)
            for k0 in range(0, kc, per):
                k1 = min(kc, k0 + per)
                if between and k0 in between:
                    between[k0]()
                slot, w, there = next_weights((k1 - k0) * n, k1 - k0, k1 < kc or kc <= per)
                for t in range(2):
                    for j, (o, m) in enumerate(parts):
                        for c in range(k0, k1):
                            done = mm3(bs[t][j].ap[:, 0:m], cut(xT, ALL, c, slice(t * P, t * P + P)),
                                       cut(w, ALL, c - k0, slice(o, o + m)), c == 0,
                                       c == kc - 1 and bias is None,
                                       there, bs[t][j].free if c == 0 else None, xready[c // 2])
                        if k1 == kc:
                            if bias is not None:
                                done = mm_last(bs[t][j].ap[:, 0:m], ones1, bias[0:1, o:o + m], False, True)
                            got(t, o, m, bs[t][j], done)
                slot.free = [pe.now()]

        eps_ln, eps_rms, eps_gn = SM[:, 0:1], SM[:, 1:2], SM[:, 2:3]
        ones1 = cst("ones")[0:1, :]
        STAT = sb("STAT", [P, 2, 16])

        def rstd(out, var, eps, scale, *after):
            k = fn(out, var, ACT.Sqrt, *after, bias=eps, scale=scale)
            return recip(out, out, k)

        tf_free = [[], []]

        def transposed(src, dst, c_n, ready, scale=None, shift=None, free=None):
            done, banks, got = [], [bank() for _ in range(c_n // 2)], {}
            for t in range(2):
                for c in range(c_n):
                    b = banks[c // 2]
                    got[c // 2] = (tr_last if (t, c % 2) == (1, 1) else tr)(
                        b.ap[:, (c % 2) * 256 + t * P:(c % 2) * 256 + t * P + P],
                        src[:, t, c * P:(c + 1) * P], ready[t], b.free)
            for c in range(0, c_n, 2):
                b, k = banks[c // 2], got[c // 2]
                w = (c // 2) % 2
                hi, lo = (x[:, c:c + 2, :] for x in dst)
                flat_bank = b.ap[:, :].rearrange("p (c t) -> p c t", c=2)
                if scale is None:
                    k = cp(act, hi, flat_bank, k, free)
                    d = tt(dve, lo, flat_bank, hi.bitcast(F32), ALU.subtract, k)
                    b.free = [d]
                    done.append(d)
                    continue
                for i in range(2):
                    sc, sh = scale(c + i), shift(c + i) if shift else None
                    x, y = b.ap[:, i * 256:i * 256 + 256], TF[:, w, i * 256:i * 256 + 256]
                    if w == 0:
                        d = (ts(dve, y, x, sc, None, ALU.mult, None, k, tf_free[w]) if sh is None
                             else ts(dve, y, x, sc, sh, ALU.mult, ALU.add, k, tf_free[w]))
                    elif sh is None:
                        d = fn(y, x, ACT.Copy, k, tf_free[w], scale=sc)
                    else:
                        d = fn(y, x, ACT.Identity, k, tf_free[w], bias=sh, scale=sc)
                b.free = [d]
                state["tf", w] = d
                if w == 1:
                    for v in range(2):
                        hi, lo = (x[:, c - 2 + 2 * v:c + 2 * v, :] for x in dst)
                        y = TF[:, v, :].rearrange("p (c t) -> p c t", c=2)
                        k = cp(act, hi, y, state["tf", v], free)
                        k = tt(dve, lo, y, hi.bitcast(F32), ALU.subtract, k)
                        tf_free[v] = [k]
                        done.append(k)
            return done

        def gain_rows(i, *after):
            g = a["ln_g"].rearrange("a b d -> (a b) d")[i:i + 1, :]
            b = a["ln_b"].rearrange("a b d -> (a b) d")[i:i + 1, :]
            s_gain.issue(pool, GB[:, 0, :], g.to_broadcast([P, D]), *after)
            return s_gain.issue(pool, GB[:, 1, :], b.to_broadcast([P, D]), *after)

        state = {"x": None, "gb": None}

        def normalised(t):
            k = gather_moments(STAT[:, t, 12:14], STAT[:, t, 0:12], state[("st", t, 0)], state[("st", t, 512)])
            mu, rs, off_ = STAT[:, t, 12:13], STAT[:, t, 14:15], STAT[:, t, 15:16]
            k = rstd(rs, STAT[:, t, 13:14], eps_ln, 1.0, k)
            k = ts(dve, off_, mu, rs, -1.0, ALU.mult, ALU.mult, k)
            c = 512 * t
            x = XN[:, t, c:]
            k2 = fn(x, x, ACT.Identity, k, bias=off_, scale=rs)
            if t:
                x = XN[:, t, 0:c]
                k = ts(dve, x, x, rs, off_, ALU.mult, ALU.add, k)
            state["xn", t] = [k, k2]

        def residual_norm(i):
            def got(t, o, m, b, done):
                k = stt(XN[:, t, o:o + m], X[:, t, o:o + m], ALPHA, b.ap[:, 0:m], ALU.mult, ALU.add,
                        done, state["x"])
                b.free = [k]
                k = moments(STAT[:, t, 6 * (o // 512):6 * (o // 512) + 6], XN[:, t, o:o + m], k)
                state[("st", t, o)] = k
                if o == 512:
                    normalised(t)
            return got

        def finish_norm(i, xt_free):
            ready = [state["xn", 0], state["xn", 1]]
            if i == 3:
                cut_ = 704
                for t in range(2):
                    done = []
                    for q, c in ((dve, slice(0, cut_)), (pool, slice(cut_, D))):
                        k = tt(q, X[:, t, c], XN[:, t, c], GB[:, 0, c], ALU.mult, ready[t], state["gb"])
                        done.append(tt(q, X[:, t, c], X[:, t, c], GB[:, 1, c], ALU.add, k))
                    ready[t] = done
                state["x"] = ready
                return ready
            ev = transposed(XN, XT, 8, ready, lambda c: VEC[:, 0, 31 + 8 * i + c:32 + 8 * i + c],
                            lambda c: VEC[:, 0, 63 + 8 * i + c:64 + 8 * i + c], xt_free)
            out = []
            for t in range(2):
                k = tt(pool, X[:, t, :], XN[:, t, :], GB[:, 0, :], ALU.mult, ready[t], state["gb"])
                out.append(tt(pool, X[:, t, :], X[:, t, :], GB[:, 1, :], ALU.add, k))
            state["x"] = out
            state["gb"] = gain_rows(i + 1, out)
            return ev

        WIN = a["even_w_in"][0]
        W2 = a["w_in_2"][0]
        WA = a["w_ada_2"][0]
        RW_COLS = [(1552 + 128 * i, 128) for i in range(14)] + [(3248, 128)]
        GLR_COLS = [(1536, 128)]
        QK_COLS = [(128 * i, 128) for i in range(4)]
        COLS_2 = [(128 * i, 128) for i in range(8)] + [(1536 + 128 * i, 128) for i in range(6)]
        COLS_1 = [(128 * i, 128) for i in range(32)]

        def plan_ffn(layer):
            W = a["ffn_w_gate_up"][layer]
            piece = 12 * layer
            for m, pieces_n in enumerate((1, 1, 1, 0, 1, 1, 0, 1, 1, 0, 1)):
                for c0 in (256 * m, FFN + 256 * m):
                    plan_columns(W, 8, [(c0, 128), (c0 + 128, 128)])
                for _ in range(pieces_n):
                    plan_piece(piece)
                    piece += 1
            for k0 in range(0, 22, 2):
                plan_rows(a["ffn_w_down"][layer][k0 * P:k0 * P + 256], 2, 0, 1024)
                if k0 in (2, 6, 10, 14):
                    plan_piece(piece)
                    piece += 1
            assert piece == 12 * layer + 12

        def plan_piece(piece):
            j, k0 = piece // 4, 2 * (piece % 4)
            src = WA[k0 * P:k0 * P + 256, 1024 * j:1024 * j + 1024].rearrange("(c p) n -> p c n", p=P)
            plan.append((src, 2048, 2, lambda w, there: modulation_piece(piece, w, there)))

        plan_columns(WIN, 8, RW_COLS[12:])
        for i in (4, 0, 8):
            plan_columns(WIN, 8, RW_COLS[i:i + 4])
        plan_columns(WIN, 8, GLR_COLS)
        plan_columns(WIN, 8, QK_COLS)
        plan_rows(WIN, 8, 512, 1024)
        gates.append(len(plan))
        plan_rows(a["even_w_out"][0][512:1024], 4, 0, 1024)
        plan_rows(a["even_w_out"][0][0:512], 4, 0, 1024)
        plan_ffn(0)
        plan_rows(a["mla_w_in"][0], 8, 0, 1024)
        plan_rows(a["mla_w_in"][0], 8, 1024, 32)
        plan_rows(a["mla_w_q_b"][0], 6, 0, 1536)
        plan_rows(a["mla_w_kv_b"][0], 2, 0, 1024)
        plan_rows(a["mla_w_kv_b"][0], 2, 1024, 1024)
        plan_rows(a["mla_w_out"][0], 8, 0, 1024)
        plan_ffn(1)
        plan_columns(W2, 8, COLS_2)
        plan_rows(W2, 8, 1024, 512)
        plan_rows(a["w_out_2"][0], 8, 0, 1024)
        plan_columns(a["w1_2"][0], 8, COLS_1)
        plan_rows(a["w2_2"][0], 32, 0, 1024)

        t_x = s_const.issue(act, X[:, :, :], a["x"].rearrange("b (t p) d -> p (b t) d", p=P))
        s_c2 = Dma(sem("s_c2"))
        send()
        t_id = s_c2.issue(act, CST[:, 0:P], a["consts"][:, 0:P])
        VR = at(0, 2, 128)
        O_ = {}
        off = [256]

        def take(name, *shape):
            n = int(np.prod(shape))
            O_[name] = at(off[0], *shape)
            off[0] += n
            return O_[name]

        GW2 = take("gw2", 256)
        W2A2 = take("w2a2", 512)
        G2 = take("g2", 2, 512)
        LNG = take("lng", 512)
        LNB = take("lnb", 512)
        GNG = take("gng", 128)
        RW0 = take("rw0", 768)
        k = fill(pool, VR, 0.0)
        k_g2 = fill(pool, G2[0:96, 1, :], 0.0)
        fill(pool, eps_ln, LN_EPS)
        fill(pool, eps_rms, RMS_EPS)
        fill(pool, eps_gn, GN_EPS)
        fill(pool, SM[:, 3:4], 1.0)
        k_sm = fill(pool, SM[:, 4:6], 0.0)
        k_sm = fill(pool, SM[64:128, 4:5], 1.0, k_sm)
        t_eps = fill(pool, SM[0:64, 5:6], 1.0, k_sm)
        s_vec = Dma(sem("s_vec"))

        def vrow(half, r, src, n):
            full = n // P
            flat = src
            if full:
                s_vec.issue(sp, VR[r:r + full, half, :], flat[:, 0:full * P].rearrange("a (r p) -> (a r) p", p=P), k)
            if n % P:
                s_vec.issue(sp, VR[r + full:r + full + 1, half, 0:n % P], flat[:, full * P:n], k)

        for r, name, n in ((0, "rwkv_mu", 1792), (15, "rwkv_k_k", 512), (19, "rwkv_k_a", 512),
                           (23, "rwkv_a0", 512)):
            vrow(0, r, a[name], n)
        s_vec.issue(sp, VR[14:15, 0, 96:128], a["rwkv_mu"][:, 1792:1824], k)
        vrow(0, 27, a["rwkv_r_k"].rearrange("a h n -> a (h n)"), 512)
        s_vec.issue(sp, VR[31:63, 0, :], a["ln_g"].rearrange("a b (r p) -> (a b r) p", p=P), k)
        s_vec.issue(sp, VR[63:95, 0, :], a["ln_b"].rearrange("a b (r p) -> (a b r) p", p=P), k)
        vrow(0, 95, a["mla_q_norm_g"], 768)
        vrow(0, 101, a["mla_kv_norm_g"], 256)
        vrow(1, 0, a["b1_2"], 4096)
        vrow(1, 32, a["b_ada_2"], 6144)
        s_vec.issue(sp, VR[80:112, 1, :], a["norm_gains_2"].rearrange("a b (r p) -> (a b r) p", p=P), k)
        vrow(1, 112, a["c_2"], 1024)
        t_vec = (s_vec.sem, s_vec.n)
        t_cst = Dma(sem("s_cst")).issue(sp, CST[:, P:], a["consts"][:, P:])
        s_ev = Dma(sem("s_ev"))
        s_ev.issue(sp, GW2[0:16, :], a["gla_gate_w2"][0])
        s_ev.issue(sp, W2A2[0:64, :], a["rwkv_w2"][0])
        s_ev.issue(sp, W2A2[64:128, :], a["rwkv_a2"][0])
        s_ev.issue(sp, G2[:, 0, :], a["rwkv_g2"][0, 0:128, :])
        s_ev.issue(sp, G2[96:128, 1, :], a["rwkv_g2"][0, 128:160, :])
        s_ev.issue(sp, LNG, a["rwkv_ln_g"].to_broadcast([P, 512]))
        s_ev.issue(sp, LNB, a["rwkv_ln_b"].to_broadcast([P, 512]))
        s_ev.issue(sp, GNG, a["gla_norm_g"].to_broadcast([P, 128]))
        s_ev.issue(sp, RW0[0:1, 0:512], a["rwkv_w0"])
        s_ev.issue(sp, RW0[0:1, 512:768], a["gla_gate_b"])
        t_ev = (s_ev.sem, s_ev.n)
        state["x"] = t_x

        prepare()
        t_xt = transposed(X, XT, 8, [[t_x, t_id]] * 2)
        for h in range(2):
            b = bank()
            k = tr_last(b.ap[:, 0:128], VR[:, h, :], t_vec)
            t_v = cp(dve, VEC[:, h, :], b.ap[:, 0:128], k)
            b.free = [t_v]

        def vec(half, i):
            return VEC[:, half, i:i + 1]

        dm = off[0]
        Dm = take("D", 15, 256)
        PT = at(off[0], 15, 257)
        base = off[0]

        t_zero = fill(pool, Dm[0:96, 14, :], 0.0)
        zero = fill(dve, PT[:, :, 0:1], 0.0)
        ptd = {}

        def got_rw(i, b, n, done):
            if i + n == 15:
                k = cp(act, PT[96:128, 14, 1:257], b.ap[96:128, 0:256], done)
            else:
                k = cp(act, PT[:, i:i + n, 1:257], b.ap[:, :].rearrange("p (c t) -> p c t", c=2), done)
            b.free = [k]
            for j in range(i, i + n):
                pn = slice(96 if j == 14 else 0, 128)
                d = tt(dve, Dm[pn, j, :], PT[pn, j, 0:256], PT[pn, j, 1:257], ALU.subtract, k, zero)
                ptd[j] = stt(Dm[pn, j, :], Dm[pn, j, :], VEC[pn, 0, j:j + 1], PT[pn, j, 1:257],
                             ALU.mult, ALU.add, d, t_v)

        columns(8, RW_COLS[12:], XT, lambda i, b, n, done: got_rw(i + 12, b, n, done), t_xt)

        def rw_columns(i0, then=None):
            def got(i, b, n, done):
                got_rw(i + i0, b, n, done)
                if then:
                    then(i // 2)

            columns(8, RW_COLS[i0:i0 + 4], XT, got, t_xt)


        off[0] += 15 * 257
        GQK = take("gqk", 4, 256)
        GLR = take("glr", 256)
        GV = take("gv", 2, 512)
        GG = take("gg", 2, 512)
        G = take("g", 2, 512)
        RKM = take("rkm", 4, 8)
        SML = take("sml", 128)
        gl = {}

        def got_qk(i, b, n, done):
            src = b.ap[:, :].rearrange("p (c t) -> p c t", c=2)
            if i == 0:
                gl["q"] = fn(GQK[:, 0:2, :], src, ACT.Copy, done, scale=0.125)
                b.free = [gl["q"]]
            else:
                gl["k"] = cp(act, GQK[:, 2:4, :], src, done)
                b.free = [gl["k"]]

        def got_lr(i, b, n, done):
            gl["lr"] = cp(act, GLR[0:16, :], b.ap[0:16, 0:256], done)
            b.free = [gl["lr"]]

        def got_vg(t, o, m, b, done):
            if o == 0:
                gl["v", t] = cp(act, GV[:, t, :], b.ap[:, :], done)
            else:
                gl["v", t] = fn(GG[:, t, :], b.ap[:, :], ACT.Silu, done)
                gl["g", t] = gl["v", t]
            b.free = [gl["v", t]]


        SIG = take("sig", 2, 512)
        ee = off[0]
        EE = take("ee", 3, 4, 256)
        AA = take("aa", 4, 256)
        KK = take("kk", 4, 256)
        KP = take("kp", 4, 256)
        assert off[0] <= ARENA - 8192 and ee + 2048 <= SPLITS
        CAR = GB.rearrange("p a b -> p (a b)").rearrange("p (i t w d) -> p i t w d", i=4, t=2, w=2)
        kt = base
        KT = at(kt, 4, 256)
        BT = at(kt + 1024, 4, 256)
        VT = at(kt + 2048, 2, 512)
        KB = G2
        S0 = at(dm + 3072, 4, 64)
        RHS = at(dm + 3328, 512)
        r_, k_, v_ = Dm[:, 0:4, :], Dm[:, 4:8, :], Dm[:, 8:12, :]
        t_th = fn(Dm[0:64, 12, :], Dm[0:64, 12, :], ACT.Tanh, ptd[12])
        t_sg = fn(Dm[:, 13, :], Dm[:, 13, :], ACT.Sigmoid, ptd[13])
        t_sg = fn(Dm[96:128, 14, :], Dm[96:128, 14, :], ACT.Sigmoid, ptd[14], t_zero)
        rw_columns(4)
        for q in (pe, dve, act, pool):
            q.wait(t_eps, t_cst)
        t_sig = []
        for t in range(2):
            b = bank()
            mm(b.ap[:, :], Dm[0:64, 12, t * P:t * P + P], W2A2[0:64, :], True, False, t_th, t_ev, b.free)
            k = mm_last(b.ap[:, :], ones1, RW0[0:1, 0:512], False, True, t_eps)
            t_sig.append(fn(SIG[:, t, :], b.ap[:, :], ACT.Sigmoid, k))
            b.free = [t_sig[-1]]
        t_a = []
        for i in range(4):
            b = bank()
            k = mm_last(b.ap[:, 0:256], W2A2[64:128, i * P:i * P + P], Dm[64:128, 12, :], True, True,
                        ptd[12], t_ev, b.free)
            t_a.append(fn(AA[:, i, :], b.ap[:, 0:256], ACT.Sigmoid, k, t_v, bias=vec(0, 23 + i)))
            b.free = [t_a[-1]]
        t_g = []
        for t in range(2):
            b = bank()
            mm(b.ap[:, :], Dm[:, 13, t * P:t * P + P], G2[:, 0, :], True, False, t_sg, t_ev, b.free)
            k = mm_last(b.ap[:, :], Dm[:, 14, t * P:t * P + P], G2[:, 1, :], False, True, k_g2)
            t_g.append(cp(act, G[:, t, :], b.ap[:, :], k))
            b.free = [t_g[-1]]
        t_kk = []
        for i in range(4):
            k = ts(dve, KK[:, i, :], Dm[:, 4 + i, :], vec(0, 15 + i), None, ALU.mult, None, ptd[4 + i])
            t_kk.append(tt(dve, KP[:, i, :], KK[:, i, :], KK[:, i, :], ALU.mult, k))
        sq = []
        for i in range(0, 4, 2):
            b = bank()
            mm(b.ap[:, 0:256], cst("heads"), KP[:, i, :], True, True, t_kk[i], b.free)
            k = mm_last(b.ap[:, 256:512], cst("heads"), KP[:, i + 1, :], True, True, t_kk[i + 1])
            k = ts(dve, KP[:, i:i + 2, :], b.ap[:, :].rearrange("p (c t) -> p c t", c=2), 1e-24, None,
                   ALU.max, None, k)
            b.free = [k]
            t_kk[i] = t_kk[i + 1] = fn(KP[:, i:i + 2, :], KP[:, i:i + 2, :], ACT.Sqrt, k)

        def unit_key(i):
            k = recip(KP[:, i, :], KP[:, i, :], t_kk[i])
            sq.append(tt(dve, KK[:, i, :], KK[:, i, :], KP[:, i, :], ALU.mult, k))

        rw_columns(0, unit_key)
        t_e = {}
        for i in range(4):
            b = bank()
            for w, name in enumerate(("cinc", "cexc")):
                for t in range(2):
                    f = mm_last if (w, t) == (1, 1) else mm
                    k = f(b.ap[:, w * 256 + t * P:w * 256 + t * P + P], SIG[:, t, i * P:i * P + P],
                          cst(name), True, True, t_sig[t], b.free)
            fn(EE[:, 0, i, :], b.ap[:, 0:256], ACT.Exp, k, scale=-DECAY)
            fn(EE[:, 1, i, :], b.ap[:, 0:256], ACT.Exp, k, scale=DECAY)
            t_e[i] = fn(EE[:, 2, i, :], b.ap[:, 256:512], ACT.Exp, k, scale=-DECAY)
            b.free = [t_e[i]]
        b = bank()
        for i in range(4):
            mm(b.ap[:, i:i + 1], SIG[:, 0, i * P:i * P + P], SM[:, 4:5], True, False, b.free)
            k = mm_last(b.ap[:, i:i + 1], SIG[:, 1, i * P:i * P + P], SM[:, 5:6], False, True)
        t_gm = fn(SML[:, 0:4], b.ap[:, 0:4], ACT.Exp, k, scale=-DECAY)
        b.free = [t_gm]
        rw_columns(8, lambda i: unit_key(i + 2))
        columns(8, GLR_COLS, XT, got_lr, t_xt)
        tl = []

        def operands(i):
            ka = vec(0, 19 + i)
            k = ts(dve, KP[:, i, :], AA[:, i, :], 1.0, ka, ALU.subtract, ALU.mult, t_a[i], sq)
            k = stt(KP[:, i, :], KP[:, i, :], 1.0, Dm[:, 4 + i, :], ALU.add, ALU.mult, k)
            tl.append(tt(dve, KT[:, i, :], KP[:, i, :], EE[:, 1, i, :], ALU.mult, k, t_e[i]))
            tl.append(stt(CAR[:, i, :, 0, :], KK[:, i, :].rearrange("p (a b) -> p a b", a=2), -1.0,
                          EE[:, 2, i, :].rearrange("p (a b) -> p a b", a=2), ALU.mult, ALU.mult, t_e[i]))
            k2 = tt(pool, AA[:, i, :], AA[:, i, :], KK[:, i, :], ALU.mult, sq, t_a[i], k)
            tl.append(tt(pool, BT[:, i, :], AA[:, i, :], EE[:, 1, i, :], ALU.mult, k2, t_e[i]))
            tl.append(tt(pool, CAR[:, i, :, 1, :], Dm[:, i, :].rearrange("p (a b) -> p a b", a=2),
                         EE[:, 0, i, :].rearrange("p (a b) -> p a b", a=2), ALU.mult, t_e[i], ptd[i]))
            tl.append(tt(pool, KP[:, i, :], KP[:, i, :], Dm[:, i, :], ALU.mult, k, tl[-4]))

        columns(8, QK_COLS, XT, lambda i, b, n, done: (got_qk(i, b, n, done), operands(i // 2)), t_xt)
        rows(8, 1024, XT, got_vg, t_xt, between={2: lambda: operands(2), 4: lambda: operands(3)})
        t_til = tl
        k = fill(pool, RKM, 0.0)
        for i in range(4):
            for hh in range(2):
                k = cp(pool, RKM[64 * hh:64 * hh + 64, i, 2 * i + hh:2 * i + hh + 1],
                       VEC[64 * hh:64 * hh + 64, 0, 27 + i:28 + i], k, t_v)
        t_rkm = k
        b = bank()
        for t in range(2):
            for i in range(4):
                f = mm_last if (t, i) == (1, 3) else mm
                k = f(b.ap[:, 8 * t:8 * t + 8], KP[:, i, t * P:t * P + P], RKM[:, i, :], i == 0, i == 3,
                      t_til, t_rkm, b.free)
        t_bon = cp(dve, SML[:, 8:24], b.ap[:, 0:16], k)
        b.free = [t_bon]
        t_vt = []
        for t in range(2):
            b = bank()
            for i in range(4):
                f = tr_last if i == 3 else tr
                k = f(b.ap[:, i * P:i * P + P], Dm[:, 8 + i, t * P:t * P + P], ptd[8 + i], b.free)
            t_vt.append(cp(act, VT[:, t, :], b.ap[:, :], k, list(ptd.values())))
            b.free = [t_vt[-1]]
        for w, src in enumerate((KT, BT)):
            b = bank()
            for i in range(4):
                f = tr_last if i == 3 else tr
                k = f(b.ap[:, i * P:i * P + P], src[:, i, 0:P], b.free)
            t_kb = cp(act, KB[:, w, :], b.ap[:, :], k, t_g)
            b.free = [t_kb]

        LA = SIG
        t_la = []
        for t in range(2):
            b = bank()
            m_, e_ = XN[:, t, 0:256], XN[:, t, 256:512]
            mm(b.ap[:, 0:256], GLR[0:16, t * P:t * P + P], GW2[0:16, :], True, False, gl["lr"], t_ev, b.free)
            k = mm_last(b.ap[:, 0:256], ones1, RW0[0:1, 512:768], False, True)
            k1 = fn(e_, b.ap[:, 0:256], ACT.Abs, k)
            k2 = ts(dve, m_, b.ap[:, 0:256], -1.0, 0.0, ALU.mult, ALU.max, k1)
            b.free = [k2]
            k = fn(e_, e_, ACT.Exp, k1, scale=-1.0)
            k = fn(e_, e_, ACT.Ln, k, bias=SM[:, 3:4])
            t_la.append(tt(dve, LA[:, t, 0:256], m_, e_, ALU.add, k, k2, t_gm, t_e[3]))
        mats = ARENA - 8192
        AAB = at(mats, 16, 128)
        PP = at(mats + 4096, 16, 128)
        AAK = at(ee + 2048, 16, 128)
        ARB = at(ee + 4096, 16, 128)
        ARK = at(mats + 2048, 16, 128)
        TI = at(dm, 16, 128)
        TJ = at(kt, 16, 128)
        ALA = at(ee, 16, 128)
        t_m = {}
        for s in range(16):
            t, h = s // 8, s % 8
            r = slice(64 * (h % 2), 64 * (h % 2) + 64)
            b = bank()
            for j, lhs in enumerate((BT, KT)):
                k = (mm_last if j else mm)(
                    b.ap[:, 256 * j:256 * j + 256], lhs[r, h // 2, t * P:t * P + P],
                    CAR[r, h // 2, t, :, :].rearrange("p a b -> p (a b)"), True, True, t_til, t_bon, b.free)
            for i, (dst, m) in enumerate(((AAB, "strict"), (ARB, "incl"), (AAK, "strict"), (ARK, "incl"))):
                t_m[s] = tt(dve, dst[:, s, :], b.ap[:, 128 * i:128 * i + 128], cst(m), ALU.mult, k)
            b.free = [t_m[s]]
        NG = 4
        t_ti = [None] * NG
        t_tj = [None] * NG
        t_al = [None] * NG
        t_pp = [None] * NG

        def group(x, g):
            return x[:, 4 * g:4 * g + 4, :]

        def pview(g):
            return PP[:, 4 * g:4 * g + 4, :]

        def flat(x):
            return x.rearrange("p s t -> p (s t)")

        bc = lambda name: cst(name).unsqueeze(1).to_broadcast([P, 4, P])
        free_al = [None] * NG
        BON = at(dm + 2048, 2, 512)

        def gated_bonus(t):
            k = tt(dve, BON[:, t].rearrange("p (h n) -> p h n", h=8), VT[:, t, :].rearrange("p (h n) -> p h n", h=8),
                   SML[:, 8 + 8 * t:16 + 8 * t].unsqueeze(2).to_broadcast([P, 8, 64]), ALU.mult, t_bon, t_vt, t_til)
            k = tt(dve, BON[:, t], BON[:, t], LNB, ALU.add, k, t_ev)
            k = tt(dve, BON[:, t], BON[:, t], G[:, t], ALU.mult, k, t_g)
            tt(dve, G[:, t], G[:, t], LNG, ALU.mult, k)

        for lv in range(7):
            if lv in (2, 3):
                gated_bonus(lv - 2)
            for g in range(NG):
                need = t_m[4 * g + 3]
                t_al[g] = tt(pool, group(ALA, g), group(AAB, g), bc(f"lvl{lv}"), ALU.mult, need, t_til,
                             free_al[g])
                b = bank()
                for s in range(4):
                    k = (mm_last if s == 3 else mm)(
                        b.ap[:, s * P:s * P + P], ALA[:, 4 * g + s, :],
                        ident if lv == 0 else TI[:, 4 * g + s, :], True, True,
                        t_al[g], t_ti[g], b.free)
                free_al[g] = k
                if lv == 0:
                    t_ti[g] = tt(dve, group(TI, g), b.ap[:, :].rearrange("p (s t) -> p s t", s=4),
                                 bc("ident"), ALU.add, k, t_vt, t_til)
                    b.free = [t_ti[g]]
                    t_tj[g] = tt(dve, group(TJ, g), group(ALA, g), bc("ident"), ALU.add, t_al[g], t_kb)
                    free_al[g] = [k, t_tj[g]]
                else:
                    t_pp[g] = cp(act, pview(g), b.ap[:, :].rearrange("p (s t) -> p s t", s=4), k, t_ti[g], t_tj[g])
                    b.free = [t_pp[g]]
            if lv == 0:
                continue
            for g in range(NG):
                p_ = pview(g)
                bj = bank()
                for s in range(4):
                    kj = (mm_last if s == 3 else mm)(bj.ap[:, s * P:s * P + P], p_[:, s, :],
                                                     TJ[:, 4 * g + s, :], True, True, t_pp[g], t_tj[g], bj.free)
                if lv < 6:
                    bi = bank()
                    for s in range(4):
                        ki = (mm_last if s == 3 else mm)(bi.ap[:, s * P:s * P + P], TJ[:, 4 * g + s, :],
                                                         p_[:, s, :], True, True, bi.free)
                    t_ti[g] = tt(dve, flat(group(TI, g)), bi.ap[:, :], flat(group(TI, g)), ALU.add, ki)
                    bi.free = [t_ti[g]]
                else:
                    ki = kj
                t_tj[g] = tt(dve, flat(group(TJ, g)), bj.ap[:, :], flat(group(TJ, g)), ALU.add, kj, ki)
                bj.free = [t_tj[g]]

        Y = [None, None]
        O = XN

        def chunk_steps():
            t_s0 = None
            for t in range(2):
                rd = []
                for j in range(2):
                    b = bank()
                    r = slice(64 * j, 64 * j + 64)
                    for i in range(4):
                        h = 2 * i + j
                        sl = slice(64 * i, 64 * i + 64)
                        k = (mm_last if t == 0 and i == 3 else mm)(
                            b.ap[:, sl], AAK[:, 8 * t + h, :], VT[:, t, 64 * h:64 * h + 64], True, t == 0,
                            t_m[15], t_vt[t], b.free)
                        if t:
                            k = mm_last(b.ap[:, sl], CAR[r, i, t, 0, :], S0[r, i, :], False, True, t_s0)
                    rd.append(cp(dve, RHS[:, 256 * j:256 * j + 256], b.ap[:, 0:256], k, t_s0, t_g))
                    b.free = [rd[j]]
                yield
                b = bank()
                for h in range(8):
                    sl = slice(256 * (h % 2) + 64 * (h // 2), 256 * (h % 2) + 64 * (h // 2) + 64)
                    k2 = (mm_last if h == 7 else mm)(b.ap[:, sl], TJ[:, 8 * t + h, :], RHS[:, sl], True, True,
                                                     rd[h % 2], t_tj, b.free)
                t_u = cp(dve, RHS, b.ap[:, :], k2)
                b.free = [t_u]
                yield
                yt = []
                for j in range(2):
                    b = bank()
                    r = slice(64 * j, 64 * j + 64)
                    for i in range(4):
                        h = 2 * i + j
                        sl = slice(64 * i, 64 * i + 64)
                        mm(b.ap[:, sl], ARK[:, 8 * t + h, :], VT[:, t, 64 * h:64 * h + 64], True, False, b.free)
                        k = (mm_last if t == 0 and i == 3 else mm)(
                            b.ap[:, sl], ARB[:, 8 * t + h, :], RHS[:, 256 * j + 64 * i:256 * j + 64 * i + 64],
                            False, t == 0, t_u)
                        if t:
                            k = mm_last(b.ap[:, sl], CAR[r, i, t, 1, :], S0[r, i, :], False, True)
                    dst = O[:, t, 512:1024].rearrange("p (i j n) -> p j i n", i=4, j=2)[:, j]
                    yt.append(cp(act, dst, b.ap[:, 0:256].rearrange("p (i n) -> p i n", i=4), k))
                    b.free = [yt[j]]
                Y[t] = yt
                yield
                if t == 0:
                    b = bank()
                    for i in range(4):
                        sl = slice(128 * i, 128 * i + 128)
                        mm(b.ap[:, sl], KB[:, 0, sl], VT[:, 0, sl], True, False, t_kb, b.free)
                        k = mm_last(b.ap[:, sl], KB[:, 1, sl],
                                    RHS.rearrange("p (j i v) -> p i j v", j=2, i=4)[:, i], False, True)
                    for j in range(2):
                        pr = slice(64 * j, 64 * j + 64)
                        t_s0 = tt(dve, S0[pr, :, :],
                                  b.ap[pr, :].rearrange("p (i v) -> p i v", i=4)[:, :, 64 * j:64 * j + 64],
                                  SML[pr, 0:4].unsqueeze(2).to_broadcast([64, 4, 64]), ALU.mult, k, t_gm, t_g)
                    b.free = [t_s0]

        def group_norm(t):
            y = O[:, t, 512:1024].rearrange("p (h n) -> p h n", h=8)
            tm = LNB.rearrange("p (h n) -> p h n", h=8)
            st = SML[:, 32 + 16 * t:48 + 16 * t]
            mu, va = st[:, 0:8], st[:, 8:16]
            b8 = lambda v: v.unsqueeze(2).to_broadcast([P, 8, 64])
            k = total(mu, y, Y[t])
            k = ts(dve, mu, mu, 1.0 / 64, None, ALU.mult, None, k)
            k = tt(dve, y, y, b8(mu), ALU.subtract, k)
            k = tt(dve, tm, y, y, ALU.mult, k)
            k = total(va, tm, k)
            k = rstd(va, va, eps_gn, 1.0 / 64, k, t_eps)
            k = tt(dve, y, y, b8(va), ALU.mult, k)
            k = tt(dve, y, y, G[:, t, :].rearrange("p (h n) -> p h n", h=8), ALU.mult, k)
            Y[t] = tt(dve, y, y, BON[:, t].rearrange("p (h n) -> p h n", h=8), ALU.add, k)

        AT = TI.rearrange("p s t -> p (s t)")

        def pieces(x):
            return [x.rearrange("p s t -> p (s t)")[:, 512 * i:512 * i + 512].rearrange("p (c t) -> p c t", c=2)
                    for i in range(x.shape[1] // 4)]

        QE, KE, EG = pieces(PP), pieces(AAB), pieces(ALA)
        inverse_done = [pe.now(), dve.now(), act.now(), pool.now()]
        at0 = fill(dve, AT[:, 0:1024], 0.0, inverse_done)
        t_at, t_cr = at0, None
        gq, gk = GQK[:, 0:2, :], GQK[:, 2:4, :]
        used = [inverse_done] * 4

        def decayed(lv):
            if lv < 0:
                return gq, gk, [gl["q"], gl["k"]]
            i = lv % 4
            b = bank()
            for c in range(2):
                for t in range(2):
                    m = cst(f"acc{lv}") if lv < 7 else cst(("after", "upto")[t])
                    k = (mm_last if (c, t) == (1, 1) else mm)(
                        b.ap[:, c * 256 + t * P:c * 256 + t * P + P], LA[:, t, c * P:c * P + P], m,
                        True, True, t_la, b.free)
            k = fn(EG[i], b.ap[:, :].rearrange("p (c t) -> p c t", c=2), ACT.Exp, k, used[i], scale=-1.0 / 16)
            b.free = [k]
            return QE[i], KE[i], [tt(dve, QE[i], gq, EG[i], ALU.mult, k, gl["q"], used[i]),
                                  tt(pool, KE[i], gk, EG[i], ALU.mult, k, gl["k"], used[i])]

        def level_products(lv, q_, k_e, ready):
            nonlocal t_at, t_cr
            for j in range(2):
                r = slice(64 * j, 64 * j + 64)
                b = bank()
                if lv < 7:
                    for c in range(2):
                        for t in range(2):
                            k = (mm_last if (c, t) == (1, 1) else mm)(
                                b.ap[:, (2 * c + t) * P:(2 * c + t) * P + P],
                                k_e[r, c, t * P:t * P + P], q_[r, c, t * P:t * P + P], True, True,
                                ready, b.free)
                    name = "ident" if lv < 0 else f"lvl{lv}"
                    mask = cst(name).bitcast(I32).unsqueeze(1).to_broadcast([P, 4, P])
                    dst = AT[:, 512 * j:512 * j + 512].rearrange("p (s t) -> p s t", s=4)
                    t_at = select(dst, mask, b.ap[:, :].rearrange("p (s t) -> p s t", s=4), k, t_at)
                    b.free = [t_at]
                else:
                    for c in range(2):
                        k = (mm_last if c else mm)(b.ap[:, c * P:c * P + P], k_e[r, c, 0:P],
                                                   q_[r, c, P:2 * P], True, True, ready, b.free)
                    t_cr = cp(dve, AT[:, 1024 + 256 * j:1280 + 256 * j], b.ap[:, 0:256], k, at0)
                    b.free = [t_cr]
            if lv >= 0:
                used[lv % 4] = [k]

        ops = {lv: decayed(lv) for lv in range(-1, 2)}
        steps = chunk_steps()
        for lv in range(-1, 8):
            next(steps, None)
            if lv + 3 < 8:
                ops[lv + 3] = decayed(lv + 3)
            level_products(lv, *ops[lv])
            if lv == 3:
                group_norm(0)
            if lv == 5:
                for t in range(2):
                    gg = GG[:, t, :].rearrange("p (h n) -> p h n", h=4)
                    gl["g", t] = tt(pool, gg, gg, GNG.unsqueeze(1).to_broadcast([P, 4, P]), ALU.mult,
                                    gl["g", t], t_ev)
        for _ in steps:
            pass
        state["gb"] = gain_rows(0, dve.now(), act.now(), pe.now(), pool.now())
        flow["splits"] = [Buf(parts_at(SPLITS + 4096 * i, 2048)) for i in range(3)]
        for b in flow["splits"]:
            b.free = [pe.now()]
        flow["open"], flow["turn"] = True, 0
        TM3 = ALA.rearrange("p s t -> p (s t)")
        YG = [None, None]
        used_up = [pe.now(), dve.now(), act.now()]
        group_norm(1)
        held = []
        for t in range(2):
            b = bank()
            for h in range(4):
                sl = slice(h * P, h * P + P)
                blk = 512 * (h % 2) + (2 * (h // 2) + t) * P
                crs = 1024 + 256 * (h % 2) + 128 * (h // 2)
                k = (mm_last if t == 0 and h == 3 else mm)(
                    b.ap[:, sl], AT[:, blk:blk + P], GV[:, t, sl], True, t == 0,
                    t_at, gl["v", 0], gl["v", 1], b.free)
                if t:
                    k = mm_last(b.ap[:, sl], AT[:, crs:crs + P], GV[:, 0, sl], False, True, t_cr)
            held.append((b, k))
        prepare()
        OT = parts_at(dm, 8, 256)
        mixed = transposed(O[:, :, 512:], cut(OT, ALL, slice(0, 4)), 4, Y, free=Y)
        for t in range(2):
            b, k = held[t]
            o = O[:, t, 0:512].rearrange("p (h n) -> p h n", h=4)
            ss = SML[:, 64 + 4 * t:68 + 4 * t]
            tm = TM3[:, t * 512:t * 512 + 512].rearrange("p (h n) -> p h n", h=4)
            for h in range(4):
                k1 = fn(tm[:, h, :], b.ap[:, h * P:h * P + P], ACT.Square, k, used_up, accum_out=ss[:, h:h + 1])
            k1 = rstd(ss, ss, eps_rms, 1.0 / 128, k1)
            b4 = ss.unsqueeze(2).to_broadcast([P, 4, P])
            gg = GG[:, t, :].rearrange("p (h n) -> p h n", h=4)
            k = tt(dve, o, b.ap[:, :].rearrange("p (h n) -> p h n", h=4), b4, ALU.mult, k1)
            b.free = [k]
            YG[t] = tt(dve, o, o, gg, ALU.mult, k, gl["g", t])
        rows(8, 1024, OT, residual_norm(0), mixed, between={4: lambda: mixed.extend(
            transposed(O, cut(OT, ALL, slice(4, 8)), 4, YG, free=YG))})
        t_xt = finish_norm(0, pe.now())

        MOD = at(SPLITS - 48, 48)
        G12 = at(SPLITS - 48 - 2048, 2, 1024)
        ACCA = at(11264, 2, 1024)
        CSL = at(13312, 8)
        GN = XN[:, 1, :]
        ada = {"later": None}

        def start_modulation(which):
            prev = [dve.now(), act.now(), pe.now(), pool.now()]
            ada["c"] = fn(CSL, VEC[:, 1, 112:120], ACT.Silu, *prev)
            ada["acc"] = [prev, prev]
            g = G12[:, which, :]
            j = 2 + 3 * which
            sa = Dma(sem(f"s_ada{which}"))
            sa.issue(pool, g, a["b_ada_2"][:, 1024 * j:1024 * j + 1024].to_broadcast([P, D]), *prev)
            ada["gate"] = sa.issue(pool, GN, a["norm_gains_2"][0, 1 + 2 * which:2 + 2 * which, :]
                                   .to_broadcast([P, D]))

        def modulation_sums():
            if ada["later"]:
                ada["later"]()
                ada["later"] = None

        def modulation_piece(piece, w, there):
            j, k0 = piece // 4, 2 * (piece % 4)
            acc = ACCA[:, j % 2, :]
            k = ada.get("k")
            for c in range(2):
                if k0 + c == 0:
                    k = ts(dve, acc, w[:, c, :], CSL[:, 0:1], None, ALU.mult, None, there, ada["c"],
                           ada["acc"][j % 2])
                else:
                    k = stt(acc, w[:, c, :], CSL[:, k0 + c:k0 + c + 1], acc, ALU.mult, ALU.add, there, k)
            ada["k"] = k
            if k0 == 6:
                assert ada["later"] is None
                ada["later"] = lambda: modulation_column(j, acc, k)
            return k

        def modulation_column(j, acc, k):
            b = bank()
            if j in (2, 5):
                g = G12[:, j // 3, :]
                for o in range(0, 1024, 512):
                    if o:
                        b = bank()
                    k2 = mm_last(b.ap[:, :], cst("ones"), acc[:, o:o + 512], True, True, k, b.free)
                    k3 = tt(dve, g[:, o:o + 512], b.ap[:, :], g[:, o:o + 512], ALU.add, k2, ada["gate"])
                    k3 = tt(dve, g[:, o:o + 512], g[:, o:o + 512], GN[:, o:o + 512], ALU.mult, k3)
                    b.free = [k3]
                ada["g", j // 3] = k3
            else:
                for i in range(8):
                    k2 = (mm_last if i == 7 else mm)(b.ap[:, i:i + 1], acc[:, i * P:i * P + P], SM[:, 3:4],
                                                     True, True, k, b.free)
                k3 = tt(dve, MOD[:, 8 * j:8 * j + 8], b.ap[:, 0:8], VEC[:, 1, 32 + 8 * j:40 + 8 * j],
                        ALU.add, k2, t_v)
                if j in (1, 4):
                    k3 = stt(MOD[:, 8 * j:8 * j + 8], MOD[:, 8 * j:8 * j + 8], 1.0,
                             VEC[:, 1, 80 + 16 * (j // 3):88 + 16 * (j // 3)], ALU.add, ALU.mult, k3)
                b.free = [k3]
                ada["m", j] = k3
            ada["acc"][j % 2] = [k2]

        def ffn(layer, i, along=None):
            nonlocal t_xt
            HT = parts_at(0, 22, 256)
            UP = XN[:, 0, :].rearrange("p (a b) -> p a b", a=2)
            start_modulation(layer)
            x_done = state["x"]
            free_up, pend = [x_done, x_done], []
            xready = []
            for j in range(0, 22, 2):
                if along and j == 4:
                    spread = along()
                if along and j == 8:
                    state["along"] = spread()
                if j == 14:
                    modulation_sums()
                bs = []
                for _ in range(2):
                    slot, w, there = next_weights(2048, 8)
                    b = bank()
                    for h in range(2):
                        for c in range(8):
                            k = mm3(b.ap[:, 256 * h:256 * h + 256], cut(w, ALL, c, slice(h * P, h * P + P)),
                                    cut(XT, ALL, c), c == 0, c == 7, there, b.free, t_xt[c // 2])
                    slot.free = [k]
                    bs.append((b, k))
                u = UP[:, (j // 2) % 2, :]
                (bg, kg), (bu, ku) = bs
                kg = fn(u, bg.ap[:, :], ACT.Silu, kg, free_up[(j // 2) % 2])
                bg.free = [kg]
                d = tt(dve, u, bu.ap[:, :], u, ALU.mult, ku, kg)
                bu.free = [d]
                hi, lo = (x[:, j:j + 2, :].rearrange("p c t -> p (c t)") for x in HT)
                k = cp(act, hi, u, d)
                k = tt(dve, lo, u, hi.bitcast(F32), ALU.subtract, k)
                free_up[(j // 2) % 2] = k
                xready.append(k)
            rows(22, 1024, HT, residual_norm(i), xready, between={6: modulation_sums, 20: modulation_sums})
            t_xt = finish_norm(i, pe.now())

        ffn(0, 1)

        off[0] = 0
        QQ = take("qq", 2, 1536)
        KF = take("kf", 2, 1536)
        V2 = take("v2", 2, 1024)
        ct = off[0]
        CT = parts_at(ct, 8, 256)
        off[0] += 4096
        MK = take("mk", 384)
        PS_ = take("pos", 2)
        FR = take("fr", 16)
        CS = take("cs", 2, 2, 16)
        RT = take("rt", 2, 4, 16)
        ST2 = take("st2", 256)
        CQ = take("cq", 2, 1056)
        R2 = take("r2", 2, 2, 256)
        assert off[0] <= SPLITS - 2096
        QK = [at(ct + 512 * i, 512) for i in range(4)]
        PR = [at(ct + 2048 + 512 * i, 2, 256) for i in range(2)] + [
            XN[:, i // 2, 512 * (i % 2):512 * (i % 2) + 512].rearrange("p (a b) -> p a b", a=2) for i in range(4)]
        PX = at(ct + 3072, 2, 512)
        PI_ = sb("PI", [P, 2], I32)
        prev = [state["x"], t_xt, pe.now()]
        s_odd = Dma(sem("s_odd"))
        s_odd.issue(pool, MK, a["mla_mask"], *prev)
        s_odd.issue(pool, FR, a["rope_freq"], *prev)
        t_odd = (s_odd.sem, s_odd.n)
        t_pos = Dma(sem("s_pos")).issue(pool, PI_[:, :], a["positions"].rearrange("b (t p) -> p (b t)", p=P),
                            allow_slow_non_contiguous=True)
        od = {}
        SQ = QQ

        def got_p(t, o, m, b, done):
            k = cp(act if o == 512 else dve, CQ[:, t, o:o + m], b.ap[:, 0:m], done)
            b.free = [k]
            od[t, o] = k

        rows(8, 1024, XT, got_p, t_xt)
        rows(8, 32, XT, lambda t, o, m, b, done: got_p(t, 1024, m, b, done), t_xt)
        kn = []
        for t in range(2):
            k = stats = None
            for j, (lo, n) in enumerate(((0, 768), (768, 256))):
                acc = ST2[:, 2 * t + j:2 * t + j + 1]
                k = ttr(SQ[:, t, lo:lo + n], CQ[:, t, lo:lo + n], CQ[:, t, lo:lo + n], 0.0, ALU.mult, ALU.add, acc, od[t, 0], od[t, 512])
                k = rstd(acc, acc, eps_rms, 1.0 / n, k)
                k = ts(dve, CQ[:, t, lo:lo + n], CQ[:, t, lo:lo + n], acc, None, ALU.mult, None, k)
            kn.append(k)
        k = transposed(CQ, CT, 8, kn, lambda c: vec(0, 95 + c) if c < 6 else vec(0, 101 + c - 6))

        k_ps = cp(dve, PS_, PI_[:, :], t_pos, t_odd)
        parts = [6.28125]
        rest = 2 * np.pi - parts[0]
        for bits in (14, 22):
            p_ = float(np.floor(rest * 2.0 ** bits) / 2.0 ** bits)
            parts.append(p_)
            rest -= p_
        parts.append(float(np.float32(rest)))
        MAGIC = 1.5 * 2.0 ** 23
        t_cs = []
        for t in range(2):
            ang, n_ = RT[:, t, 0, :], RT[:, t, 1, :]
            k1 = ts(dve, ang, FR, PS_[:, t:t + 1], None, ALU.mult, None, k_ps)
            k1 = ts(dve, n_, ang, float(1 / (2 * np.pi)), MAGIC, ALU.mult, ALU.add, k1)
            k1 = ts(dve, n_, n_, MAGIC, None, ALU.subtract, None, k1)
            for p_ in parts:
                k1 = stt(ang, n_, -p_, ang, ALU.mult, ALU.add, k1)
            k1 = ts(dve, ang, ang, 3.1415925, -3.1415925, ALU.min, ALU.max, k1)
            k2 = fn(CS[:, t, 1, :], ang, ACT.Sin, k1)
            k2 = fn(n_, ang, ACT.Sin, k2, scale=0.5)
            k2 = tt(dve, n_, n_, n_, ALU.mult, k2)
            t_cs.append(ts(dve, CS[:, t, 0, :], n_, -2.0, 1.0, ALU.mult, ALU.add, k2))

        def rope(x, t, n, *after):
            pr = x.rearrange("p h (i two) -> p h i two", two=2)
            x1, x2 = pr[:, :, :, 0], pr[:, :, :, 1]
            cos = CS[:, t, 0, :].unsqueeze(1).to_broadcast([P, n, 16])
            sin = CS[:, t, 1, :].unsqueeze(1).to_broadcast([P, n, 16])
            u = R2[:, 0, 0, 0:n * 16].rearrange("p (h i) -> p h i", h=n)
            v = R2[:, 0, 1, 0:n * 16].rearrange("p (h i) -> p h i", h=n)
            w = R2[:, 1, 0, 0:n * 16].rearrange("p (h i) -> p h i", h=n)
            y = R2[:, 1, 1, 0:n * 16].rearrange("p (h i) -> p h i", h=n)
            k1 = tt(dve, u, x1, cos, ALU.mult, t_cs, dve.now(), *after)
            k2 = tt(dve, v, x2, sin, ALU.mult)
            k3 = tt(dve, w, x1, sin, ALU.mult)
            k4 = tt(dve, y, x2, cos, ALU.mult)
            k5 = tt(dve, x1, u, v, ALU.subtract, k4)
            return tt(dve, x2, w, y, ALU.add, k5)

        def got_q(t, o, m, b, done):
            k = fn(QQ[:, t, o:o + m], b.ap[:, 0:m], ACT.Copy, done, kn, scale=MLA_SCALE)
            b.free = [k]
            od["q", t] = k

        rows(6, 1536, CT, got_q, k)

        def got_kv(half):
            def got(t, o, m, b, done):
                h0 = 8 * half + 4 * (o // 512)
                src = b.ap[:, :].rearrange("p (h n) -> p h n", h=4)
                kf = KF[:, t, :].rearrange("p (h n) -> p h n", h=16)[:, h0:h0 + 4, 0:64]
                v2 = V2[:, t, :].rearrange("p (h n) -> p h n", h=16)[:, h0:h0 + 4, :]
                k = cp(act, kf, src[:, :, 0:64], done)
                k = cp(act, v2, src[:, :, 64:128], done)
                b.free = [k]
                od["kv", t] = k
            return got

        t_q, kr = [], []
        for t in range(2):
            q16 = QQ[:, t, :].rearrange("p (h n) -> p h n", h=16)
            t_q.append(rope(q16[:, :, 64:96], t, 16, od["q", t]))
            kr.append(rope(CQ[:, t, 1024:1056].unsqueeze(1), t, 1, od[t, 1024]))
            kf = KF[:, t, :].rearrange("p (h n) -> p h n", h=16)[:, :, 64:96]
            kr[t] = cp(dve, kf, CQ[:, t, 1024:1056].unsqueeze(1).to_broadcast([P, 16, 32]), kr[t])
        for half in range(2):
            rows(2, 1024, cut(CT, ALL, slice(6, 8)), got_kv(half), k[3:])
        def attend(q_of, k_of, mask_of, v_of, out, sink=None, ready=None, first=None, scored=None):
            MX = ST2[:, 16:48]
            SU = ST2[:, 48:80]
            NM = ST2[:, 80:112]
            RS = ST2[:, 112:144]
            pr_free, px_free, result = {}, {}, []
            turn["banks"] = 6
            items = [(t, h) for h in range(16) for t in range(2)]
            soft, scale, moved, leaving = {}, {}, {}, []

            def softened(i):
                t, h = items[i]
                nk, w = P * (t + 1), i % 6
                mx, nm, su, rs = (x[:, i:i + 1] for x in (MX, NM, SU, RS))
                q, kq = q_of(h, t)
                kk, kkk = k_of(h, nk)
                b = bank()
                k = mm_last(b.ap[:, 0:nk], q, kk, True, True, kq, kkk, b.free)
                if scored is not None:
                    scored[h] = k
                pr = PR[w][:, 0, 0:nk]
                old = normed(i - 3)
                next(old, None)
                k = ttr(pr, b.ap[:, 0:nk], mask_of(h, t), NEG, ALU.add, ALU.max, mx, k, pr_free.get(w), ready)
                b.free = [k]
                next(old, None)
                if sink is not None and h >= 8:
                    k = tt(dve, mx, mx, sink[:, h - 8:h - 7], ALU.max, k)
                next(old, None)
                k = ts(dve, nm, mx, -1.0, None, ALU.mult, None, k)
                soft[i] = fn(PR[w][:, 1, 0:nk], pr, ACT.Exp, k, bias=nm, accum_out=su)
                if sink is not None and h >= 8:
                    soft[i] = fn(rs, sink[:, h - 8:h - 7], ACT.Exp, soft[i], bias=nm)

            def normed(i):
                if i < 0:
                    return
                t, h = items[i]
                su, rs, k = SU[:, i:i + 1], RS[:, i:i + 1], soft[i]
                if sink is not None and h >= 8:
                    k = tt(dve, su, su, rs, ALU.add, k)
                yield
                k = recip(rs, su, k)
                yield
                ex = PR[i % 6][:, 1, 0:P * (t + 1)]
                scale[i] = ts(dve, ex, ex, rs, None, ALU.mult, None, k)

            def turned(i):
                t, h = items[i]
                nk, ex = P * (t + 1), PR[i % 6][:, 1]
                b = bank()
                for j in range(t + 1):
                    kt = (tr_last if j == t else tr)(b.ap[:, j * P:j * P + P], ex[:, j * P:j * P + P],
                                                     scale[i], b.free)
                pr_free[i % 6] = kt
                moved[i] = cp(act, PX[:, i % 2, 0:nk], b.ap[:, 0:nk], kt, px_free.get(i % 2))
                b.free = [moved[i]]

            def weighed(i):
                t, h = items[i]
                px = PX[:, i % 2]
                bo = psum[6 + (h // 4) % 2]
                at_ = 256 * ((h % 4) // 2) + P * t
                for j in range(t + 1):
                    v, kv = v_of(h, j)
                    kp = (mm_last if j == t else mm)(
                        bo.ap[64 * (h % 2):64 * (h % 2) + 64, at_:at_ + P], v, px[:, j * P:j * P + P],
                        j == 0, j == t, moved[i], kv, bo.free)
                px_free[i % 2] = kp
                if (t, h % 4) == (1, 3):
                    leaving.append([kp, bo, h // 4])

            def left():
                if not leaving:
                    return
                kp, bo, g = leaving[0]
                hi, lo = (x[:, 2 * g:2 * g + 2, :] for x in out)
                src = bo.ap[:, :].rearrange("p (c t) -> p c t", c=2)
                if len(leaving[0]) == 3 and kp[0] is pe.sem:
                    leaving[0] = [cp(act, hi, src, kp), bo, g]
                    return
                k = tt(dve, lo, src, hi.bitcast(F32), ALU.subtract, kp)
                bo.free = [k]
                result.append(k)
                leaving.pop(0)

            n = len(items)
            if first:
                first(0)
            for i in range(n + 7):
                if first and i < n and i % 2 == 0:
                    first(i // 2 + 1)
                if 0 <= i - 5 < n:
                    turned(i - 5)
                if i < n:
                    softened(i)
                else:
                    for _ in normed(i - 3 if i - 3 < n else -1):
                        pass
                left()
                if 0 <= i - 6 < n:
                    weighed(i - 6)
            while leaving:
                left()
            turn["banks"] = 8
            return result

        t_k = [[kr[t], od["kv", t]] for t in range(2)]
        t_hd, scored = {}, {}

        def turn_head(h):
            if h > 15:
                return
            b = bank()
            for j, (src, toks) in enumerate(((QQ, t_q), (KF, t_k))):
                for t in range(2):
                    k = (tr_last if t and j else tr)(
                        b.ap[0:96, 256 * j + t * P:256 * j + t * P + P], src[:, t, 96 * h:96 * h + 96],
                        toks[t], b.free)
            t_hd[h] = cp(dve if h % 2 else act, QK[h % 4][0:96, :], b.ap[0:96, :], k, kv_read, scored.get(h - 4))
            b.free = [t_hd[h]]

        kv_read = pe.now()
        k = attend(lambda h, t: (QK[h % 4][0:96, t * P:t * P + P], t_hd[h]),
                   lambda h, nk: (QK[h % 4][0:96, 256:256 + nk], t_hd[h]),
                   lambda h, t: MK[:, 128 * t:128 * t + 128 + 128 * t],
                   lambda h, j: (V2[:, j, 64 * h:64 * h + 64], od["kv", j]), XT, None, t_odd, turn_head, scored)
        rows(8, 1024, XT, residual_norm(2), k)
        t_xt = finish_norm(2, pe.now())

        BIAS = at(13320, 16, 256)
        SNK = at(13320 + 4096, 8)
        RB, HOT, MKV = TF[:, 1, 384:400], TF[:, 0, 0:384], TF[:, 1, 0:384]
        assert 13320 + 4104 <= SPLITS - 2096

        def spread_biases():
            prev = [t_xt, state["x"], dve.now(), act.now()]
            s_n = Dma(sem("s_n"))
            s_n.issue(pool, RB[0:32, :], a["rel_bias_2"], *prev)
            s_n.issue(pool, HOT[0:32, :], a["bucket_hot"])
            s_n.issue(pool, MKV[0:16, :], a["bucket_mask"])
            t_n = s_n.issue(pool, SNK, a["sinks_2"].to_broadcast([P, 8]))

            def spread():
                b = bank()
                k = mm_last(b.ap[0:16, 0:384], RB[0:32, :], HOT[0:32, :], True, True, t_n, b.free)
                k = tt(dve, MKV[0:16, :], b.ap[0:16, 0:384], MKV[0:16, :], ALU.add, k)
                b.free = [k]
                s_bv = Dma(sem("s_bv"))
                sc = nc.dram_tensor("scratch", [16, P, 384], F32, kind="Internal").ap()
                k = s_bv.issue(pool, sc, MKV[0:16, :].unsqueeze(1).to_broadcast([16, P, 384]), k)
                k = s_bv.issue(pool, BIAS, bass.AP(sc.tensor, sc.offset + 127, [[383, 128], [384 * P, 16], [1, 256]]), k)
                tf_free[0], tf_free[1] = [k], [k]
                return [t_n, k]
            return spread

        ffn(1, 3, spread_biases)
        t_bias = state["along"]

        MODS = [ada["m", j] for j in (0, 1, 3, 4)]

        state["m"] = [None, None]

        def scaled(t):
            acc = STAT[:, t, 0:1]
            if t:
                k = ttr(XN[:, t, :], X[:, t, :], X[:, t, :], 0.0, ALU.mult, ALU.add, acc, state["x"][t])
            else:
                k = fn(XN[:, t, :], X[:, t, :], ACT.Square, state["x"][t], accum_out=acc)
            k = rstd(acc, acc, eps_rms, 1.0 / D, k)
            c = 512 * t
            k2 = fn(XN[:, t, c:], X[:, t, c:], ACT.Copy, k, scale=acc)
            if t:
                k = ts(dve, XN[:, t, 0:c], X[:, t, 0:c], acc, None, ALU.mult, None, k)
            state["m"][t] = [k, k2]

        def modulated(i, xt_free):
            return transposed(XN, XT, 8, state["m"], lambda c: MOD[:, 24 * i + 8 + c:24 * i + 9 + c],
                              lambda c: MOD[:, 24 * i + c:24 * i + c + 1], [MODS, xt_free])

        def gated_residual(i, then):
            old = list(state["x"])

            def got(t, o, m, b, done):
                k = fn(GB[:, 1, 0:m], b.ap[:, 0:m], ACT.Square, done, old, state.get("sq"),
                       accum_out=STAT[:, t, 2 + o // 512:3 + o // 512])
                state["sq"] = k
                k = tt(dve, XN[:, t, o:o + m], b.ap[:, 0:m], G12[:, i, o:o + m], ALU.mult, k, ada["g", i])
                b.free = [k]
                if o == 512:
                    acc = STAT[:, t, 2:3]
                    k2 = tt(dve, acc, acc, STAT[:, t, 3:4], ALU.add, state["sq"], k)
                    k2 = rstd(acc, acc, eps_rms, 1.0 / D, k2)
                    state["x"][t] = stt(X[:, t, :], XN[:, t, :], acc, X[:, t, :], ALU.mult, ALU.add, k2, k)
                    then(t)
            return got

        for t in range(2):
            scaled(t)
        t_xt = modulated(0, [t_xt, pe.now()])
        prev = [dve.now(), act.now(), pe.now(), pool.now()]
        off[0] = 0
        QA = take("qa", 12, 256)
        KBT = take("kbt", 3, 256)
        VBT = take("vbt", 256)
        VA = take("va", 2, 640)
        pr = take("pr3", 6, 2, 256)
        PR = [pr[:, i] for i in range(6)]
        PX = take("px3", 2, 512)
        ST2 = take("st3", 256)
        assert off[0] <= 13320
        qk = {}

        def got_q2(i, b, n, done):
            src = b.ap[:, 0:256 * n].rearrange("p (c t) -> p c t", c=n)
            if i < 4 or i >= 8:
                if i == 12:
                    k = cp(act, KBT[:, 0, :], b.ap[:, 0:256], done)
                    k = cp(act, VBT, b.ap[:, 256:512], done)
                else:
                    k = fn(QA[:, i:i + n, :], src, ACT.Copy, done, scale=0.125)
            else:
                k = cp(act, QA[:, i:i + n, :], src, done)
            b.free = [k]
            for j in range(n):
                qk[i + j] = k

        columns(8, COLS_2, XT, got_q2, t_xt)
        b = bank()
        k = mm_last(b.ap[:, 0:256], cst("swap"), KBT[:, 0, :], True, True, qk[12], b.free)
        t_sw = cp(act, KBT[:, 1, :], b.ap[:, 0:256], k)
        b.free = [t_sw]
        vv = {}

        def got_va(c0):
            def got(t, o, m, b, done):
                k = cp(act, VA[:, t, c0:c0 + m], b.ap[:, 0:m], done)
                b.free = [k]
                vv[t] = k
            return got

        b = bank()
        for t in range(2):
            k = (tr_last if t else tr)(b.ap[:, t * P:t * P + P], VBT[:, t * P:t * P + P], qk[13], b.free)
        t_vb = cp(act, VA[:, :, 512:640], b.ap[:, 0:256].rearrange("p (t n) -> p t n", t=2), k)
        b.free = [t_vb]
        rows(8, 512, XT, got_va(0), t_xt)

        def q2(h, t):
            r = slice(64 * (h % 2), 64 * (h % 2) + 64)
            i = h // 2 if h < 8 else 8 + (h - 8) // 2
            return QA[r, i, t * P:t * P + P], qk[i]

        def k2_(h, nk):
            r = slice(64 * (h % 2), 64 * (h % 2) + 64)
            if h < 8:
                return QA[r, 4 + h // 2, 0:nk], qk[4 + h // 2]
            g = (h - 8) // 4
            return KBT[r, 0 if g == h % 2 else 1, 0:nk], [qk[12], t_sw]

        def v2_(h, j):
            if h < 8:
                return VA[:, j, 64 * h:64 * h + 64], vv[j]
            g = (h - 8) // 4
            return VA[:, j, 512 + 64 * g:576 + 64 * g], [vv[j], t_vb]

        k = attend(q2, k2_, lambda h, t: BIAS[:, h, 128 * (1 - t):256], v2_, XT, SNK, t_bias)
        rows(8, 1024, XT, gated_residual(0, scaled), k)
        t_xt = modulated(1, pe.now())
        HT = parts_at(0, 32, 256)
        assert 2 * 8192 <= SPLITS - 2096
        hs = []
        H_ = [XN[:, 0, 512 * i:512 * i + 512] for i in range(2)]
        h_free = [t_xt, t_xt]
        BT2 = GB[:, 0, :]
        t_b2 = Dma(sem("s_b2")).issue(pool, BT2[0:1, :], a["b2_2"], state["x"], *prev)

        def got_h(i, b, n, done):
            w = (i // 2) % 2
            x = H_[w]
            for j in range(n):
                k = fn(x[:, 256 * j:256 * j + 256], b.ap[:, 256 * j:256 * j + 256], ACT.Relu, done, h_free[w],
                       bias=VEC[:, 1, i + j:i + j + 1])
            b.free = [k]
            k = tt(dve, x, x, x, ALU.mult, k)
            hi, lo = (v[:, i:i + n, :].rearrange("p c t -> p (c t)") for v in HT)
            k = cp(act, hi, x, k)
            h_free[w] = tt(dve, lo, x, hi.bitcast(F32), ALU.subtract, k)
            hs.append(h_free[w])

        columns(8, COLS_1, XT, got_h, t_xt)
        pe.wait(t_b2)
        s_out = Dma(sem("s_out"))
        od_ = a["out"].rearrange("b (t p) d -> p (b t) d", p=P)

        def store(t):
            state["out"] = s_out.issue(sp, od_[:, t, :], X[:, t, :], state["x"][t])

        rows(32, 1024, HT, gated_residual(1, store), hs, BT2)
        sp.wait(state["out"])

        block = ctx.enter_context(nc.Block())
        block.sync(sp.emit)
        block.scalar(act.emit)
        block.vector(dve.emit)
        block.gpsimd(pool.emit)
        block.tensor(pe.emit)


_INS = ["x", "positions", "even_w_in", "gla_gate_w2", "gla_gate_b", "gla_norm_g", "rwkv_mu", "rwkv_w0", "rwkv_w2",
        "rwkv_a0", "rwkv_a2", "rwkv_g2", "rwkv_k_k", "rwkv_k_a", "rwkv_r_k", "rwkv_ln_g", "rwkv_ln_b", "even_w_out",
        "mla_w_in", "mla_q_norm_g", "mla_w_q_b", "mla_kv_norm_g", "mla_w_kv_b", "mla_w_out", "ffn_w_gate_up",
        "ffn_w_down", "ln_g", "ln_b", "c_2", "w_in_2", "w_out_2", "sinks_2", "rel_bias_2", "w_ada_2", "b_ada_2",
        "norm_gains_2", "w1_2", "b1_2", "w2_2", "b2_2"]


def kernel(**inputs):
    import numpy as _np
    import concourse.bacc as _bacc
    from concourse import mybir as _mybir
    from concourse.bass_utils import run_bass_kernel_spmd as _run

    nc = _bacc.Bacc("TRN2", target_bir_lowering=False, num_devices=1)
    hot, mask = bucket_rows()
    given = {name: _np.ascontiguousarray(inputs[name]) for name in _INS}
    given.update(consts=constants(), bucket_hot=hot, bucket_mask=mask, mla_mask=mla_mask(), rope_freq=rope_rows())
    arrays, aps = {}, {}
    for name, x in given.items():
        arrays[f"in_{name}_dram"] = x
        aps[name] = nc.dram_tensor(f"in_{name}_dram", x.shape, _mybir.dt.from_np(x.dtype), kind="ExternalInput").ap()
    aps["out"] = nc.dram_tensor("out_0_dram", (1, S, D), _mybir.dt.float32, kind="ExternalOutput").ap()
    program(nc, aps)
    r = _run(nc, [arrays], core_ids=[0])
    return r.results[0]["out_0_dram"]
```
